# Optimizing a Trainium2 kernel written in Bass

```python
import jax, jax.numpy as jnp
from jax import lax
import numpy as np

D_MODEL = 1024
BATCH = 1
SEQ = 512
DEPTH = 2

D_MIX = D_MODEL
HG_HEADS = 4
HG_DK = 128
HG_DV = 128
HG_W = HG_HEADS * HG_DV
HG_CHUNK = 64
NSA_HEADS = 8
NSA_KV_HEADS = 2
NSA_DH = 64
NSA_G = NSA_HEADS // NSA_KV_HEADS
NSA_W = NSA_HEADS * NSA_DH
KV_W = NSA_KV_HEADS * NSA_DH
CMP_BLOCK = 32
CMP_STRIDE = 16
CMP_HIDDEN = 128
SLC_BLOCK = 64
SLC_TOPK = 16
SLC_Q_BLOCK = 64
WINDOW = 512
Q_BLOCK = 128
FORCE_SCORE = 1e4
ROPE_THETA = 500000.0
ROPE_DIM = NSA_DH // 4
PLE_DIM = 256
RMS_EPS = 1e-6
IN_SPLITS = (HG_W,) * 5 + (NSA_W,) + (KV_W,) * 6 + (3 * NSA_HEADS, NSA_W)
IN_COLS = 5 * HG_W + NSA_W + 6 * KV_W + 3 * NSA_HEADS + NSA_W


def rmsnorm(x, g):
    xf = x.astype(jnp.float32)
    var = jnp.mean(xf * xf, axis=-1, keepdims=True)
    return (xf * lax.rsqrt(var + RMS_EPS)).astype(x.dtype) * g

def masked_softmax(s, mask):
    s = jnp.where(mask, s.astype(jnp.float32), -jnp.inf)
    m = jnp.max(s, axis=-1, keepdims=True)
    m = jnp.where(jnp.isfinite(m), m, 0.0)
    e = jnp.where(mask, jnp.exp(s - m), 0.0)
    return e / jnp.maximum(jnp.sum(e, axis=-1, keepdims=True), 1e-30)

def rope_tables(seq):
    pos = jnp.arange(seq, dtype=jnp.float32)
    inv = ROPE_THETA ** (-jnp.arange(0, ROPE_DIM, 2, dtype=jnp.float32) / ROPE_DIM)
    ang = pos[:, None] * inv[None, :]
    return jnp.cos(ang), jnp.sin(ang)

def partial_rope(x, cos, sin):
    half = ROPE_DIM // 2
    x1, x2, xp = x[..., :half], x[..., half:ROPE_DIM], x[..., ROPE_DIM:]
    c = cos.astype(x.dtype)
    s = sin.astype(x.dtype)
    return jnp.concatenate([x1 * c - x2 * s, x1 * s + x2 * c, xp], axis=-1)

def heads(a, n):
    B, T, W = a.shape
    return a.reshape(B, T, n, W // n).transpose(0, 2, 1, 3)

def hgrn2_chunkwise(q, log_f, k, v):
    B, H, T, DK = q.shape
    DV = v.shape[-1]
    C = HG_CHUNK
    N = T // C

    def to_chunks(a):
        return jnp.moveaxis(a.reshape(B, H, N, C, a.shape[-1]), 2, 0)

    causal = jnp.tril(jnp.ones((C, C), dtype=bool))[:, :, None]

    def step(S, inp):
        qi, lfi, ki, vi = inp
        b = jnp.cumsum(lfi.astype(jnp.float32), axis=-2)
        diff = b[..., :, None, :] - b[..., None, :, :]
        decay = jnp.exp(jnp.where(causal, diff, -jnp.inf))
        A = jnp.einsum('bhtd,bhsd,bhtsd->bhts', qi, ki, decay)
        o = jnp.einsum('bhts,bhsv->bhtv', A, vi) + jnp.einsum('bhtd,bhdv->bhtv', qi * jnp.exp(b), S)
        b_last = b[..., -1:, :]
        S_new = jnp.exp(b_last[..., 0, :])[..., None] * S + jnp.einsum(
            'bhsd,bhsv->bhdv', ki * jnp.exp(b_last - b), vi)
        return S_new, o

    S0 = jnp.zeros((B, H, DK, DV), jnp.float32)
    _, o = lax.scan(step, S0, (to_chunks(q), to_chunks(log_f), to_chunks(k), to_chunks(v)))
    return jnp.moveaxis(o, 0, 2).reshape(B, H, T, DV).astype(v.dtype)

def compress(kv, pe, w1, w2):
    B, G, T, dh = kv.shape
    NC = (T - CMP_BLOCK) // CMP_STRIDE + 1
    idx = jnp.arange(NC)[:, None] * CMP_STRIDE + jnp.arange(CMP_BLOCK)[None, :]
    blocks = kv[:, :, idx, :] + pe
    flat = blocks.reshape(B, G, NC, CMP_BLOCK * dh)
    return jax.nn.silu(flat @ w1) @ w2

def window_attn(q, k, v, scale):
    B, KVH, G, T, dh = q.shape
    NB = T // Q_BLOCK
    NW = WINDOW // Q_BLOCK
    pad = ((0, 0), (0, 0), (WINDOW, 0), (0, 0))
    kb = jnp.pad(k, pad).reshape(B, KVH, NB + NW, Q_BLOCK, dh)
    vb = jnp.pad(v, pad).reshape(B, KVH, NB + NW, Q_BLOCK, dh)
    band_k = jnp.concatenate([kb[:, :, i:i + NB] for i in range(NW + 1)], axis=3)
    band_v = jnp.concatenate([vb[:, :, i:i + NB] for i in range(NW + 1)], axis=3)
    qb = q.reshape(B, KVH, G, NB, Q_BLOCK, dh)
    s = jnp.einsum('bgnxqd,bgxkd->bgnxqk', qb, band_k) * scale
    qpos = jnp.arange(NB)[:, None] * Q_BLOCK + jnp.arange(Q_BLOCK)[None, :]
    kpos = jnp.arange(NB)[:, None] * Q_BLOCK - WINDOW + jnp.arange((NW + 1) * Q_BLOCK)[None, :]
    d = qpos[:, :, None] - kpos[:, None, :]
    mask = (d >= 0) & (d < WINDOW) & (kpos[:, None, :] >= 0)
    p = masked_softmax(s, mask)
    o = jnp.einsum('bgnxqk,bgxkd->bgnxqd', p.astype(v.dtype), band_v)
    return o.reshape(B, KVH, G, T, dh)

def selected_attn(q, k, v, sel, scale):
    B, KVH, G, T, dh = q.shape
    K = sel.shape[-1]
    NB = T // SLC_Q_BLOCK
    qb = jnp.moveaxis(q.reshape(B, KVH, G, NB, SLC_Q_BLOCK, dh), 3, 0)
    sb = jnp.moveaxis(sel.reshape(B, KVH, NB, SLC_Q_BLOCK, K), 2, 0)
    t0 = jnp.arange(NB) * SLC_Q_BLOCK
    bi = jnp.arange(B)[:, None, None, None]
    gi = jnp.arange(KVH)[None, :, None, None]

    def one(args):
        qx, sx, s0 = args
        tok = (sx[..., None] * SLC_BLOCK + jnp.arange(SLC_BLOCK)).reshape(B, KVH, SLC_Q_BLOCK, K * SLC_BLOCK)
        kg = k[bi, gi, tok]
        vg = v[bi, gi, tok]
        s = jnp.einsum('bgnqd,bgqkd->bgnqk', qx, kg) * scale
        qpos = s0 + jnp.arange(SLC_Q_BLOCK)
        mask = (tok <= qpos[:, None])[:, :, None]
        p = masked_softmax(s, mask)
        return jnp.einsum('bgnqk,bgqkd->bgnqd', p.astype(vg.dtype), vg)

    o = lax.map(one, (qb, sb, t0))
    return jnp.moveaxis(o, 0, 3).reshape(B, KVH, G, T, dh)

def first_inputs(seed: int = 0) -> dict:
    key = jax.random.key(seed)
    ks = jax.random.split(key, 16)
    n = jax.random.normal
    f32 = jnp.float32
    return {
        "x": n(ks[0], (BATCH, SEQ, D_MODEL), f32),
        "p": n(ks[1], (DEPTH, BATCH, SEQ, PLE_DIM), f32),
        "norm_g": 1.0 + 0.05 * n(ks[2], (DEPTH, D_MODEL), f32),
        "w_in": n(ks[3], (DEPTH, D_MODEL, IN_COLS), f32) * D_MODEL ** -0.5,
        "hgrn_lb": 0.5 * n(ks[4], (DEPTH, HG_HEADS * HG_DK), f32),
        "hgrn_onorm_g": 1.0 + 0.05 * n(ks[5], (DEPTH, HG_DV), f32),
        "nsa_qnorm_g": 1.0 + 0.05 * n(ks[6], (DEPTH, NSA_DH), f32),
        "nsa_knorm_g": 1.0 + 0.05 * n(ks[7], (DEPTH, 3, NSA_DH), f32),
        "cmp_pe": 0.1 * n(ks[8], (DEPTH, 2, CMP_BLOCK, NSA_DH), f32),
        "cmp_w1": n(ks[9], (DEPTH, 2, CMP_BLOCK * NSA_DH, CMP_HIDDEN), f32) * (CMP_BLOCK * NSA_DH) ** -0.5,
        "cmp_w2": n(ks[10], (DEPTH, 2, CMP_HIDDEN, NSA_DH), f32) * CMP_HIDDEN ** -0.5,
        "w_out": n(ks[11], (DEPTH, D_MIX, D_MODEL), f32) * (0.5 * D_MIX ** -0.5),
        "ple_norm_g": 1.0 + 0.05 * n(ks[12], (DEPTH, D_MODEL), f32),
        "w_pg": n(ks[13], (DEPTH, D_MODEL, D_MODEL), f32) * D_MODEL ** -0.5,
        "w_pp": n(ks[14], (DEPTH, PLE_DIM, D_MODEL), f32) * (0.5 * PLE_DIM ** -0.5),
    }

def first_block(x, p, norm_g, w_in, hgrn_lb, hgrn_onorm_g, nsa_qnorm_g, nsa_knorm_g,
              cmp_pe, cmp_w1, cmp_w2, w_out, ple_norm_g, w_pg, w_pp):
    B, T, _ = x.shape
    KVH, G, dh = NSA_KV_HEADS, NSA_G, NSA_DH
    scale = dh ** -0.5
    split_points = np.cumsum(IN_SPLITS)[:-1].tolist()

    cos, sin = rope_tables(T)
    lb_all = jnp.cumsum(jax.nn.softmax(hgrn_lb.astype(jnp.float32), axis=0), axis=0)
    lb_all = lb_all - lb_all[0]

    NC = (T - CMP_BLOCK) // CMP_STRIDE + 1
    NSB = T // SLC_BLOCK
    top_k = min(SLC_TOPK, NSB)
    c_tok = jnp.arange(NC)[:, None] * CMP_STRIDE + jnp.arange(CMP_BLOCK)[None, :]
    overlap = jnp.mean((c_tok[..., None] // SLC_BLOCK == jnp.arange(NSB)).astype(jnp.float32), axis=1)
    c_end = jnp.arange(NC) * CMP_STRIDE + CMP_BLOCK - 1
    cmp_mask = c_end[None, :] <= jnp.arange(T)[:, None]
    cur = (jnp.arange(T) // SLC_BLOCK)[:, None]
    jb = jnp.arange(NSB)[None, :]
    forced = (jb == 0) | (jb == cur) | (jb == cur - 1)
    eligible = jb <= cur

    h = x
    for i in range(DEPTH):
        xn = rmsnorm(h, norm_g[i])
        proj = xn @ w_in[i]
        (hq, hf, hi, hgo, hz, nq, kcm, vcm, ksl, vsl, kwn, vwn, ngate, nz) = jnp.split(proj, split_points, axis=-1)

        lb = lb_all[i].reshape(HG_HEADS, 1, HG_DK)
        fl = heads(hf, HG_HEADS).astype(jnp.float32)
        log_f = jnp.logaddexp(jnp.log(lb), jnp.log1p(-lb) + jax.nn.log_sigmoid(fl))
        k_hg = (1.0 - lb) * jax.nn.sigmoid(-fl)
        o_hg = hgrn2_chunkwise(heads(hq, HG_HEADS), log_f, k_hg, heads(hi, HG_HEADS))
        o_hg = rmsnorm(o_hg, hgrn_onorm_g[i]).transpose(0, 2, 1, 3).reshape(B, T, HG_W)
        y_hg = o_hg * jax.nn.sigmoid(hgo) * jax.nn.silu(hz)

        qn = rmsnorm(heads(nq, NSA_HEADS), nsa_qnorm_g[i])
        q_nope = qn.reshape(B, KVH, G, T, dh)
        q_rope = partial_rope(qn, cos, sin).reshape(B, KVH, G, T, dh)

        kc = rmsnorm(compress(heads(kcm, KVH), cmp_pe[i, 0], cmp_w1[i, 0], cmp_w2[i, 0]), nsa_knorm_g[i, 0])
        vc = compress(heads(vcm, KVH), cmp_pe[i, 1], cmp_w1[i, 1], cmp_w2[i, 1])
        s_cmp = jnp.einsum('bgntd,bgcd->bgntc', q_nope, kc) * scale
        p_cmp = masked_softmax(s_cmp, cmp_mask)
        o_cmp = jnp.einsum('bgntc,bgcd->bgntd', p_cmp.astype(vc.dtype), vc)

        imp = jnp.einsum('bgntc,cj->bgtj', p_cmp, overlap)
        score = jnp.where(forced, FORCE_SCORE, jnp.where(eligible, imp, -1.0))
        _, sel = lax.top_k(score, top_k)
        k_sl = partial_rope(rmsnorm(heads(ksl, KVH), nsa_knorm_g[i, 1]), cos, sin)
        o_slc = selected_attn(q_rope, k_sl, heads(vsl, KVH), sel, scale)

        k_wn = partial_rope(rmsnorm(heads(kwn, KVH), nsa_knorm_g[i, 2]), cos, sin)
        o_win = window_attn(q_rope, k_wn, heads(vwn, KVH), scale)

        gates = jax.nn.sigmoid(ngate).reshape(B, T, 3, KVH, G).transpose(2, 0, 3, 4, 1)[..., None]
        o_nsa = gates[0] * o_cmp + gates[1] * o_slc + gates[2] * o_win
        o_nsa = o_nsa.reshape(B, NSA_HEADS, T, dh).transpose(0, 2, 1, 3).reshape(B, T, NSA_W)
        y_nsa = o_nsa * jax.nn.silu(nz)

        h = h + jnp.concatenate([y_hg, y_nsa], axis=-1) @ w_out[i]

        gate = jax.nn.sigmoid(rmsnorm(h, ple_norm_g[i]) @ w_pg[i])
        h = h + gate * (p[i] @ w_pp[i])
    return h


MEM_LEN = 256
CONV_WIDTH = 256
CONV_K = 3
RET_HEADS = 4
RET_QK_DIM = 64
RET_V_DIM = 128
RET_CHUNK = 128
RET_QK = RET_HEADS * RET_QK_DIM
RET_V = RET_HEADS * RET_V_DIM
ROPE_BASE = 10000.0
SG_GROUPS = 4
SG_GROUP_DIM = 64
SG_WIDTH = SG_GROUPS * SG_GROUP_DIM
SG_CHUNK = 128
N_BRANCH = 3
XA_HEADS = 4
XA_HEAD_DIM = D_MODEL // XA_HEADS
D_FF = -(-8 * D_MODEL // (3 * 256)) * 256
EPS = 1e-6

IN_WIDTHS = (CONV_WIDTH, CONV_WIDTH, CONV_WIDTH,
             RET_QK, RET_QK, RET_V, RET_V,
             2 * SG_WIDTH,
             N_BRANCH * D_MODEL)
IN_COLS_2 = int(sum(IN_WIDTHS))
IN_SPLITS_2 = [int(s) for s in np.cumsum(IN_WIDTHS)[:-1]]


def rmsnorm_2(x, g):
    xf = x.astype(jnp.float32)
    y = xf * lax.rsqrt(jnp.mean(xf * xf, axis=-1, keepdims=True) + EPS)
    return (y * g.astype(jnp.float32)).astype(x.dtype)

def layernorm(x, g):
    xf = x.astype(jnp.float32)
    mu = jnp.mean(xf, axis=-1, keepdims=True)
    var = jnp.mean(jnp.square(xf - mu), axis=-1, keepdims=True)
    return ((xf - mu) * lax.rsqrt(var + EPS) * g.astype(jnp.float32)).astype(x.dtype)

def short_conv_mixer(a_x, a_c, a_b, conv_w):
    z = a_c * a_x
    S = z.shape[1]
    zp = jnp.pad(z, ((0, 0), (CONV_K - 1, 0), (0, 0)))
    y = sum(conv_w[k] * zp[:, k:k + S] for k in range(CONV_K))
    return a_b * y

def rotary(x):
    S, Dh = x.shape[1], x.shape[-1]
    half = Dh // 2
    inv = ROPE_BASE ** (-jnp.arange(half, dtype=jnp.float32) / half)
    ang = jnp.arange(S, dtype=jnp.float32)[:, None] * inv[None, :]
    cos = jnp.cos(ang)[None, :, None, :]
    sin = jnp.sin(ang)[None, :, None, :]
    xf = x.astype(jnp.float32)
    x1, x2 = xf[..., :half], xf[..., half:]
    return jnp.concatenate([x1 * cos - x2 * sin, x1 * sin + x2 * cos], axis=-1)

def retention(q, k, v, gn_gain):
    B, S, H, dk = q.shape
    dv = v.shape[-1]
    C = RET_CHUNK
    N = S // C
    out_dtype = v.dtype
    gamma = 1.0 - jnp.exp2(-5.0 - jnp.arange(H, dtype=jnp.float32))
    log_g = jnp.log(gamma)
    q = q.reshape(B, N, C, H, dk)
    k = k.reshape(B, N, C, H, dk) * (dk ** -0.5)
    v = v.astype(jnp.float32).reshape(B, N, C, H, dv)
    idx = jnp.arange(C, dtype=jnp.float32)
    diff = idx[:, None] - idx[None, :]
    decay = jnp.where(diff >= 0, jnp.exp(log_g[:, None, None] * jnp.maximum(diff, 0.0)), 0.0)
    scores = jnp.einsum('bnchd,bnmhd->bnhcm', q, k) * decay[None, None]
    inner = jnp.einsum('bnhcm,bnmhe->bnche', scores, v)
    zeta = jnp.exp(log_g[:, None] * (C - 1 - idx)[None, :])
    kv = jnp.einsum('bnmhd,bnmhe->nbhde', k, v * zeta.T[None, None, :, :, None])
    chunk_decay = jnp.exp(log_g * C)[None, :, None, None]

    def step(R, kv_n):
        return chunk_decay * R + kv_n, R

    _, R_prev = lax.scan(step, jnp.zeros((B, H, dk, dv), jnp.float32), kv)
    xi = jnp.exp(log_g[:, None] * (idx + 1.0)[None, :])
    cross = jnp.einsum('bnchd,nbhde->bnche', q, R_prev) * xi.T[None, None, :, :, None]
    o = (inner + cross).reshape(B, S, H, dv)
    mu = jnp.mean(o, axis=-1, keepdims=True)
    var = jnp.mean(jnp.square(o - mu), axis=-1, keepdims=True)
    o = ((o - mu) * lax.rsqrt(var + EPS)).reshape(B, S, H * dv) * gn_gain.astype(jnp.float32)
    return o.astype(out_dtype)

def spatial_gating(z, ln_g, w_s, b_s):
    B, S, _ = z.shape
    C = SG_CHUNK
    N = S // C
    u, v = jnp.split(z, 2, axis=-1)
    v = layernorm(v, ln_g).reshape(B, N, C, SG_GROUPS, SG_GROUP_DIM)
    mask = jnp.tril(jnp.ones((C, C), dtype=w_s.dtype))
    vm = jnp.einsum('gcm,bnmgd->bncgd', w_s * mask[None], v) + b_s.T[None, None, :, :, None]
    return u * vm.reshape(B, S, SG_WIDTH)

def cross_attention(h, mm, wq, wk, wv, wo):
    B, S, _ = h.shape
    M = mm.shape[1]
    q = (h @ wq).reshape(B, S, XA_HEADS, XA_HEAD_DIM)
    k = (mm @ wk).reshape(B, M, XA_HEADS, XA_HEAD_DIM)
    v = (mm @ wv).reshape(B, M, XA_HEADS, XA_HEAD_DIM)
    s = jnp.einsum('bshd,bmhd->bhsm', q, k).astype(jnp.float32) * (XA_HEAD_DIM ** -0.5)
    p = jax.nn.softmax(s, axis=-1).astype(v.dtype)
    o = jnp.einsum('bhsm,bmhd->bshd', p, v).reshape(B, S, D_MODEL)
    return o @ wo

def second_inputs(seed: int = 0) -> dict:
    key = jax.random.key(seed)
    ks = jax.random.split(key, 32)
    L = DEPTH
    f32 = jnp.float32

    def w(k, shape, fan_in):
        return jax.random.normal(k, shape, f32) * (fan_in ** -0.5)

    def gain(k, shape):
        return 1.0 + 0.02 * jax.random.normal(k, shape, f32)

    return {
        "x": jax.random.normal(ks[0], (BATCH, SEQ, D_MODEL), f32),
        "mem": jax.random.normal(ks[1], (BATCH, MEM_LEN, D_MODEL), f32),
        "norm_mix": gain(ks[2], (L, D_MODEL)),
        "w_in": w(ks[3], (L, D_MODEL, IN_COLS_2), D_MODEL),
        "conv_w": 0.5 * jax.random.normal(ks[4], (L, CONV_K, CONV_WIDTH), f32),
        "w_a_out": w(ks[5], (L, CONV_WIDTH, D_MODEL), CONV_WIDTH),
        "ret_gn": gain(ks[6], (L, RET_V)),
        "w_b_out": w(ks[7], (L, RET_V, D_MODEL), RET_V),
        "sg_ln": gain(ks[8], (L, SG_WIDTH)),
        "sg_w": w(ks[9], (L, SG_GROUPS, SG_CHUNK, SG_CHUNK), SG_CHUNK),
        "sg_b": 1.0 + 0.1 * jax.random.normal(ks[10], (L, SG_GROUPS, SG_CHUNK), f32),
        "w_c_out": w(ks[11], (L, SG_WIDTH, D_MODEL), SG_WIDTH),
        "w_o": w(ks[12], (L, D_MODEL, D_MODEL), D_MODEL),
        "norm_xa": gain(ks[13], (L, D_MODEL)),
        "norm_mem": gain(ks[14], (L, D_MODEL)),
        "xa_q": w(ks[15], (L, D_MODEL, D_MODEL), D_MODEL),
        "xa_k": w(ks[16], (L, D_MODEL, D_MODEL), D_MODEL),
        "xa_v": w(ks[17], (L, D_MODEL, D_MODEL), D_MODEL),
        "xa_o": w(ks[18], (L, D_MODEL, D_MODEL), D_MODEL),
        "norm_ffn": gain(ks[19], (L, D_MODEL)),
        "w1": w(ks[20], (L, D_MODEL, D_FF), D_MODEL),
        "w3": w(ks[21], (L, D_MODEL, D_FF), D_MODEL),
        "w2": w(ks[22], (L, D_FF, D_MODEL), D_FF),
        "final_norm": gain(ks[23], (D_MODEL,)),
    }

def second_block(x, mem, norm_mix, w_in, conv_w, w_a_out, ret_gn, w_b_out, sg_ln, sg_w, sg_b,
              w_c_out, w_o, norm_xa, norm_mem, xa_q, xa_k, xa_v, xa_o, norm_ffn, w1, w3, w2,
              final_norm):
    B, S, _ = x.shape
    for l in range(DEPTH):
        h = rmsnorm_2(x, norm_mix[l])
        p = h @ w_in[l]
        a_x, a_c, a_b, q, k, v, g, z, gates = jnp.split(p, IN_SPLITS_2, axis=-1)
        y_a = short_conv_mixer(a_x, a_c, a_b, conv_w[l]) @ w_a_out[l]
        qr = rotary(q.reshape(B, S, RET_HEADS, RET_QK_DIM))
        kr = rotary(k.reshape(B, S, RET_HEADS, RET_QK_DIM))
        r = retention(qr, kr, v.reshape(B, S, RET_HEADS, RET_V_DIM), ret_gn[l])
        y_b = (jax.nn.silu(g) * r) @ w_b_out[l]
        y_c = spatial_gating(jax.nn.gelu(z), sg_ln[l], sg_w[l], sg_b[l]) @ w_c_out[l]
        g_a, g_b, g_c = jnp.split(jax.nn.sigmoid(gates), N_BRANCH, axis=-1)
        merged = g_a * y_a + g_b * y_b + g_c * y_c
        x = x + merged @ w_o[l]
        h = rmsnorm_2(x, norm_xa[l])
        mm = rmsnorm_2(mem, norm_mem[l])
        x = x + cross_attention(h, mm, xa_q[l], xa_k[l], xa_v[l], xa_o[l])
        h = rmsnorm_2(x, norm_ffn[l])
        x = x + (jax.nn.silu(h @ w1[l]) * (h @ w3[l])) @ w2[l]
    return rmsnorm_2(x, final_norm)


def setup_inputs(seed=0):
    out = dict(first_inputs(seed))
    for name, value in second_inputs(seed + 1).items():
        if name != "x":
            out[name + "_2"] = value
    return out


def reference(
    x, p, norm_g, w_in, hgrn_lb, hgrn_onorm_g, nsa_qnorm_g, nsa_knorm_g, cmp_pe, cmp_w1, cmp_w2,
    w_out, ple_norm_g, w_pg, w_pp, mem_2, norm_mix_2, w_in_2, conv_w_2, w_a_out_2, ret_gn_2,
    w_b_out_2, sg_ln_2, sg_w_2, sg_b_2, w_c_out_2, w_o_2, norm_xa_2, norm_mem_2, xa_q_2, xa_k_2,
    xa_v_2, xa_o_2, norm_ffn_2, w1_2, w3_2, w2_2, final_norm_2,
):
    x = first_block(
        x, p, norm_g, w_in, hgrn_lb, hgrn_onorm_g, nsa_qnorm_g, nsa_knorm_g, cmp_pe, cmp_w1,
        cmp_w2, w_out, ple_norm_g, w_pg, w_pp,
    )
    return second_block(
        x, mem_2, norm_mix_2, w_in_2, conv_w_2, w_a_out_2, ret_gn_2, w_b_out_2, sg_ln_2, sg_w_2,
        sg_b_2, w_c_out_2, w_o_2, norm_xa_2, norm_mem_2, xa_q_2, xa_k_2, xa_v_2, xa_o_2,
        norm_ffn_2, w1_2, w3_2, w2_2, final_norm_2,
    )


_drawn_inputs = setup_inputs


def setup_inputs(seed=0):
    import zlib

    import numpy as np

    out = dict(_drawn_inputs(seed))
    spreads = {}
    factors = {'hgrn_onorm_g': 3.812,
     'nsa_qnorm_g': 8.0,
     'nsa_knorm_g': 8.0,
     'cmp_pe': 4.693,
     'ple_norm_g': 4.327,
     'ret_gn_2': 7.25,
     'sg_ln_2': 8.0,
     'norm_xa_2': 8.0,
     'norm_mem_2': 8.0,
     'norm_ffn_2': 2.951,
     'final_norm_2': 2.854}
    for name, (base, spread) in spreads.items():
        noise = np.random.default_rng([zlib.crc32(name.encode()), seed]).standard_normal(out[name].shape)
        drawn = base * np.exp(spread * noise) if base else spread * noise
        out[name] = __import__('jax').numpy.asarray(drawn.astype(out[name].dtype))
    for name, factor in factors.items():
        out[name] = (out[name] * factor).astype(out[name].dtype)
    return out
```

```python
from contextlib import ExitStack

import numpy as np

import concourse.bass as bass
from concourse import mybir

F32 = mybir.dt.float32
F32R = mybir.dt.float32r
BF16 = mybir.dt.bfloat16
U8 = mybir.dt.uint8
ALU = mybir.AluOpType
ACT = mybir.ActivationFunctionType
AX = mybir.AxisListType.X

P = 128
DEPTH = 2
D = 1024
T = 512
TT = T // P
KD = D // P
EPS = 1e-6
NEG = -1e30

HG = 4
LEVELS = 7
NH, NKV, DH = 8, 2, 64
NG = NH // NKV
NCMP = (T - 32) // 16 + 1
PLE = 256
MEM = 256
MT = MEM // P
RH, RK, RV = 4, 64, 128
SGG = 4
XH, XD = 4, 256
FT = 2816 // P

SLOTS = 4
SLOT = 1024
PARAMS_ONE = 16 * 7
PARAMS_TWO = 16 * 16
RESCALE = [float(np.exp(np.float32(np.log(np.float32(1 - 2.0 ** (-5 - i)))) * np.float32(P))) for i in range(RH)]


def constants():
    f = np.float32
    t = np.arange(T)
    tile = lambda a: np.ascontiguousarray(a.reshape(TT, P, -1).transpose(1, 0, 2)).reshape(P, -1)
    i, j = np.arange(P)[:, None], np.arange(P)[None, :]
    one = {}
    one["ident"] = np.eye(P, dtype=f)
    one["causal"] = np.where(j > i, NEG, 0).astype(f)
    inv = f(500000.0) ** (-np.arange(0, 16, 2, dtype=f) / f(16))
    ang = t[:, None].astype(f) * inv[None, :]
    one["cos"], one["sin"] = tile(np.cos(ang).astype(f)), tile(np.sin(ang).astype(f))
    seen = (np.arange(NCMP)[None, :] * 16 + 31) <= t[:, None]
    one["cbias"] = tile(np.where(seen, 0, NEG).astype(f))
    one["cseen"] = tile(seen.astype(f))
    two = {}
    inv = f(10000.0) ** (-np.arange(32, dtype=f) / f(32))
    ang = t[:, None].astype(f) * inv[None, :]
    two["rcos"], two["rsin"] = tile(np.cos(ang).astype(f)), tile(np.sin(ang).astype(f))
    lg = np.log((1.0 - np.exp2(-5.0 - np.arange(RH))).astype(f))
    c = np.arange(P, dtype=f)
    dec = np.where(j >= i, np.exp(lg[:, None, None] * np.maximum(j - i, 0).astype(f)), 0) * f(RK ** -0.5)
    two["decay"] = dec.transpose(1, 0, 2).reshape(P, -1).astype(f)
    two["zeta"] = (np.exp(lg[None, :] * (P - 1 - c)[:, None]) * f(RK ** -0.5)).astype(f)
    xi = np.exp(lg[:, None] * (c + 1)[None, :]).astype(f)
    two["xi"] = np.repeat(xi.reshape(2, 2, 1, P), RK, axis=2).reshape(2, P, P).transpose(1, 0, 2).reshape(P, -1)
    two["tril"] = (j <= i).astype(f)
    masks = np.zeros((P, LEVELS + 1, P), f)
    for lv in range(LEVELS):
        m = 64 >> lv
        masks[:, lv, :] = (i // (2 * m) == j // (2 * m)) & (i // m % 2 == 0) & (j // m % 2 == 1)
    masks[:, LEVELS, :] = i == j
    return one, two, masks.reshape(P, -1)


def fm_chunks(w, c0, tiles):
    return [(w, 0, KD, c0 + P * i, P) for i in range(tiles)]


def tm_chunks(w, c0, cols, tiles=KD, step=2, k0=0):
    return [(w, k, min(step, k0 + tiles - k), c0, cols) for k in range(k0, k0 + tiles, step)]


class Signal:

    def __init__(self, sem, before, per):
        self.sem, self.before, self.per = sem, before, per
        self.made = self.seen = 0

    def up(self):
        self.made += 1
        return self.sem, 1

    def at(self, l, n):
        return self.sem, l * self.per + (self.before + n)

    def next(self, l):
        self.seen += 1
        return self.at(l, self.seen)

    def last(self, l):
        return self.at(l, self.made)


class Groups:

    def __init__(self, steps, groups_of, banks, filled, emptied):
        self.place, used, turn = {}, [0] * 8, {}
        for step in steps:
            for name, choice in groups_of(step):
                n = turn.get(choice, 0)
                turn[choice] = n + 1
                b = choice[n % len(choice)]
                self.place[name] = (b, used[b])
                used[b] += 1
        self.banks, self.f, self.e = banks, filled, emptied

    def ps(self, name):
        return self.banks[self.place[name][0]]

    def free(self, name, l):
        b, n = self.place[name]
        return self.e[b].at(l, n)

    def full(self, name):
        return self.f[self.place[name][0]].up()

    def filled(self, name, l):
        b, n = self.place[name]
        return self.f[b].at(l, n + 1)

    def empty(self, name):
        return self.e[self.place[name][0]].up()

    def evacuated(self, name, l):
        b, n = self.place[name]
        return self.e[b].at(l, n + 1)


ALL, LOW, HIGH = tuple(range(8)), (0, 1, 2, 3), (4, 5, 6, 7)


def merged_in(main, side, first):
    out, n = list(main[:first]), len(main) - first
    done = 0
    for i, step in enumerate(main[first:]):
        out.append(step)
        upto = -(-len(side) * (i + 1) // n)
        out += side[done:upto]
        done = upto
    return out


def fm(kind, w, c0, tiles):
    return [("fm", kind, i, s) for i, s in enumerate(fm_chunks(w, c0, tiles))]


def tm(kind, *a, **k):
    specs = tm_chunks(*a, **k)
    return [("tm", kind, i, len(specs), s) for i, s in enumerate(specs)]


def steps_one():
    main = (tm("v", "w_in", 1024, 512) + tm("go", "w_in", 1536, 512) + tm("z", "w_in", 2048, 512)
            + tm("nq", "w_in", 2560, 512)
            + tm("ks", "w_in", 3328, 256) + tm("kw", "w_in", 3584, 280) + tm("nz", "w_in", 3864, 512))
    side = []
    for h in range(HG):
        side += [("hg_prep", h)] + [("hg_level", h, lv) for lv in range(LEVELS + 1)] + [("hg_kv", h), ("hg_out", h)]
    s = [("norm", "mix")] + fm("hq", "w_in", 0, HG) + fm("hf", "w_in", 512, HG) + merged_in(main, side, 12) + tm("kc", "w_in", 3072, 256, step=4)
    s += [("q_norm",), ("k_norm",)]
    for w in range(2):
        s += [("c_in", w)] + [("c_hid", w, i, (f"cmp_w1_{w}", 8 * i, 8, 0, P)) for i in range(2)]
    s += [("hg_turn", h) for h in range(HG)]
    s += [("c_out",), ("q_rope",), ("c_key",), ("p_turn",)]
    for qt in range(TT):
        s += [("c_att", qt)] + [("att", qt, br, h) for br in range(2) for h in range(NH)] + [("att_out", qt)]
    for n in range(2):
        s += tm(f"out{n}", "w_out", 512 * n, 512)
    s += [("norm", "ple")]
    for n in range(2):
        s += tm(f"pp{n}", "w_pp", 512 * n, 512, tiles=2) + tm(f"pg{n}", "w_pg", 512 * n, 512)
    return s


def groups_one(step):
    kind = step[0]
    if kind == "norm":
        return [((step[1], k), HIGH + LOW) for k in range(KD)]
    if kind == "fm":
        return [((step[1], step[2]), HIGH)]
    if kind == "tm":
        high = step[1][:2] == "pp"
        return [((step[1], tt), ((4 + tt) if high else tt,)) for tt in range(TT)] if step[2] == 0 else []
    if kind == "hg_prep":
        return [(("kd", step[1]), HIGH)]
    if kind == "hg_level":
        return [(("A", step[1], step[2]), HIGH)]
    if kind == "hg_kv":
        return [(("kv", step[1]), HIGH)]
    if kind == "hg_out":
        return [(("o", step[1]), HIGH)]
    if kind == "hg_turn":
        return [(("yT", step[1]), HIGH)]
    if kind == "p_turn":
        return [(("pT", k), HIGH) for k in range(PLE // P)]
    if kind == "q_norm":
        return [(("qn", n), LOW) for n in range(NG)]
    if kind == "q_rope":
        return [(("qr", n), LOW) for n in range(NG)]
    if kind == "k_norm":
        return [(("kT", br), LOW) for br in range(2)]
    if kind == "c_in":
        return ([(("pe",), HIGH)] if step[1] == 0 else []) + [(("ct", step[1], g), HIGH) for g in range(NKV)]
    if kind == "c_hid":
        return [(("ch", step[1]), HIGH)] if step[2] == 0 else []
    if kind == "c_out":
        return [(("co",), HIGH)]
    if kind == "c_key":
        return [(("ck",), HIGH)]
    if kind == "c_att":
        qt = step[1]
        return [(("cs", qt, g), (3 + g,)) for g in range(NKV)] + [(("cp", qt, i), (3 + i,)) for i in range(2)] + [(("o_c", qt), (7,))]
    if kind == "att":
        qt, br, h = step[1:]
        return [(("s",) + step[1:], (0, 1, 2)), (("p",) + step[1:], (3, 4))] + ([(("o_a", qt, br), (5 + br,))] if h == 0 else [])
    if kind == "att_out":
        return [(("nT", step[1]), (0, 1, 2))]
    return []


def numbered(steps):
    chunks = [s for s in steps if isinstance(s[-1], tuple) and len(s[-1]) == 5]
    return {s: j for j, s in enumerate(chunks)}, [s[-1] for s in chunks]


HALVES = ((0, 12), (12, FT))


def steps_two():
    s = [("norm", "mix")] + fm("ax", "w_in_2", 0, 2) + tm("g", "w_in_2", 1792, 512) + tm("qk", "w_in_2", 768, 512) + tm("v", "w_in_2", 1280, 512)
    conv = fm("ac", "w_in_2", 256, 2) + fm("ab", "w_in_2", 512, 2)
    ret = []
    for p in range(RH // 2):
        ret += [("ret_pair", p)]
        for hh in (2 * p, 2 * p + 1):
            ret += [("ret_in", hh), ("ret_out", hh)]
    s += merged_in(conv + tm("z", "w_in_2", 2304, 512)[:3], ret + [("ret_turn", hh) for hh in range(RH)], 0)
    s += tm("z", "w_in_2", 2304, 512)[3:]
    width = {"a": 2, "b": 4, "c": 2}

    def branch(b, n):
        col = 2816 + D * "abc".index(b) + 512 * n
        return tm(f"g{b}{n}", "w_in_2", col, 512) + tm(f"y{b}{n}", f"w_{b}_out_2", 512 * n, 512, tiles=width[b])

    s += merged_in(branch("a", 0) + branch("a", 1), [("sg_w",), ("sg_norm",), ("sg_mix",), ("sg_turn",)], 0)
    for b in "bc":
        s += branch(b, 0) + branch(b, 1)
    s += [("mg_turn",)]
    for n in range(2):
        s += tm(f"wo{n}", "w_o_2", 512 * n, 512)
    s += [("norm", "xa")] + fm("xq", "xa_q_2", 0, KD) + [("mem",)] + fm("xk", "xa_k_2", 0, KD)
    for n in range(2):
        s += tm(f"xv{n}", "xa_v_2", 512 * n, 512)
    s += [("xatt", hh, qt) for hh in range(XH) for qt in range(TT)]
    for n in range(2):
        s += tm(f"xw{n}", "xa_o_2", 512 * n, 512)
    s += [("norm", "ffn")]
    for i, (a, b) in enumerate(HALVES):
        for f in range(a, b):
            s += [("fm", "u", f, ("w1_2", 0, KD, f * P, P)), ("fm", "w", f, ("w3_2", 0, KD, f * P, P))]
        for n in range(2):
            s += tm(f"d{i}{n}", "w2_2", 512 * n, 512, tiles=b - a, k0=a)
    return s


def groups_two(step):
    kind = step[0]
    if kind == "norm":
        return [((step[1], k), HIGH + LOW) for k in range(KD)]
    if kind == "fm":
        return [((step[1], step[2]), HIGH)]
    if kind == "tm":
        return [((step[1], tt), (tt,)) for tt in range(MT if step[1][:2] == "xv" else TT)] if step[2] == 0 else []
    if kind == "ret_pair":
        return [(("qP", step[1]), HIGH), (("kP", step[1]), HIGH)]
    if kind == "ret_in":
        return [(("rs", step[1]), HIGH), (("rk", step[1]), HIGH)]
    if kind == "ret_out":
        return [(("ro", step[1]), HIGH)]
    if kind == "ret_turn":
        return [(("ybT", step[1]), HIGH)]
    if kind == "sg_w":
        return [(("ws",), HIGH)]
    if kind == "sg_mix":
        return [(("vm", tt), HIGH) for tt in range(TT)]
    if kind == "sg_turn":
        return [(("ycT", k), HIGH) for k in range(2)]
    if kind == "mg_turn":
        return [(("mT", k), HIGH + LOW) for k in range(KD)]
    if kind == "mem":
        return [(("mm", k), LOW) for k in range(KD)]
    if kind == "xatt":
        hh, qt = step[1:]
        out = [(("xs", hh, qt), (0, 1, 2)), (("xp", hh, qt), (3, 4))]
        return out + ([(("xo", hh, i), (5, 6, 7)) for i in range(2)] if qt == TT - 1 else [])
    return []


def build(nc, d, out, counts):
    made = []

    with ExitStack() as ctx:
        def sb(name, shape, dt=F32, where=ctx):
            return where.enter_context(nc.sbuf_tensor(name, shape, dt))

        def sem(name):
            return ctx.enter_context(nc.semaphore(name))

        raw = sb("raw", [P, SLOTS, SLOT])
        whi = sb("whi", [P, SLOTS, SLOT], F32R)
        wlo = sb("wlo", [P, SLOTS, SLOT], F32R)
        h = sb("h", [P, TT, D])
        xhi = sb("xhi", [P, KD, T], F32R)
        xlo = sb("xlo", [P, KD, T], F32R)
        ident = sb("ident", [P, P])
        eps = sb("eps", [P, 1])
        ones = sb("ones", [P, 1])
        ss = sb("ss", [P, TT])
        rstd = sb("rstd", [P, TT])
        lnv = sb("lnv", [P, 32])
        et = sb("et", [P, 2, T])
        sq = sb("sq", [P, 2, T])
        tA, tB, tC, tD = (sb(f"t{c}", [P, T]) for c in "ABCD")
        diag = tD[:, :].rearrange("p (t q) -> p t q", t=TT)
        banks = [ctx.enter_context(nc.psum_tensor(f"bank{b}", [P, 512], F32)) for b in range(8)]

        one = ExitStack()
        k1 = {n: sb("k1_" + n, [P, w], where=one) for n, w in d["w1"].items() if n not in ("ident", "causal")}
        identb = sb("identb", [P, P], BF16, one)
        causal = sb("causal", [P, P], BF16, one)
        masks = sb("masks", [P, LEVELS + 1, P], U8, one)
        lbraw = sb("lbraw", [P, 2, HG], where=one)
        lbt = sb("lbt", [P, DEPTH, 3, HG], where=one)
        lbs = sb("lbs", [P, 6, HG], where=one)
        lbc = sb("lbc", [P, 3, HG], where=one)
        gmix = sb("gmix", [P, KD], where=one)
        gple = sb("gple", [P, KD], where=one)
        onorm = sb("onorm", [P, P], where=one)
        qg = sb("qg", [P, DH], where=one)
        kg = sb("kg", [P, 3, DH], where=one)
        w2 = sb("w2", [P, 2, DH], where=one)
        pe_raw = sb("pe_raw", [P, P], where=one)
        qT = sb("qT", [P, HG, T], where=one)
        kT = sb("kT", [P, HG, T], where=one)
        bT = sb("bT", [P, HG, T], where=one)
        ghg = sb("ghg", [P, TT, T], where=one)
        dE = sb("dE", [P, 2, T], where=one)
        Ql = sb("Ql", [P, 2, T], where=one)
        Kl = sb("Kl", [P, 2, T], where=one)
        At = sb("At", [P, 2, TT, P], where=one)
        decays = sb("decays", [P, 4, T], where=one)
        eB, kdx, qdec, kdec = (decays[:, i, :] for i in range(4))
        kdt = tC[:, :].rearrange("p (c d) -> p c d", c=TT)
        ebl = sb("ebl", [P, TT], where=one)
        S = tB[:, 0:(TT - 1) * P].rearrange("p (c d) -> p c d", c=TT - 1)
        ssh = sb("ssh", [P, TT], where=one)
        rsh = sb("rsh", [P, TT], where=one)
        kk = sb("kk", [P, TT, 2, P], where=one)
        vv = sb("vv", [P, TT, 2, P], where=one)
        nzs = sb("nzs", [P, TT, T], where=one)
        gts = sb("gts", [P, TT, 3, NH], where=one)
        ssq = sb("ssq", [P, TT, NH], where=one)
        rsq = sb("rsq", [P, TT, NH], where=one)
        ssk = sb("ssk", [P, 16], where=one)
        rsk = sb("rsk", [P, 16], where=one)
        peT = sb("peT", [P, 2, 16], where=one)
        ssc = sb("ssc", [32, 2], where=one)
        rsc = sb("rsc", [32, 2], where=one)
        mx = sb("mx", [P, NH], where=one)
        nm = sb("nm", [P, 4], where=one)
        sums = sb("sums", [P, 3, NH], where=one)
        coef = sb("coef", [P, 3, NH], where=one)
        qTn, qTr, kTn = qT, kT, bT
        cin = bT[:, 2:4, :].rearrange("p a t -> p (a t)")[:, 0:16 * 2 * NCMP].rearrange("p (j g c) -> p j g c", j=16, g=2)
        cs = eB[:, 0:NH * NCMP].rearrange("p (h c) -> p h c", h=NH)
        ce = kdx[:, 0:NH * NCMP].rearrange("p (h c) -> p h c", h=NH)
        pcT = Kl[0:32, :, :].rearrange("p a (b q) -> p (a b) q", q=P)
        hid = Ql[:, 0, 0:4 * NCMP].rearrange("p (w c) -> p w c", w=2)
        kcn = Ql[:, 1, 0:P].rearrange("p (g d) -> p g d", g=NKV)
        vc = eB[0:32, 256:256 + P].rearrange("p (g d) -> p g d", g=NKV)
        kcT = eB[:, 384:416]
        kvc = decays[:, :, :].rearrange("p i (w a d) -> p i w a d", a=2, d=DH)
        p_raw = kk[:, :, :, :].rearrange("p t b c -> p t (b c)")
        Pb, Pt, y = dE, Ql, qdec
        with ExitStack() as early:
            v = sb("v", [P, TT, T], where=early)
            q = sb("q", [P, TT, NG, NKV, DH], where=early)
        chi, clo = (sb(n, [P, 16, 2, NCMP], F32R, one) for n in ("chi", "clo"))
        sb("beside_q", [P, 64], where=one)
        pT = sb("pT", [P, 2, 2, T], F32R, one)
        one.close()

        two = ExitStack()
        k2 = {n: sb("k2_" + n, [P, w], where=two) for n, w in d["w2"].items()}
        gmix2, gxa, gmem, gffn = (sb(n, [P, KD], where=two) for n in ("gmix2", "gxa", "gmem", "gffn"))
        convw = sb("convw", [P, 2, 3], where=two)
        sgb = sb("sgb", [P, SGG], where=two)
        ssm = sb("ssm", [P, 8], where=two)
        rsm = sb("rsm", [P, 8], where=two)
        mux = sb("mux", [P, TT], where=two)
        ssv = sb("ssv", [P, TT], where=two)
        rsv = sb("rsv", [P, TT], where=two)
        nmx = sb("nmx", [P, 4], where=two)
        sumx = sb("sumx", [P, 4], where=two)
        recx = sb("recx", [P, 4], where=two)
        mix = ExitStack()
        yaT = sb("yaT", [P, 2, 2, T], F32R, mix)
        ybT = sb("ybT", [P, 2, RH, T], F32R, mix)
        ycT = sb("ycT", [P, 2, 2, T], F32R, mix)
        mg = sb("mg", [P, TT, D], where=mix)
        qkr = mg[:, 0:2, :].rearrange("p a (b h d) -> p (a b) h d", b=2, d=RK)
        v2 = mg[:, 2:4, :].rearrange("p a (b n) -> p (a b) n", b=2)
        gg = sb("gg", [P, TT, T], where=mix)
        qp, kp, qx = (sb(n, [P, T], where=mix) for n in ("qp", "kp", "qx"))
        ds = sb("ds", [P, T], where=mix)
        R = sb("R", [P, TT - 1, P], where=mix)
        wsT = sb("wsT", [P, SGG, P], where=mix)
        sgw = sb("sgw", [P, SGG, P], where=mix)
        cx = sb("cx", [P, 2, T], where=mix)
        zp = sb("zp", [P, 2, T + 2], where=mix)
        retgn = sb("retgn", [P, T], where=mix)
        sgln = sb("sgln", [P, 256], where=mix)
        mix.close()
        xat = ExitStack()
        mem = sb("mem", [P, MT, D], where=xat)
        mmT = sb("mmT", [P, 2, KD, MEM], F32R, xat)
        qx8 = sb("qx8", [P, KD, T], where=xat)
        kx8 = sb("kx8", [P, KD, MEM], where=xat)
        vx = sb("vx", [P, MT, D], where=xat)
        Px = sb("Px", [P, 2, MEM], where=xat)
        PxT = sb("PxT", [P, 2, MT, T], where=xat)
        xat.close()
        ffn = ExitStack()
        gT = sb("gT", [P, 2, HALVES[0][1], T], F32R, ffn)
        gfin = sb("gfin", [P, D], where=ffn)
        ffn.close()
        two.close()

        def signal(name, credit=0):
            s = sem(name)
            per = [counts.get((name, st), 0) for st in (1, 2)]
            pair = [Signal(s, credit, per[0]), Signal(s, credit + DEPTH * per[0], per[1])]
            for st, one_ in enumerate(pair):
                made.append((name, st + 1, one_))
            return pair

        f_pairs = [signal(f"filled{b}") for b in range(8)]
        e_pairs = [signal(f"emptied{b}", 1) for b in range(8)]
        steps1, steps2 = steps_one(), steps_two()
        G1 = Groups(steps1, groups_one, banks, [x[0] for x in f_pairs], [x[0] for x in e_pairs])
        G2 = Groups(steps2, groups_two, banks, [x[1] for x in f_pairs], [x[1] for x in e_pairs])
        number1, chunks1 = numbered(steps1)
        number2, chunks2 = numbered(steps2)
        N1, N2 = len(chunks1), len(chunks2)
        assert N1 % SLOTS == 0 and N2 % SLOTS == 0, (N1, N2)

        raw_loaded = [sem(f"raw_loaded{i}") for i in range(SLOTS)]
        hi_split = sem("hi_split")
        lo_split = sem("lo_split")
        chunk_begun = sem("chunk_begun")
        setup = sem("setup")
        made_ready = sem("made_ready")
        params = [sem("params1"), sem("params2")]

        class Ring:

            def __init__(self, base, n):
                self.base, self.n = base, n

            def loaded(self, l, j):
                return raw_loaded[j % SLOTS], l * (16 * self.n // SLOTS) + 16 * ((self.base + j) // SLOTS + 1)

            def raw_free(self, l, j):
                return lo_split, l * self.n + (self.base + j + 1)

            def parts_free(self, l, j):
                return chunk_begun, l * self.n + (self.base + j + 1)

            def split(self, l, j):
                return lo_split, l * self.n + (self.base + j + 1 + SLOTS)

        ring1, ring2 = Ring(0, N1), Ring(DEPTH * N1, N2)

        dve_step, act_step = signal("dve_step"), signal("act_step")
        hi_done = signal("hi_done")
        exp_done = signal("exp_done")
        sq_done = signal("sq_done")
        ss_done = signal("ss_done")
        rs_done = signal("rs_done")
        diag_ready = signal("diag_ready")
        fg_b, fg_c, fg_d = (signal(f"forget_{c}")[0] for c in "bcd")
        b_ready = signal("b_ready")[0]
        d_ready, e_ready, qk_ready = signal("d_ready")[0], signal("e_ready")[0], signal("qk_ready")[0]
        prep_exp, prep_done = signal("prep_exp")[0], signal("prep_done")[0]
        q_ready, k_ready, qr_ready, kc_ready = (signal(n)[0] for n in ("q_ready", "k_ready", "qr_ready", "kc_ready"))
        cin_ready, clo_ready = signal("cin_ready")[0], signal("clo_ready")[0]
        cs_ready, ce_done, cp_ready = (signal(n)[0] for n in ("cs_ready", "ce_done", "cp_ready"))
        nm_ready = signal("nm_ready")
        y_ready = signal("y_ready")
        sg_ready, rot_ready, qx_ready, yb_ready, sgw_ready = (signal(n)[1] for n in ("sg_ready", "rot_ready", "qx_ready", "yb_ready", "sgw_ready"))
        ya_ready, g_ready, mg_ready, px_ready = (signal(n)[1] for n in ("ya_ready", "g_ready", "mg_ready", "px_ready"))
        p_loaded = sem("p_loaded")
        mem_loaded = sem("mem_loaded")
        setup_step, act_setup = sem("setup_step"), sem("act_setup")
        gain_loaded = sem("gain_loaded")
        fin_step, fin_root, fin_done = sem("fin_step"), sem("fin_root"), sem("fin_done")
        out_done = sem("out_done")

        def tensor_one(pe, l):
            G, ring = G1, ring1

            def chunk(step):
                pe.wait_ge(*ring.split(l, number1[step]))
                return number1[step] % SLOTS

            def turn(name, tiles, src, m=P):
                pe.wait_ge(*G.free(name, l))
                for i in range(tiles):
                    mm = pe.transpose(G.ps(name)[:, i * P:i * P + m], src(i), ident[0:m, 0:m])
                mm.then_inc(*G.full(name))

            def product(step, names, rows, k_of):
                _, _, i, n, (_, k0, nk, _, cols) = step
                s = chunk(step)
                for tt in range(TT):
                    if i == 0:
                        pe.wait_ge(*G.free(names[tt], l))
                    for kk_ in range(nk):
                        a, b = rows[0][:, k_of(k0 + kk_), tt * P:(tt + 1) * P], rows[1][:, k_of(k0 + kk_), tt * P:(tt + 1) * P]
                        wh, wl = whi[:, s, kk_ * cols:(kk_ + 1) * cols], wlo[:, s, kk_ * cols:(kk_ + 1) * cols]
                        o = G.ps(names[tt])[:, 0:cols]
                        mm = pe.matmul(o, a, wh, start=(i == 0 and kk_ == 0), stop=False)
                        if tt == 0 and kk_ == 0:
                            mm.then_inc(chunk_begun, 1)
                        pe.matmul(o, a, wl, start=False, stop=False)
                        mm = pe.matmul(o, b, wh, start=False, stop=(i == n - 1 and kk_ == nk - 1))
                    if i == n - 1:
                        mm.then_inc(*G.full(names[tt]))

            def step_norm(step):
                which = step[1]
                pe.wait_ge(*diag_ready[0].next(l))
                for k in range(KD):
                    pe.wait_ge(*G.free((which, k), l))
                    for tt in range(TT):
                        mm = pe.matmul(G.ps((which, k))[:, tt * P:(tt + 1) * P], h[:, tt, k * P:(k + 1) * P],
                                       diag[:, tt, :], start=True, stop=True)
                    mm.then_inc(*G.full((which, k)))

            def step_fm(step):
                name = step[1:3]
                s = chunk(step)
                pe.wait_ge(*G.free(name, l))
                for k in range(KD):
                    if name == ("hq", 0):
                        pe.wait_ge(*G.evacuated(("mix", k), l))
                    wh, wl = whi[:, s, k * P:(k + 1) * P], wlo[:, s, k * P:(k + 1) * P]
                    mm = pe.matmul(G.ps(name)[:, :], wh, xhi[:, k, :], start=(k == 0), stop=False)
                    if k == 0:
                        mm.then_inc(chunk_begun, 1)
                    pe.matmul(G.ps(name)[:, :], wh, xlo[:, k, :], start=False, stop=False)
                    mm = pe.matmul(G.ps(name)[:, :], wl, xhi[:, k, :], start=False, stop=(k == KD - 1))
                mm.then_inc(*G.full(name))

            def step_tm(step):
                kind, i = step[1], step[2]
                if i == 0 and kind == "out0":
                    for g in [("yT", hh) for hh in range(HG)] + [("nT", qt) for qt in range(TT)]:
                        pe.wait_ge(*G.evacuated(g, l))
                if i == 0 and kind == "pg0":
                    for k in range(KD):
                        pe.wait_ge(*G.evacuated(("ple", k), l))
                if kind[:2] == "pp":
                    for k in range(2):
                        pe.wait_ge(*G.evacuated(("pT", k), l))
                    rows = (pT[:, 0], pT[:, 1])
                else:
                    rows = (xhi, xlo)
                product(step, [(kind, tt) for tt in range(TT)], rows, lambda k: k)

            def step_p_turn(step):
                pe.wait_ge(p_loaded, l * 16 + 16)
                for k in range(2):
                    turn(("pT", k), TT, lambda tt: p_raw[:, tt, k * P:(k + 1) * P])

            def step_hg_prep(step):
                pe.wait_ge(*prep_done.at(l, step[1] + 1))
                turn(("kd", step[1]), TT, lambda c: kdec[:, c * P:(c + 1) * P])

            def step_hg_level(step):
                hh, lv = step[1:]
                name = ("A", hh, lv)
                if lv < LEVELS:
                    pe.wait_ge(*qk_ready.at(l, LEVELS * hh + lv + 1))
                    kl, ql = Kl[:, lv % 2], Ql[:, lv % 2]
                else:
                    kl, ql = kT[:, hh], qT[:, hh]
                pe.wait_ge(*G.free(name, l))
                for c in range(TT):
                    mm = pe.matmul(G.ps(name)[:, c * P:(c + 1) * P], kl[:, c * P:(c + 1) * P], ql[:, c * P:(c + 1) * P],
                                   start=True, stop=True)
                mm.then_inc(*G.full(name))

            def step_hg_kv(step):
                hh = step[1]
                name = ("kv", hh)
                if hh == 0:
                    for tt in range(TT):
                        pe.wait_ge(*G.evacuated(("v", tt), l))
                pe.wait_ge(*G.evacuated(("kd", hh), l))
                pe.wait_ge(*G.free(name, l))
                for c in range(TT - 1):
                    mm = pe.matmul(G.ps(name)[:, c * P:(c + 1) * P], kdt[:, c, :], v[:, c, hh * P:(hh + 1) * P],
                                   start=True, stop=True)
                mm.then_inc(*G.full(name))

            def step_hg_out(step):
                hh = step[1]
                name = ("o", hh)
                pe.wait_ge(*G.evacuated(("kv", hh), l))
                for lv in range(LEVELS - 2, LEVELS + 1):
                    pe.wait_ge(*G.evacuated(("A", hh, lv), l))
                pe.wait_ge(*G.free(name, l))
                for c in range(TT):
                    o = G.ps(name)[:, c * P:(c + 1) * P]
                    mm = pe.matmul(o, At[:, hh % 2, c, :], v[:, c, hh * P:(hh + 1) * P], start=True, stop=(c == 0))
                    if c:
                        mm = pe.matmul(o, qdec[:, c * P:(c + 1) * P], S[:, c - 1, :], start=False, stop=True)
                mm.then_inc(*G.full(name))

            def step_hg_turn(step):
                hh = step[1]
                pe.wait_ge(*G.evacuated(("o", hh), l))
                turn(("yT", hh), TT, lambda c: ghg[:, c, hh * P:(hh + 1) * P])

            def step_q_norm(step):
                pe.wait_ge(*q_ready.next(l))
                for n in range(NG):
                    turn(("qn", n), TT, lambda tt: q[:, tt, n].rearrange("p g d -> p (g d)"))

            def step_q_rope(step):
                pe.wait_ge(*qr_ready.next(l))
                for n in range(NG):
                    turn(("qr", n), TT, lambda tt: q[:, tt, n].rearrange("p g d -> p (g d)"))

            def step_k_norm(step):
                pe.wait_ge(*k_ready.next(l))
                for br in range(2):
                    turn(("kT", br), TT, lambda tt: kk[:, tt, br, :])

            def step_c_in(step):
                w = step[1]
                if w == 0:
                    for tt in range(TT):
                        pe.wait_ge(*G.evacuated(("kc", tt), l))
                    pe.wait_ge(*G.free(("pe",), l))
                    pe.transpose(G.ps(("pe",))[:, 0:P], pe_raw[:, :], ident[:, :]).then_inc(*G.full(("pe",)))
                for g in range(NKV):
                    turn(("ct", w, g), TT, lambda tt: kvc[:, tt, 2 * w + g].rearrange("p a d -> p (a d)"))

            def step_c_hid(step):
                w, i = step[1], step[2]
                name = ("ch", w)
                s = chunk(step)
                if i == 0:
                    pe.wait_ge(*clo_ready.next(l))
                    pe.wait_ge(*G.free(name, l))
                o = G.ps(name)[:, 0:2 * NCMP]
                for j in range(8):
                    a, b = (x[:, 8 * i + j].rearrange("p g c -> p (g c)") for x in (chi, clo))
                    wh, wl = whi[:, s, j * P:(j + 1) * P], wlo[:, s, j * P:(j + 1) * P]
                    mm = pe.matmul(o, wh, a, start=(i == 0 and j == 0), stop=False)
                    if j == 0:
                        mm.then_inc(chunk_begun, 1)
                    pe.matmul(o, wh, b, start=False, stop=False)
                    mm = pe.matmul(o, wl, a, start=False, stop=(i == 1 and j == 7))
                if i == 1:
                    mm.then_inc(*G.full(name))

            def step_c_out(step):
                for w in range(2):
                    pe.wait_ge(*G.evacuated(("ch", w), l))
                pe.wait_ge(*G.free(("co",), l))
                for w in range(2):
                    for g in range(NKV):
                        mm = pe.matmul(G.ps(("co",))[0:NCMP, (2 * w + g) * DH:(2 * w + g + 1) * DH],
                                       hid[:, w, g * NCMP:(g + 1) * NCMP], w2[:, w, :], start=True, stop=True)
                mm.then_inc(*G.full(("co",)))

            def step_c_key(step):
                pe.wait_ge(*kc_ready.next(l))
                pe.wait_ge(*G.free(("ck",), l))
                pe.transpose(G.ps(("ck",))[:, 0:P], kcn.rearrange("p g d -> p (g d)"), ident[:, :]).then_inc(*G.full(("ck",)))

            def step_c_att(step):
                qt = step[1]
                if qt == 0:
                    pe.wait_ge(*G.evacuated(("ck",), l))
                    for n in range(NG):
                        pe.wait_ge(*G.evacuated(("qn", n), l))
                for g in range(NKV):
                    name = ("cs", qt, g)
                    pe.wait_ge(*G.free(name, l))
                    for n in range(NG):
                        mm = pe.matmul(G.ps(name)[:, n * 32:n * 32 + NCMP], qTn[g * DH:(g + 1) * DH, n, qt * P:(qt + 1) * P],
                                       kcT[g * DH:(g + 1) * DH, 0:NCMP], start=True, stop=True)
                    mm.then_inc(*G.full(name))
                pe.wait_ge(*cp_ready.next(l))
                for i in range(2):
                    name = ("cp", qt, i)
                    pe.wait_ge(*G.free(name, l))
                    for n in range(4):
                        mm = pe.transpose(G.ps(name)[0:NCMP, n * P:(n + 1) * P], ce[:, 4 * i + n, :], ident[:, :])
                    mm.then_inc(*G.full(name))
                name = ("o_c", qt)
                pe.wait_ge(*G.free(name, l))
                for i in range(2):
                    pe.wait_ge(*G.evacuated(("cp", qt, i), l))
                for hh in range(NH):
                    mm = pe.matmul(G.ps(name)[:, hh * DH:(hh + 1) * DH], pcT[0:NCMP, hh, :], vc[0:NCMP, hh // NG, :],
                                   start=True, stop=True)
                mm.then_inc(*G.full(name))

            def scores(qt, br, hh):
                name, g, n = ("s", qt, br, hh), hh // NG, hh % NG
                pe.wait_ge(*G.free(name, l))
                o = G.ps(name)
                pe.matmul(o[:, 0:(qt + 1) * P], qTr[g * DH:(g + 1) * DH, n, qt * P:(qt + 1) * P],
                          kTn[g * DH:(g + 1) * DH, br, 0:(qt + 1) * P], start=True, stop=False)
                pe.matmul(o[:, qt * P:(qt + 1) * P], identb[:, :], causal[:, :], start=False, stop=True)\
                  .then_inc(*G.full(name))

            def probs_turn(qt, br, hh):
                name = ("p", qt, br, hh)
                pe.wait_ge(*G.evacuated(("s", qt, br, hh), l))
                pe.wait_ge(*G.free(name, l))
                for kt in range(qt + 1):
                    mm = pe.transpose(G.ps(name)[:, kt * P:(kt + 1) * P], Pb[:, hh % 2, kt * P:(kt + 1) * P], ident[:, :])
                mm.then_inc(*G.full(name))

            def values(qt, br, hh):
                name, g = ("o_a", qt, br), hh // NG
                pe.wait_ge(*G.evacuated(("p", qt, br, hh), l))
                if hh == 0:
                    pe.wait_ge(*G.free(name, l))
                for kt in range(qt + 1):
                    mm = pe.matmul(G.ps(name)[:, hh * DH:(hh + 1) * DH], Pt[:, hh % 2, kt * P:(kt + 1) * P],
                                   vv[:, kt, br, g * DH:(g + 1) * DH], start=(kt == 0), stop=(kt == qt))
                if hh == NH - 1:
                    mm.then_inc(*G.full(name))

            def step_att(step):
                qt = step[1]
                u = step[2] * NH + step[3]
                unit = lambda i: (qt, i // NH, i % NH)
                if u == 0:
                    if qt == 0:
                        for n in range(NG):
                            pe.wait_ge(*G.evacuated(("qr", n), l))
                        for br in range(2):
                            pe.wait_ge(*G.evacuated(("kT", br), l))
                    scores(*unit(0))
                    scores(*unit(1))
                    probs_turn(*unit(0))
                if u + 2 < 2 * NH:
                    scores(*unit(u + 2))
                if u + 1 < 2 * NH:
                    probs_turn(*unit(u + 1))
                values(*unit(u))

            def step_att_out(step):
                pe.wait_ge(*y_ready[0].next(l))
                turn(("nT", step[1]), 4, lambda f: y[:, f * P:(f + 1) * P])

            table = {"norm": step_norm, "fm": step_fm, "tm": step_tm, "p_turn": step_p_turn, "hg_prep": step_hg_prep,
                     "hg_level": step_hg_level, "hg_kv": step_hg_kv, "hg_out": step_hg_out, "hg_turn": step_hg_turn,
                     "q_norm": step_q_norm, "q_rope": step_q_rope, "k_norm": step_k_norm, "c_in": step_c_in,
                     "c_hid": step_c_hid, "c_out": step_c_out, "c_key": step_c_key, "c_att": step_c_att,
                     "att": step_att, "att_out": step_att_out}
            for step in steps1:
                table[step[0]](step)

        def scalar_one(act, l):
            G, ring = G1, ring1
            eu = [None, None]
            n_et = [0]
            n_sq = [0]
            sigs = dict(act_step=act_step[0], hi=hi_done[0], ex=exp_done[0], sq=sq_done[0], ss=ss_done[0], rs=rs_done[0])

            def link(ins):
                ins.then_inc(*sigs["act_step"].up())
                act.wait_ge(*sigs["act_step"].last(l))

            def split(j):
                if j < N1:
                    act.wait_ge(*ring.loaded(l, j))
                    act.wait_ge(*ring.parts_free(l, j))
                    nc.scalar.copy(whi[:, j % SLOTS, :], raw[:, j % SLOTS, :]).then_inc(hi_split, 1)

            def exp_neg(name, cols=T):
                i = n_et[0] % 2
                n_et[0] += 1
                if eu[i]:
                    act.wait_ge(*G.evacuated(eu[i], l))
                eu[i] = name
                act.wait_ge(*G.filled(name, l))
                nc.scalar.activation(et[:, i, 0:cols], G.ps(name)[:, 0:cols], ACT.Exp, scale=-1.0).then_inc(*sigs["ex"].up())

            def square_place():
                i = n_sq[0]
                n_sq[0] += 1
                if i >= 2:
                    act.wait_ge(*sigs["ss"].at(l, i - 1))
                return sq[:, i % 2, :]

            def root(dst, src, count, cols, sums_made):
                if sums_made:
                    act.wait_ge(*sigs["ss"].at(l, sums_made))
                if sigs["rs"].made:
                    act.wait_ge(*sigs["rs"].last(l))
                rows = src.shape[0]
                link(nc.scalar.activation(lnv[0:rows, 0:cols], src, ACT.Ln, scale=1.0 / count, bias=eps[0:rows, :]))
                nc.scalar.activation(dst, lnv[0:rows, 0:cols], ACT.Exp, scale=-0.5).then_inc(*sigs["rs"].up())

            def copy_group(dst, name, src=None):
                act.wait_ge(*G.filled(name, l))
                nc.scalar.copy(dst, G.ps(name)[:, :] if src is None else src).then_inc(*G.empty(name))

            def hi(dst, name, src=None):
                act.wait_ge(*G.filled(name, l))
                nc.scalar.copy(dst, G.ps(name)[:, :] if src is None else src).then_inc(*sigs["hi"].up())

            sums_made = [0]

            def step_norm(step):
                which = step[1]
                gain = {"mix": gmix, "ple": gple}[which]
                act.wait_ge(params[0], l * PARAMS_ONE + PARAMS_ONE)
                for tt in range(TT):
                    if which == "mix":
                        act.wait_ge(*G.e[tt].at(l, 0))
                    else:
                        act.wait_ge(*G.evacuated(("out1", tt), l))
                    ins = nc.scalar.activation(sq[:, :, :].rearrange("p a t -> p (a t)"), h[:, tt, :], ACT.Square, accum_out=ss[:, tt:tt + 1])
                    link(ins)
                root(rstd[:, :], ss[:, :], D, TT, 0)
                for k in range(KD):
                    act.wait_ge(*G.filled((which, k), l))
                    nc.scalar.activation(xhi[:, k, :], G.ps((which, k))[:, :], ACT.Identity, scale=gain[:, k:k + 1])\
                      .then_inc(*sigs["hi"].up())

            def step_fm(step):
                name = step[1:3]
                hh = step[2]
                if step[1] == "hq":
                    copy_group(qT[:, hh, :], name)
                    return
                act.wait_ge(*G.filled(name, l))
                link(nc.scalar.activation(tA[:, :], G.ps(name)[:, :], ACT.Abs))
                link(nc.scalar.activation(tA[:, :], tA[:, :], ACT.Exp, scale=-1.0))
                if hh:
                    act.wait_ge(*b_ready.at(l, hh))
                nc.scalar.activation(tB[:, :], tA[:, :], ACT.Ln, bias=1.0).then_inc(*fg_b.up())
                act.wait_ge(*G.evacuated(name, l))
                nc.scalar.activation(kT[:, hh, :], tC[:, :], ACT.Exp, bias=lbc[:, 0, hh:hh + 1])
                act.wait_ge(*fg_c.at(l, hh + 1))
                link(nc.scalar.activation(tB[:, :], tA[:, :], ACT.Exp))
                nc.scalar.activation(tB[:, :], tB[:, :], ACT.Ln, bias=1.0).then_inc(*fg_d.up())

            def step_tm(step):
                _, kind, i, n, _ = step
                if i < n - 1:
                    return
                for tt in range(TT):
                    name = (kind, tt)
                    if kind == "v":
                        copy_group(v[:, tt, :], name)
                    elif kind == "go":
                        act.wait_ge(*G.filled(name, l))
                        nc.scalar.activation(ghg[:, tt, :], G.ps(name)[:, :], ACT.Exp, scale=-1.0).then_inc(*G.empty(name))
                    elif kind in ("z", "nz", "pg0", "pg1"):
                        exp_neg(name)
                    elif kind == "nq":
                        place = square_place()
                        act.wait_ge(*G.filled(name, l))
                        src = G.ps(name)[:, :].rearrange("p (g n d) -> p g n d", g=NKV, n=NG)
                        for g in range(NKV):
                            nc.scalar.copy(q[:, tt, :, g, :], src[:, g])
                        nc.scalar.activation(place, G.ps(name)[:, :], ACT.Square).then_inc(*G.empty(name))
                        sums_made[0] += 1
                    elif kind == "kc":
                        act.wait_ge(*G.filled(name, l))
                        src = G.ps(name)[:, 0:256].rearrange("p (w d) -> p w d", d=DH)
                        nc.scalar.copy(kvc[:, tt, :, 0, :], src)
                        nc.scalar.copy(kvc[:, tt, :, 1, :], src).then_inc(*G.empty(name))
                    elif kind in ("ks", "kw"):
                        br = 0 if kind == "ks" else 1
                        act.wait_ge(*G.filled(name, l))
                        nc.scalar.copy(kk[:, tt, br, :], G.ps(name)[:, 0:P])
                        ins = nc.scalar.copy(vv[:, tt, br, :], G.ps(name)[:, P:2 * P])
                        if br:
                            ins = nc.scalar.activation(gts[:, tt].rearrange("p b h -> p (b h)"), G.ps(name)[:, 2 * P:2 * P + 24],
                                                       ACT.Exp, scale=-1.0)
                        ins.then_inc(*G.empty(name))

            def level_decay(hh, lv):
                act.wait_ge(*d_ready.next(l))
                nc.scalar.activation(dE[:, lv % 2, :], dE[:, lv % 2, :], ACT.Exp).then_inc(*e_ready.up())

            def step_hg_prep(step):
                hh = step[1]
                act.wait_ge(*b_ready.at(l, hh + 1))
                nc.scalar.activation(eB[:, :], bT[:, hh, :], ACT.Exp)
                for c in range(TT):
                    at = slice(c * P, (c + 1) * P)
                    nc.scalar.activation(kdx[:, at], bT[:, hh, at], ACT.Exp, scale=-1.0, bias=bT[:, hh, (c + 1) * P - 1:(c + 1) * P])
                nc.scalar.activation(ebl[:, :], bT[:, hh, P - 1::P], ACT.Exp).then_inc(*prep_exp.up())
                level_decay(hh, 0)
                copy_group(kdt[:, :, :].rearrange("p c d -> p (c d)"), ("kd", hh))

            def step_hg_level(step):
                hh, lv = step[1:]
                if lv + 1 < LEVELS:
                    level_decay(hh, lv + 1)

            def step_hg_out(step):
                name = ("o", step[1])
                place = square_place()
                act.wait_ge(*G.filled(name, l))
                nc.scalar.activation(place, G.ps(name)[:, :], ACT.Square).then_inc(*sigs["sq"].up())
                sums_made[0] += 1
                root(rsh[:, :], ssh[:, :], P, TT, sums_made[0])

            def step_hg_turn(step):
                hi(xhi[:, step[1], :], ("yT", step[1]))

            def step_p_turn(step):
                for k in range(2):
                    hi(pT[:, 0, k, :], ("pT", k))

            def step_q_norm(step):
                root(rsq[:, :, :].rearrange("p t h -> p (t h)"), ssq[:, :, :].rearrange("p t h -> p (t h)"), DH, 32, sums_made[0])
                for n in range(NG):
                    copy_group(qTn[:, n, :], ("qn", n))

            def step_q_rope(step):
                for n in range(NG):
                    copy_group(qTr[:, n, :], ("qr", n))

            def step_k_norm(step):
                sums_made[0] += 1
                n_sq[0] += 1
                root(rsk[:, :], ssk[:, :], DH, 16, sums_made[0])
                for br in range(2):
                    copy_group(kTn[:, br, :], ("kT", br))
                act.dma_start(p_raw, d["p"][bass.ds(l, 1)].rearrange("o b (t p) c -> p (o b t) c", p=P)).then_inc(p_loaded, 16)

            def step_c_in(step):
                w = step[1]
                if w == 0:
                    copy_group(peT[:, :, :].rearrange("p w j -> p (w j)"), ("pe",), G.ps(("pe",))[:, 0:32])
                act.wait_ge(*G.evacuated(("ct", w, 1), l))
                nc.scalar.copy(chi[:, :, :, :], cin).then_inc(*sigs["hi"].up())

            def step_c_hid(step):
                if step[2] == 1:
                    exp_neg(("ch", step[1]), 2 * NCMP)

            def step_c_out(step):
                place = square_place()
                act.wait_ge(*G.filled(("co",), l))
                ps = G.ps(("co",))
                nc.scalar.copy(vc[0:NCMP].rearrange("p g d -> p (g d)"), ps[0:NCMP, P:2 * P])
                nc.scalar.activation(place[0:NCMP, 0:P], ps[0:NCMP, 0:P], ACT.Square).then_inc(*sigs["sq"].up())
                sums_made[0] += 1
                root(rsc[0:NCMP, :], ssc[0:NCMP, :], DH, 2, sums_made[0])

            def step_c_key(step):
                copy_group(kcT[:, 0:NCMP], ("ck",), G.ps(("ck",))[:, 0:NCMP])

            def step_c_att(step):
                qt = step[1]
                act.wait_ge(*cs_ready.next(l))
                nc.scalar.activation(ce, cs, ACT.Exp).then_inc(*ce_done.up())
                for i in range(2):
                    copy_group(pcT[0:NCMP, 4 * i:4 * i + 4, :].rearrange("p b q -> p (b q)"), ("cp", qt, i), G.ps(("cp", qt, i))[0:NCMP, :])

            def probs(qt, br, hh):
                name, n = ("s", qt, br, hh), (qt + 1) * P
                act.wait_ge(*nm_ready[0].next(l))
                nc.scalar.activation(Pb[:, hh % 2, 0:n], G.ps(name)[:, 0:n], ACT.Exp, bias=nm[:, (br * NH + hh) % 4:(br * NH + hh) % 4 + 1],
                                     accum_out=sums[:, 1 + br, hh:hh + 1]).then_inc(*G.empty(name))

            def step_att(step):
                qt = step[1]
                u = step[2] * NH + step[3]
                for i in ([0, 1, 2] if u == 0 else [u + 2]):
                    if i < 2 * NH:
                        probs(qt, i // NH, i % NH)

            def step_att_out(step):
                qt = step[1]
                name = ("nT", qt)
                hi(xhi[:, HG:KD, qt * P:(qt + 1) * P], name, G.ps(name)[:, :].rearrange("p (f q) -> p f q", f=4))

            table = {"norm": step_norm, "fm": step_fm, "tm": step_tm, "p_turn": step_p_turn, "hg_prep": step_hg_prep,
                     "hg_level": step_hg_level, "hg_out": step_hg_out, "hg_turn": step_hg_turn,
                     "q_norm": step_q_norm, "q_rope": step_q_rope, "k_norm": step_k_norm, "c_in": step_c_in,
                     "c_hid": step_c_hid, "c_out": step_c_out, "c_key": step_c_key, "c_att": step_c_att,
                     "att": step_att, "att_out": step_att_out}
            for j in range(SLOTS - 1):
                split(j)
            for step in steps1:
                if step in number1:
                    split(number1[step] + SLOTS - 1)
                if step[0] in table:
                    table[step[0]](step)

        def vector_one(dve, l):
            G = G1
            tt_, ts, stt = nc.vector.tensor_tensor, nc.vector.tensor_scalar, nc.vector.scalar_tensor_tensor
            step_sig, hi_s, ex, sq_s, ss_s, rs = dve_step[0], hi_done[0], exp_done[0], sq_done[0], ss_done[0], rs_done[0]
            n_et, n_sq = [0], [0]

            def link(ins):
                ins.then_inc(*step_sig.up())
                dve.wait_ge(*step_sig.last(l))

            def et_place():
                i = n_et[0] % 2
                n_et[0] += 1
                dve.wait_ge(*ex.next(l))
                return et[:, i, :]

            def lo(dst, name, part, src=None, gain=None):
                dve.wait_ge(*hi_s.next(l))
                ps = G.ps(name)[:, :] if src is None else src
                if gain is None:
                    tt_(dst, ps, part.bitcast(F32), ALU.subtract).then_inc(*G.empty(name))
                else:
                    stt(dst, ps, gain, part.bitcast(F32), ALU.mult, ALU.subtract).then_inc(*G.empty(name))

            def step_norm(step):
                which = step[1]
                gain = {"mix": gmix, "ple": gple}[which]
                dve.wait_ge(params[0], l * PARAMS_ONE + PARAMS_ONE)
                dve.wait_ge(*rs.next(l))
                for tt in range(TT):
                    ins = ts(diag[:, tt, :], ident[:, :], rstd[:, tt:tt + 1], None, ALU.mult)
                ins.then_inc(*diag_ready[0].up())
                if which == "mix":
                    nc.vector.tensor_copy(lbc[:, :, :], lbt[:, bass.ds(l, 1), :, :].rearrange("p a c h -> p (a c) h"))
                for k in range(KD):
                    lo(xlo[:, k, :], (which, k), xhi[:, k, :], gain=gain[:, k:k + 1])

            def step_fm(step):
                if step[1] == "hq":
                    return
                name, hh = step[1:3], step[2]
                x = G.ps(name)[:, :]
                c1, a, c1a = (lbc[:, i, hh:hh + 1] for i in range(3))
                dve.wait_ge(*G.filled(name, l))
                dve.wait_ge(*fg_b.at(l, hh + 1))
                link(stt(tA[:, :], x, 0.0, tB[:, :], ALU.min, ALU.subtract))
                tt_(tC[:, :], tA[:, :], x, ALU.subtract).then_inc(*G.empty(name))
                ts(tD[:, :], tA[:, :], c1, a, ALU.add, ALU.max)
                link(ts(tA[:, :], tA[:, :], c1a, None, ALU.add))
                stt(tA[:, :], tA[:, :], -1.0, tA[:, :], ALU.mult, ALU.min).then_inc(*fg_c.up())
                dve.wait_ge(*fg_d.at(l, hh + 1))
                link(tt_(tD[:, :], tD[:, :], tB[:, :], ALU.add))
                for c in range(TT):
                    at = slice(c * P, (c + 1) * P)
                    ins = nc.vector.tensor_tensor_scan(bT[:, hh, at], ones[:, :].to_broadcast([P, P]), tD[:, at], 0.0, ALU.mult, ALU.add)
                ins.then_inc(*b_ready.up())

            def step_tm(step):
                _, kind, i, n, _ = step
                if i < n - 1:
                    return
                for tt in range(TT):
                    name = (kind, tt)
                    ps = G.ps(name)[:, :] if name in G.place else None
                    if kind == "z":
                        e, g = et_place(), ghg[:, tt, :]
                        link(ts(e, e, 1.0, None, ALU.add))
                        dve.wait_ge(*G.evacuated(("go", tt), l))
                        link(stt(g, g, 1.0, e, ALU.add, ALU.mult))
                        link(nc.vector.reciprocal(g, g))
                        tt_(g, g, ps, ALU.mult).then_inc(*G.empty(name))
                        dve.wait_ge(*G.evacuated(name, l))
                        g3 = ghg[:, tt, :].rearrange("p (h d) -> p h d", h=HG)
                        link(tt_(g3, g3, onorm[:, :].unsqueeze(1).to_broadcast([P, HG, P]), ALU.mult))
                    elif kind == "nz":
                        e, g = et_place(), nzs[:, tt, :]
                        link(ts(g, e, 1.0, None, ALU.add))
                        link(nc.vector.reciprocal(g, g))
                        tt_(g, g, ps, ALU.mult).then_inc(*G.empty(name))
                    elif kind == "nq":
                        place = sq[:, n_sq[0] % 2, :]
                        n_sq[0] += 1
                        dve.wait_ge(*G.evacuated(name, l))
                        nc.vector.tensor_reduce(ssq[:, tt, :].rearrange("p (n g) -> p g n", g=NKV),
                                                place.rearrange("p (g n d) -> p g n d", g=NKV, n=NG), AX, ALU.add).then_inc(*ss_s.up())
                    elif kind[:3] == "out":
                        at = h[:, tt, int(kind[3]) * T:(int(kind[3]) + 1) * T]
                        dve.wait_ge(*G.filled(name, l))
                        tt_(at, at, ps, ALU.add).then_inc(*G.empty(name))
                    elif kind[:2] == "pg":
                        other = ("pp" + kind[2], tt)
                        at = h[:, tt, int(kind[2]) * T:(int(kind[2]) + 1) * T]
                        e = et_place()
                        link(ts(e, e, 1.0, None, ALU.add))
                        link(nc.vector.reciprocal(e, e))
                        dve.wait_ge(*G.filled(other, l))
                        tt_(e, e, G.ps(other)[:, :], ALU.mult).then_inc(*G.empty(other))
                        dve.wait_ge(*G.evacuated(other, l))
                        tt_(at, at, e, ALU.add).then_inc(*G.empty(name))

            def halves(t, lv):
                m = 64 >> lv
                x = t.rearrange("p (n a m) -> p n a m", a=2, m=m)
                return x[:, :, 0, :], x[:, :, 1, :], x[:, :, 0, m - 1:m].to_broadcast([P, T // (2 * m), m])

            def level_logs(hh, lv):
                before = LEVELS * hh + lv - (2 if lv >= 2 else 1 if lv == 0 else 3)
                if before >= 0:
                    dve.wait_ge(*qk_ready.at(l, before + 1))
                left, right, mid = halves(bT[:, hh, :], lv)
                dl, dr, _ = halves(dE[:, lv % 2, :], lv)
                tt_(dr, right, mid, ALU.subtract)
                tt_(dl, mid, left, ALU.subtract).then_inc(*d_ready.up())

            def keep(hh, lv):
                name = ("A", hh, lv)
                nc.vector.copy_predicated(At[:, hh % 2, :, :], masks[:, lv, :].unsqueeze(1).to_broadcast([P, TT, P]),
                                          G.ps(name)[:, :].rearrange("p (c t) -> p c t", c=TT)).then_inc(*G.empty(name))

            def step_hg_prep(step):
                hh = step[1]
                level_logs(hh, 0)
                dve.wait_ge(*prep_exp.at(l, hh + 1))
                tt_(qdec[:, :], qT[:, hh, :], eB[:, :], ALU.mult)
                tt_(kdec[:, :], kT[:, hh, :], kdx[:, :], ALU.mult).then_inc(*prep_done.up())

            def step_hg_level(step):
                hh, lv = step[1:]
                if lv + 1 < LEVELS:
                    level_logs(hh, lv + 1)
                if lv < LEVELS:
                    if lv >= 2:
                        dve.wait_ge(*G.filled(("A", hh, lv - 2), l))
                    if lv >= 3:
                        dve.wait_ge(*G.evacuated(("A", hh, lv - 3), l))
                    dve.wait_ge(*e_ready.next(l))
                    el, er, _ = halves(dE[:, lv % 2, :], lv)
                    tt_(halves(Ql[:, lv % 2, :], lv)[1], halves(qT[:, hh, :], lv)[1], er, ALU.mult)
                    tt_(halves(Kl[:, lv % 2, :], lv)[0], halves(kT[:, hh, :], lv)[0], el, ALU.mult).then_inc(*qk_ready.up())
                    if lv >= 2:
                        keep(hh, lv - 2)

            def step_hg_kv(step):
                hh = step[1]
                name = ("kv", hh)
                ps = G.ps(name)
                dve.wait_ge(*G.filled(name, l))
                dve.wait_ge(*G.evacuated(("A", hh, LEVELS - 3), l))
                nc.vector.tensor_copy(S[:, 0, :], ps[:, 0:P]).then_inc(*step_sig.up())
                keep(hh, LEVELS - 2)
                dve.wait_ge(*step_sig.last(l))
                dve.wait_ge(*G.evacuated(("A", hh, LEVELS - 2), l))
                stt(S[:, 1, :], S[:, 0, :], ebl[:, 1:2], ps[:, P:2 * P], ALU.mult, ALU.add).then_inc(*step_sig.up())
                keep(hh, LEVELS - 1)
                dve.wait_ge(*step_sig.last(l))
                dve.wait_ge(*G.evacuated(("A", hh, LEVELS - 1), l))
                stt(S[:, 2, :], S[:, 1, :], ebl[:, 2:3], ps[:, 2 * P:3 * P], ALU.mult, ALU.add).then_inc(*G.empty(name))
                keep(hh, LEVELS)

            def step_hg_out(step):
                hh = step[1]
                name = ("o", hh)
                place = sq[:, n_sq[0] % 2, :]
                n_sq[0] += 1
                dve.wait_ge(*sq_s.next(l))
                nc.vector.tensor_reduce(ssh[:, :], place.rearrange("p (c d) -> p c d", c=TT), AX, ALU.add).then_inc(*ss_s.up())
                dve.wait_ge(*rs.next(l))
                t3 = tA[:, :].rearrange("p (c d) -> p c d", c=TT)
                link(tt_(t3, G.ps(name)[:, :].rearrange("p (c d) -> p c d", c=TT), rsh[:, :].unsqueeze(2).to_broadcast([P, TT, P]), ALU.mult))
                g = ghg[:, :, hh * P:(hh + 1) * P]
                tt_(g, g, t3, ALU.mult).then_inc(*G.empty(name))

            def step_hg_turn(step):
                lo(xlo[:, step[1], :], ("yT", step[1]), xhi[:, step[1], :])

            def step_p_turn(step):
                for k in range(2):
                    lo(pT[:, 1, k, :], ("pT", k), pT[:, 0, k, :])

            def step_q_norm(step):
                q3 = q[:, :, :, :, :].rearrange("p t n g d -> p (t n g) d")
                r = rsq[:, :, :].rearrange("p t h -> p (t h)").unsqueeze(2).to_broadcast([P, TT * NH, DH])
                dve.wait_ge(*rs.next(l))
                link(stt(q3, q3, DH ** -0.5, r, ALU.mult, ALU.mult))
                tt_(q3, q3, qg[:, :].unsqueeze(1).to_broadcast([P, TT * NH, DH]), ALU.mult).then_inc(*q_ready.up())

            def rotate(x, n, done):
                part = [t[:, 0:TT * n * 8].rearrange("p (t n d) -> p t n d", t=TT, n=n) for t in (tA, tB, tC, tD)]
                cos, sin = (k1[c][:, :].rearrange("p (t d) -> p t d", t=TT).unsqueeze(2).to_broadcast([P, TT, n, 8]) for c in ("cos", "sin"))
                a, b = x[:, :, :, 0:8], x[:, :, :, 8:16]
                tt_(part[0], a, cos, ALU.mult)
                tt_(part[1], b, sin, ALU.mult)
                tt_(part[2], a, sin, ALU.mult)
                link(tt_(part[3], b, cos, ALU.mult))
                tt_(a, part[0], part[1], ALU.subtract)
                tt_(b, part[2], part[3], ALU.add).then_inc(*done.up())

            def step_q_rope(step):
                dve.wait_ge(*G.evacuated(("qn", NG - 1), l))
                rotate(q[:, :, :, :, :].rearrange("p t n g d -> p t (n g) d"), NH, qr_ready)

            def step_k_norm(step):
                g2 = gts[:, :, :, :].rearrange("p t b h -> p (t b h)")
                dve.wait_ge(*G.evacuated(("kw", TT - 1), l))
                link(ts(g2, g2, 1.0, None, ALU.add))
                link(nc.vector.reciprocal(g2, g2))
                k3 = kk[:, :, :, :].rearrange("p t b (g d) -> p (t b g) d", g=NKV)
                s3 = Kl[:, :, :].rearrange("p a (n d) -> p (a n) d", d=DH)
                link(tt_(s3, k3, k3, ALU.mult))
                nc.vector.tensor_reduce(ssk[:, :], s3, AX, ALU.add).then_inc(*ss_s.up())
                n_sq[0] += 1
                dve.wait_ge(*rs.next(l))
                link(tt_(k3, k3, rsk[:, :].unsqueeze(2).to_broadcast([P, 16, DH]), ALU.mult))
                for br in range(2):
                    kb = kk[:, :, br, :].rearrange("p t (g d) -> p t g d", g=NKV)
                    link(tt_(kb, kb, kg[:, 1 + br, :].unsqueeze(1).unsqueeze(1).to_broadcast([P, TT, NKV, DH]), ALU.mult))
                rotate(kk[:, :, :, :].rearrange("p t b (g d) -> p t (b g) d", g=NKV), 2 * NKV, k_ready)

            def step_c_in(step):
                w = step[1]
                dve.wait_ge(*G.evacuated(("pe",), l))
                for g in range(NKV):
                    name = ("ct", w, g)
                    dve.wait_ge(*G.filled(name, l))
                    for a in range(2):
                        rows = slice(a * DH, (a + 1) * DH)
                        tok = G.ps(name)[rows, :].rearrange("p (c j a) -> p a j c", j=8, a=2)[:, a]
                        for b in range(2):
                            pe8 = peT[rows, w, 8 * b:8 * b + 8].unsqueeze(2).to_broadcast([DH, 8, NCMP])
                            ins = tt_(cin[rows, 8 * b:8 * b + 8, g, :], tok[:, :, b:b + NCMP], pe8, ALU.add)
                    ins.then_inc(*G.empty(name))
                dve.wait_ge(*hi_s.next(l))
                tt_(clo[:, :, :, :].rearrange("p j g c -> p (j g c)"), cin.rearrange("p j g c -> p (j g c)"),
                    chi[:, :, :, :].rearrange("p j g c -> p (j g c)").bitcast(F32), ALU.subtract).then_inc(*clo_ready.up())

            def step_c_hid(step):
                if step[2] == 1:
                    name = ("ch", step[1])
                    e = et_place()[:, 0:2 * NCMP]
                    link(ts(e, e, 1.0, None, ALU.add))
                    link(nc.vector.reciprocal(e, e))
                    tt_(hid[:, step[1], :], e, G.ps(name)[:, 0:2 * NCMP], ALU.mult).then_inc(*G.empty(name))

            def step_c_out(step):
                place = sq[0:NCMP, n_sq[0] % 2, 0:P]
                n_sq[0] += 1
                dve.wait_ge(*sq_s.next(l))
                nc.vector.tensor_reduce(ssc[0:NCMP, :], place.rearrange("p (g d) -> p g d", g=NKV), AX, ALU.add).then_inc(*ss_s.up())
                dve.wait_ge(*rs.next(l))
                tt_(kcn[0:NCMP], G.ps(("co",))[0:NCMP, 0:P].rearrange("p (g d) -> p g d", g=NKV),
                    rsc[0:NCMP, :].unsqueeze(2).to_broadcast([NCMP, NKV, DH]), ALU.mult).then_inc(*G.empty(("co",)))
                dve.wait_ge(*G.evacuated(("co",), l))
                tt_(kcn[0:NCMP], kcn[0:NCMP], kg[0:NCMP, 0, :].unsqueeze(1).to_broadcast([NCMP, NKV, DH]), ALU.mult).then_inc(*kc_ready.up())

            def step_c_att(step):
                qt = step[1]
                bias, seen = (k1[c][:, qt * NCMP:(qt + 1) * NCMP].unsqueeze(1) for c in ("cbias", "cseen"))
                for g in range(NKV):
                    name = ("cs", qt, g)
                    dve.wait_ge(*G.filled(name, l))
                    tt_(cs[:, g * NG:(g + 1) * NG, :], G.ps(name)[:, 0:P].rearrange("p (n c) -> p n c", n=NG)[:, :, 0:NCMP],
                        bias.to_broadcast([P, NG, NCMP]), ALU.add).then_inc(*G.empty(name))
                dve.wait_ge(*G.evacuated(("cs", qt, 1), l))
                link(nc.vector.tensor_reduce(mx[:, :], cs, AX, ALU.max))
                tt_(cs, cs, mx[:, :].unsqueeze(2).to_broadcast([P, NH, NCMP]), ALU.subtract).then_inc(*cs_ready.up())
                dve.wait_ge(*ce_done.next(l))
                tt_(ce, ce, seen.to_broadcast([P, NH, NCMP]), ALU.mult).then_inc(*cp_ready.up())
                dve.wait_ge(*cp_ready.last(l))
                link(nc.vector.tensor_reduce(sums[:, 0, :], ce, AX, ALU.add))
                link(ts(sums[:, 0, :], sums[:, 0, :], 1e-30, None, ALU.max))

            def greatest(qt, br, hh):
                name, u = ("s", qt, br, hh), br * NH + hh
                dve.wait_ge(*G.filled(name, l))
                nc.vector.tensor_reduce(nm[:, u % 4:u % 4 + 1], G.ps(name)[:, 0:(qt + 1) * P], AX, ALU.max, negate=True).then_inc(*nm_ready[0].up())

            def probs_turned(qt, br, hh):
                name, n = ("p", qt, br, hh), (qt + 1) * P
                dve.wait_ge(*G.filled(name, l))
                nc.vector.tensor_copy(Pt[:, hh % 2, 0:n], G.ps(name)[:, 0:n]).then_inc(*G.empty(name))

            def step_att(step):
                qt = step[1]
                u = step[2] * NH + step[3]
                unit = lambda i: (qt, i // NH, i % NH)
                if u == 0:
                    greatest(*unit(0))
                    greatest(*unit(1))
                    probs_turned(*unit(0))
                if u + 2 < 2 * NH:
                    greatest(*unit(u + 2))
                if u + 1 < 2 * NH:
                    probs_turned(*unit(u + 1))

            def step_att_out(step):
                qt = step[1]
                wide = lambda i: coef[:, i, :].unsqueeze(2).to_broadcast([P, NH, DH])
                by_head = lambda t: t.rearrange("p (h d) -> p h d", h=NH)
                dve.wait_ge(*G.evacuated(("s", qt, 1, NH - 1), l))
                link(nc.vector.reciprocal(coef[:, :, :], sums[:, :, :]))
                link(tt_(coef[:, :, :], coef[:, :, :], gts[:, qt, :, :], ALU.mult))
                for dst, name, i in ((y, ("o_a", qt, 0), 1), (tA, ("o_a", qt, 1), 2), (tB, ("o_c", qt), 0)):
                    dve.wait_ge(*G.filled(name, l))
                    tt_(by_head(dst[:, :]), by_head(G.ps(name)[:, :]), wide(i), ALU.mult).then_inc(*G.empty(name))
                dve.wait_ge(*G.evacuated(("o_c", qt), l))
                link(tt_(y[:, :], y[:, :], tA[:, :], ALU.add))
                link(tt_(y[:, :], y[:, :], tB[:, :], ALU.add))
                tt_(y[:, :], y[:, :], nzs[:, qt, :], ALU.mult).then_inc(*y_ready[0].up())
                at = slice(qt * P, (qt + 1) * P)
                lo(xlo[:, HG:KD, at], ("nT", qt), xhi[:, HG:KD, at], src=G.ps(("nT", qt))[:, :].rearrange("p (f q) -> p f q", f=4))

            table = {"norm": step_norm, "fm": step_fm, "tm": step_tm, "p_turn": step_p_turn, "hg_prep": step_hg_prep,
                     "hg_level": step_hg_level, "hg_kv": step_hg_kv, "hg_out": step_hg_out, "hg_turn": step_hg_turn,
                     "q_norm": step_q_norm, "q_rope": step_q_rope, "k_norm": step_k_norm, "c_in": step_c_in,
                     "c_hid": step_c_hid, "c_out": step_c_out, "c_att": step_c_att,
                     "att": step_att, "att_out": step_att_out}
            for step in steps1:
                if step[0] in table:
                    table[step[0]](step)

        def tensor_two(pe, l):
            G, ring = G2, ring2

            def chunk(step):
                pe.wait_ge(*ring.split(l, number2[step]))
                return number2[step] % SLOTS

            def turn(name, tiles, src):
                pe.wait_ge(*G.free(name, l))
                for i in range(tiles):
                    mm = pe.transpose(G.ps(name)[:, i * P:(i + 1) * P], src(i), ident[:, :])
                mm.then_inc(*G.full(name))

            def normed(name, tiles, src, dg):
                pe.wait_ge(*G.free(name, l))
                for tt in range(tiles):
                    mm = pe.matmul(G.ps(name)[:, tt * P:(tt + 1) * P], src(tt), dg[:, tt, :], start=True, stop=True)
                mm.then_inc(*G.full(name))

            def step_norm(step):
                pe.wait_ge(*diag_ready[1].next(l))
                for k in range(KD):
                    normed((step[1], k), TT, lambda tt: h[:, tt, k * P:(k + 1) * P], diag)

            def step_mem(step):
                pe.wait_ge(*diag_ready[1].next(l))
                for k in range(KD):
                    normed(("mm", k), MT, lambda tt: mem[:, tt, k * P:(k + 1) * P], diag)

            first_of = {("ax", 0): "mix", ("xq", 0): "xa", ("u", 0): "ffn"}

            def step_fm(step):
                name = step[1:3]
                s = chunk(step)
                pe.wait_ge(*G.free(name, l))
                rhs = (mmT[:, 0], mmT[:, 1]) if step[1] == "xk" else (xhi, xlo)
                cols = rhs[0].shape[2]
                o = G.ps(name)[:, 0:cols]
                for k in range(KD):
                    if name in first_of:
                        pe.wait_ge(*G.evacuated((first_of[name], k), l))
                    if name == ("xk", 0):
                        pe.wait_ge(*G.evacuated(("mm", k), l))
                    wh, wl = whi[:, s, k * P:(k + 1) * P], wlo[:, s, k * P:(k + 1) * P]
                    mm = pe.matmul(o, wh, rhs[0][:, k, :], start=(k == 0), stop=False)
                    if k == 0:
                        mm.then_inc(chunk_begun, 1)
                    pe.matmul(o, wh, rhs[1][:, k, :], start=False, stop=False)
                    mm = pe.matmul(o, wl, rhs[0][:, k, :], start=False, stop=(k == KD - 1))
                mm.then_inc(*G.full(name))

            def step_tm(step):
                _, kind, i, n, (_, k0, nk, _, cols) = step
                rows, base, tiles = (xhi, xlo), 0, TT
                if kind[0] == "y":
                    rows = {"a": yaT, "b": ybT, "c": ycT}[kind[1]]
                    if i == 0 and kind == "ya0":
                        pe.wait_ge(*ya_ready.at(l, 2))
                    if i == 0 and kind == "yb0":
                        for hh in range(RH):
                            pe.wait_ge(*G.evacuated(("ybT", hh), l))
                    if i == 0 and kind == "yc0":
                        for k in range(2):
                            pe.wait_ge(*G.evacuated(("ycT", k), l))
                    rows = (rows[:, 0], rows[:, 1])
                elif kind[:2] == "xv":
                    rows, tiles = (mmT[:, 0], mmT[:, 1]), MT
                elif kind[0] == "d":
                    rows, base = (gT[:, 0], gT[:, 1]), HALVES[int(kind[1])][0]
                    if i == 0 and kind[2] == "0":
                        pe.wait_ge(*g_ready.at(l, HALVES[int(kind[1])][1]))
                elif i == 0 and kind == "wo0":
                    for k in range(KD):
                        pe.wait_ge(*G.evacuated(("mT", k), l))
                elif i == 0 and kind == "xw0":
                    pe.wait_ge(*G.evacuated(("xo", XH - 1, 1), l))
                s = chunk(step)
                for tt in range(tiles):
                    name = (kind, tt)
                    if i == 0:
                        pe.wait_ge(*G.free(name, l))
                    at = slice(tt * P, (tt + 1) * P)
                    for kk_ in range(nk):
                        a, b = rows[0][:, k0 + kk_ - base, at], rows[1][:, k0 + kk_ - base, at]
                        wh, wl = whi[:, s, kk_ * cols:(kk_ + 1) * cols], wlo[:, s, kk_ * cols:(kk_ + 1) * cols]
                        mm = pe.matmul(G.ps(name)[:, :], a, wh, start=(i == 0 and kk_ == 0), stop=False)
                        if tt == 0 and kk_ == 0:
                            mm.then_inc(chunk_begun, 1)
                        pe.matmul(G.ps(name)[:, :], a, wl, start=False, stop=False)
                        mm = pe.matmul(G.ps(name)[:, :], b, wh, start=False, stop=(i == n - 1 and kk_ == nk - 1))
                    if i == n - 1:
                        mm.then_inc(*G.full(name))

            def step_ret_pair(step):
                p = step[1]
                if p == 0:
                    pe.wait_ge(*rot_ready.next(l))
                for w, name in enumerate((("qP", p), ("kP", p))):
                    turn(name, TT, lambda tt: qkr[:, tt, 4 * w + 2 * p:4 * w + 2 * p + 2, :].rearrange("p h d -> p (h d)"))

            def step_ret_in(step):
                hh = step[1]
                part = slice(hh % 2 * RK, (hh % 2 + 1) * RK)
                pe.wait_ge(*qx_ready.at(l, hh // 2 + 1))
                pe.wait_ge(*G.evacuated(("kP", hh // 2), l))
                name = ("rs", hh)
                pe.wait_ge(*G.free(name, l))
                for c in range(TT):
                    at = slice(c * P, (c + 1) * P)
                    mm = pe.matmul(G.ps(name)[:, at], kp[part, at], qp[part, at], start=True, stop=True)
                mm.then_inc(*G.full(name))
                name = ("rk", hh)
                if hh == 0:
                    for tt in range(TT):
                        pe.wait_ge(*G.evacuated(("v", tt), l))
                pe.wait_ge(*G.free(name, l))
                for c in range(TT - 1):
                    mm = pe.matmul(G.ps(name)[part, c * P:(c + 1) * P], qkr[:, c, 4 + hh, :], v2[:, c, hh * P:(hh + 1) * P],
                                   start=True, stop=True)
                mm.then_inc(*G.full(name))

            def step_ret_out(step):
                hh = step[1]
                part = slice(hh % 2 * RK, (hh % 2 + 1) * RK)
                pe.wait_ge(*G.evacuated(("rs", hh), l))
                pe.wait_ge(*G.evacuated(("rk", hh), l))
                name = ("ro", hh)
                pe.wait_ge(*G.free(name, l))
                for c in range(TT):
                    at = slice(c * P, (c + 1) * P)
                    mm = pe.matmul(G.ps(name)[:, at], ds[:, at], v2[:, c, hh * P:(hh + 1) * P], start=True, stop=(c == 0))
                    if c:
                        mm = pe.matmul(G.ps(name)[:, at], qx[part, at], R[part, c - 1, :], start=False, stop=True)
                mm.then_inc(*G.full(name))

            def step_ret_turn(step):
                hh = step[1]
                pe.wait_ge(*yb_ready.at(l, hh + 1))
                turn(("ybT", hh), TT, lambda c: gg[:, c, hh * P:(hh + 1) * P])

            def step_sg_w(step):
                pe.wait_ge(*sgw_ready.next(l))
                turn(("ws",), SGG, lambda g: sgw[:, g, :])

            def step_sg_mix(step):
                pe.wait_ge(*sg_ready.next(l))
                pe.wait_ge(*G.evacuated(("ws",), l))
                for tt in range(TT):
                    name = ("vm", tt)
                    pe.wait_ge(*G.free(name, l))
                    for g in range(SGG):
                        mm = pe.matmul(G.ps(name)[:, g * 64:(g + 1) * 64], wsT[:, g, :], gg[:, tt, 256 + g * 64:256 + (g + 1) * 64],
                                       start=True, stop=True)
                    mm.then_inc(*G.full(name))

            def step_sg_turn(step):
                for tt in range(TT):
                    pe.wait_ge(*G.evacuated(("vm", tt), l))
                for k in range(2):
                    turn(("ycT", k), TT, lambda tt: gg[:, tt, k * P:(k + 1) * P])

            def step_mg_turn(step):
                pe.wait_ge(*mg_ready.next(l))
                for k in range(KD):
                    turn(("mT", k), TT, lambda tt: mg[:, tt, k * P:(k + 1) * P])

            def scores(u):
                hh, qt = divmod(u, TT)
                name = ("xs", hh, qt)
                pe.wait_ge(*G.free(name, l))
                for i in range(2):
                    mm = pe.matmul(G.ps(name)[:, 0:MEM], qx8[:, 2 * hh + i, qt * P:(qt + 1) * P], kx8[:, 2 * hh + i, :],
                                   start=(i == 0), stop=(i == 1))
                mm.then_inc(*G.full(name))

            def probs_turn(u):
                name = ("xp", *divmod(u, TT))
                pe.wait_ge(*px_ready.at(l, u + 1))
                turn(name, MT, lambda i: Px[:, u % 2, i * P:(i + 1) * P])

            def step_xatt(step):
                hh, qt = step[1:]
                u = hh * TT + qt
                if u == 0:
                    for name in (("xk", KD - 1), ("xv1", MT - 1)):
                        pe.wait_ge(*G.evacuated(name, l))
                    scores(0)
                    scores(1)
                    probs_turn(0)
                if u + 2 < XH * TT:
                    scores(u + 2)
                if u + 1 < XH * TT:
                    probs_turn(u + 1)
                if qt == TT - 1:
                    pe.wait_ge(*G.evacuated(("xp", hh, TT - 1), l))
                    for i in range(2):
                        name = ("xo", hh, i)
                        pe.wait_ge(*G.free(name, l))
                        for m in range(MT):
                            mm = pe.matmul(G.ps(name)[:, :], vx[:, m, hh * XD + i * P:hh * XD + (i + 1) * P], PxT[:, hh % 2, m, :],
                                           start=(m == 0), stop=(m == MT - 1))
                        mm.then_inc(*G.full(name))

            table = {"norm": step_norm, "mem": step_mem, "fm": step_fm, "tm": step_tm, "ret_pair": step_ret_pair, "ret_in": step_ret_in,
                     "ret_out": step_ret_out, "ret_turn": step_ret_turn, "sg_w": step_sg_w, "sg_mix": step_sg_mix,
                     "sg_turn": step_sg_turn, "mg_turn": step_mg_turn, "xatt": step_xatt}
            for step in steps2:
                if step[0] in table:
                    table[step[0]](step)

        def scalar_two(act, l):
            G, ring = G2, ring2
            eu, n_et, n_sq, sums_made = [None, None], [0], [0], [0]
            step_sig, hi_s, ex, sq_s, ss_s, rs = act_step[1], hi_done[1], exp_done[1], sq_done[1], ss_done[1], rs_done[1]

            def link(ins):
                ins.then_inc(*step_sig.up())
                act.wait_ge(*step_sig.last(l))

            def split(j):
                if j < N2:
                    act.wait_ge(*ring.loaded(l, j))
                    act.wait_ge(*ring.parts_free(l, j))
                    nc.scalar.copy(whi[:, j % SLOTS, :], raw[:, j % SLOTS, :]).then_inc(hi_split, 1)

            def exp_place(name):
                i = n_et[0] % 2
                n_et[0] += 1
                if eu[i]:
                    act.wait_ge(*G.evacuated(eu[i], l))
                eu[i] = name
                return et[:, i, :]

            def exp_neg(name):
                place = exp_place(name)
                act.wait_ge(*G.filled(name, l))
                nc.scalar.activation(place, G.ps(name)[:, :], ACT.Exp, scale=-1.0).then_inc(*ex.up())

            def square_place():
                i = n_sq[0]
                n_sq[0] += 1
                if i >= 2:
                    act.wait_ge(*ss_s.at(l, i - 1))
                return sq[:, i % 2, :]

            def root(dst, src, count, cols, need):
                if need:
                    act.wait_ge(*ss_s.at(l, need))
                if rs.made:
                    act.wait_ge(*rs.last(l))
                link(nc.scalar.activation(lnv[:, 0:cols], src, ACT.Ln, scale=1.0 / count, bias=eps[:, :]))
                nc.scalar.activation(dst, lnv[:, 0:cols], ACT.Exp, scale=-0.5).then_inc(*rs.up())

            def hi(dst, name, src=None):
                act.wait_ge(*G.filled(name, l))
                nc.scalar.copy(dst, G.ps(name)[:, :] if src is None else src).then_inc(*hi_s.up())

            def copy_group(dst, name, src=None):
                act.wait_ge(*G.filled(name, l))
                nc.scalar.copy(dst, G.ps(name)[:, :] if src is None else src).then_inc(*G.empty(name))

            def squares(src, sums):
                link(nc.scalar.activation(sq[:, :, :].rearrange("p a t -> p (a t)"), src, ACT.Square, accum_out=sums))

            def step_norm(step):
                which = step[1]
                gain = {"mix": gmix2, "xa": gxa, "ffn": gffn}[which]
                act.wait_ge(params[1], l * PARAMS_TWO + PARAMS_TWO)
                for tt in range(TT):
                    if which == "mix":
                        act.wait_ge(*G.e[tt].at(l, 0))
                    else:
                        act.wait_ge(*G.evacuated(({"xa": "wo1", "ffn": "xw1"}[which], tt), l))
                    squares(h[:, tt, :], ss[:, tt:tt + 1])
                if which == "xa":
                    act.dma_start(mem[:, :, :], d["mem_2"][0].rearrange("(m p) c -> p m c", p=P)).then_inc(mem_loaded, 16)
                root(rstd[:, :], ss[:, :], D, TT, 0)
                for k in range(KD):
                    act.wait_ge(*G.filled((which, k), l))
                    nc.scalar.activation(xhi[:, k, :], G.ps((which, k))[:, :], ACT.Identity, scale=gain[:, k:k + 1]).then_inc(*hi_s.up())

            def step_mem(step):
                act.wait_ge(mem_loaded, l * 16 + 16)
                for m in range(MT):
                    squares(mem[:, m, :], ssm[:, m:m + 1])
                root(rsm[:, 0:MT], ssm[:, 0:MT], D, MT, 0)
                for k in range(KD):
                    act.wait_ge(*G.filled(("mm", k), l))
                    nc.scalar.activation(mmT[:, 0, k, :], G.ps(("mm", k))[:, 0:MEM], ACT.Identity, scale=gmem[:, k:k + 1]).then_inc(*hi_s.up())

            def step_fm(step):
                name, i = step[1:3], step[2]
                if step[1] == "ax":
                    copy_group(cx[:, i, :], name)
                elif step[1] == "ab":
                    act.wait_ge(*G.evacuated(name, l))
                    nc.scalar.copy(yaT[:, 0, i, :], cx[:, i, :]).then_inc(*hi_s.up())
                elif step[1] == "xq":
                    act.wait_ge(*G.filled(name, l))
                    nc.scalar.activation(qx8[:, i, :], G.ps(name)[:, :], ACT.Identity, scale=XD ** -0.5).then_inc(*G.empty(name))
                elif step[1] == "u":
                    if i >= 2:
                        act.wait_ge(*g_ready.at(l, i - 1))
                    exp_neg(name)
                elif step[1] == "w":
                    act.wait_ge(*G.evacuated(name, l))
                    nc.scalar.copy(gT[:, 0, i % HALVES[0][1], :], et[:, (n_et[0] - 1) % 2, :]).then_inc(*hi_s.up())

            def step_tm(step):
                _, kind, i, n, _ = step
                if i < n - 1:
                    return
                for tt in range(MT if kind[:2] == "xv" else TT):
                    name = (kind, tt)
                    if kind == "v":
                        copy_group(v2[:, tt, :], name)
                    elif kind[:2] == "xv":
                        c = int(kind[2]) * T
                        copy_group(vx[:, tt, c:c + T], name)
                    elif kind == "z":
                        place = square_place()
                        act.wait_ge(*G.filled(name, l))
                        nc.scalar.activation(place, G.ps(name)[:, :], ACT.Square).then_inc(*sq_s.up())
                        sums_made[0] += 1
                        e = exp_place(name)
                        act.wait_ge(*ss_s.at(l, sums_made[0]))
                        nc.scalar.activation(e, place, ACT.Exp, scale=-2.0 * (2.0 / np.pi) ** 0.5).then_inc(*ex.up())
                    elif kind[0] == "g":
                        exp_neg(name)

            def step_ret_pair(step):
                p = step[1]
                copy_group(qp[:, :], ("qP", p))
                copy_group(kp[:, :], ("kP", p))

            def step_ret_out(step):
                place = square_place()
                act.wait_ge(*G.evacuated(("ro", step[1]), l))
                nc.scalar.activation(place, tA[:, :], ACT.Square).then_inc(*sq_s.up())
                sums_made[0] += 1
                root(rsv[:, :], ssv[:, :], P, TT, sums_made[0])

            def step_ret_turn(step):
                hi(ybT[:, 0, step[1], :], ("ybT", step[1]))

            def step_sg_w(step):
                copy_group(wsT[:, :, :].rearrange("p g c -> p (g c)"), ("ws",))

            def step_sg_norm(step):
                n_sq[0] += 1
                sums_made[0] += 1
                root(rsm[:, 4:8], ssm[:, 4:8], 256, TT, sums_made[0])

            def step_sg_turn(step):
                for k in range(2):
                    hi(ycT[:, 0, k, :], ("ycT", k))

            def step_mg_turn(step):
                for k in range(KD):
                    hi(xhi[:, k, :], ("mT", k))

            def probs(u):
                name = ("xs", *divmod(u, TT))
                act.wait_ge(*nm_ready[1].next(l))
                nc.scalar.activation(Px[:, u % 2, :], G.ps(name)[:, 0:MEM], ACT.Exp, bias=nmx[:, u % 4:u % 4 + 1],
                                     accum_out=sumx[:, u % 4:u % 4 + 1]).then_inc(*G.empty(name))

            def turned(u):
                hh, qt = divmod(u, TT)
                name = ("xp", hh, qt)
                copy_group(PxT[:, hh % 2, :, qt * P:(qt + 1) * P], name, G.ps(name)[:, 0:MEM].rearrange("p (m q) -> p m q", m=MT))

            def step_xatt(step):
                hh, qt = step[1:]
                u = hh * TT + qt
                if u == 0:
                    probs(0)
                    probs(1)
                    turned(0)
                if u + 2 < XH * TT:
                    probs(u + 2)
                if u + 1 < XH * TT:
                    turned(u + 1)
                if qt == TT - 1:
                    for i in range(2):
                        hi(xhi[:, 2 * hh + i, :], ("xo", hh, i))

            table = {"norm": step_norm, "mem": step_mem, "fm": step_fm, "tm": step_tm, "ret_pair": step_ret_pair,
                     "ret_out": step_ret_out, "ret_turn": step_ret_turn, "sg_w": step_sg_w, "sg_norm": step_sg_norm,
                     "sg_turn": step_sg_turn, "mg_turn": step_mg_turn, "xatt": step_xatt}
            for j in range(SLOTS - 1):
                split(j)
            for step in steps2:
                if step in number2:
                    split(number2[step] + SLOTS - 1)
                if step[0] in table:
                    table[step[0]](step)

        def vector_two(dve, l):
            G = G2
            tt_, ts, stt = nc.vector.tensor_tensor, nc.vector.tensor_scalar, nc.vector.scalar_tensor_tensor
            step_sig, hi_s, ex, sq_s, ss_s, rs = dve_step[1], hi_done[1], exp_done[1], sq_done[1], ss_done[1], rs_done[1]
            n_et, n_sq = [0], [0]

            def link(ins):
                ins.then_inc(*step_sig.up())
                dve.wait_ge(*step_sig.last(l))

            def et_place():
                i = n_et[0] % 2
                n_et[0] += 1
                dve.wait_ge(*ex.next(l))
                return et[:, i, :]

            def lo(dst, name, part, src=None, gain=None):
                dve.wait_ge(*hi_s.next(l))
                ps = G.ps(name)[:, :] if src is None else src
                if gain is None:
                    tt_(dst, ps, part.bitcast(F32), ALU.subtract).then_inc(*G.empty(name))
                else:
                    stt(dst, ps, gain, part.bitcast(F32), ALU.mult, ALU.subtract).then_inc(*G.empty(name))

            def diagonals(scale, tiles):
                dve.wait_ge(*rs.next(l))
                for tt in range(tiles):
                    ins = ts(diag[:, tt, :], ident[:, :], scale[:, tt:tt + 1], None, ALU.mult)
                ins.then_inc(*diag_ready[1].up())

            def step_norm(step):
                which = step[1]
                gain = {"mix": gmix2, "xa": gxa, "ffn": gffn}[which]
                dve.wait_ge(params[1], l * PARAMS_TWO + PARAMS_TWO)
                diagonals(rstd, TT)
                for k in range(KD):
                    lo(xlo[:, k, :], (which, k), xhi[:, k, :], gain=gain[:, k:k + 1])

            def step_mem(step):
                diagonals(rsm, MT)
                for k in range(KD):
                    lo(mmT[:, 1, k, :], ("mm", k), mmT[:, 0, k, :], src=G.ps(("mm", k))[:, 0:MEM], gain=gmem[:, k:k + 1])

            def step_fm(step):
                name, i = step[1:3], step[2]
                ps = G.ps(name)[:, :]
                if step[1] == "ac":
                    nc.vector.memset(zp[:, i, 0:2], 0.0)
                    dve.wait_ge(*G.evacuated(("ax", i), l))
                    dve.wait_ge(*G.filled(name, l))
                    tt_(zp[:, i, 2:T + 2], cx[:, i, :], ps, ALU.mult).then_inc(*G.empty(name))
                elif step[1] == "ab":
                    dve.wait_ge(*G.evacuated(("ac", i), l))
                    link(ts(tB[:, :], zp[:, i, 0:T], convw[:, i, 0:1], None, ALU.mult))
                    link(stt(tB[:, :], zp[:, i, 1:T + 1], convw[:, i, 1:2], tB[:, :], ALU.mult, ALU.add))
                    link(stt(tB[:, :], zp[:, i, 2:T + 2], convw[:, i, 2:3], tB[:, :], ALU.mult, ALU.add))
                    dve.wait_ge(*G.filled(name, l))
                    tt_(cx[:, i, :], tB[:, :], ps, ALU.mult).then_inc(*G.empty(name))
                    dve.wait_ge(*hi_s.next(l))
                    tt_(yaT[:, 1, i, :], cx[:, i, :], yaT[:, 0, i, :].bitcast(F32), ALU.subtract).then_inc(*ya_ready.up())
                elif step[1] == "xk":
                    dve.wait_ge(*G.filled(name, l))
                    nc.vector.tensor_copy(kx8[:, i, :], G.ps(name)[:, 0:MEM]).then_inc(*G.empty(name))
                elif step[1] == "u":
                    e = et_place()
                    link(ts(e, e, 1.0, None, ALU.add))
                    link(nc.vector.reciprocal(e, e))
                    tt_(e, e, ps, ALU.mult).then_inc(*G.empty(name))
                elif step[1] == "w":
                    e = et[:, (n_et[0] - 1) % 2, :]
                    dve.wait_ge(*G.evacuated(("u", i), l))
                    dve.wait_ge(*G.filled(name, l))
                    tt_(e, e, ps, ALU.mult).then_inc(*G.empty(name))
                    dve.wait_ge(*hi_s.next(l))
                    f = i % HALVES[0][1]
                    tt_(gT[:, 1, f, :], e, gT[:, 0, f, :].bitcast(F32), ALU.subtract).then_inc(*g_ready.up())

            def add_to_h(name, n):
                at = h[:, name[1], n * T:(n + 1) * T]
                dve.wait_ge(*G.filled(name, l))
                tt_(at, at, G.ps(name)[:, :], ALU.add).then_inc(*G.empty(name))

            def step_tm(step):
                _, kind, i, n, _ = step
                if i < n - 1 or kind == "v" or kind[:2] == "xv":
                    return
                for tt in range(TT):
                    name = (kind, tt)
                    ps = G.ps(name)[:, :]
                    if kind == "g":
                        e, g = et_place(), gg[:, tt, :]
                        link(ts(g, e, 1.0, None, ALU.add))
                        link(nc.vector.reciprocal(g, g))
                        tt_(g, g, ps, ALU.mult).then_inc(*G.empty(name))
                        dve.wait_ge(*G.evacuated(name, l))
                        link(tt_(g, g, retgn[:, :], ALU.mult))
                    elif kind == "qk":
                        dve.wait_ge(*G.filled(name, l))
                        x = ps.rearrange("p (h d) -> p h d", d=RK)
                        cos, sin = (k2[c][:, tt * 32:(tt + 1) * 32].unsqueeze(1).to_broadcast([P, 2 * RH, 32]) for c in ("rcos", "rsin"))
                        part = [t[:, 0:256].rearrange("p (h d) -> p h d", d=32) for t in (tA, tB, tC, tD)]
                        tt_(part[0], x[:, :, 0:32], cos, ALU.mult)
                        tt_(part[1], x[:, :, 32:64], sin, ALU.mult)
                        tt_(part[2], x[:, :, 0:32], sin, ALU.mult)
                        tt_(part[3], x[:, :, 32:64], cos, ALU.mult).then_inc(*G.empty(name))
                        dve.wait_ge(*G.evacuated(name, l))
                        tt_(qkr[:, tt, :, 0:32], part[0], part[1], ALU.subtract)
                        ins = tt_(qkr[:, tt, :, 32:64], part[2], part[3], ALU.add)
                        if tt == TT - 1:
                            ins.then_inc(*rot_ready.up())
                        else:
                            link(ins)
                    elif kind == "z":
                        place = sq[:, n_sq[0] % 2, :]
                        n_sq[0] += 1
                        dve.wait_ge(*sq_s.next(l))
                        link(ts(place, place, 0.044715, 1.0, ALU.mult, ALU.add))
                        tt_(place, place, ps, ALU.mult).then_inc(*ss_s.up())
                        e = et_place()
                        link(ts(e, e, 1.0, None, ALU.add))
                        link(nc.vector.reciprocal(e, e))
                        tt_(gg[:, tt, :], e, ps, ALU.mult).then_inc(*G.empty(name))
                    elif kind[0] == "g":
                        at = slice(int(kind[2]) * T, (int(kind[2]) + 1) * T)
                        g = mg[:, tt, at] if kind[1] == "a" else gg[:, tt, :]
                        e = et_place()
                        link(ts(g, e, 1.0, None, ALU.add))
                        nc.vector.reciprocal(g, g).then_inc(*G.empty(name))
                    elif kind[0] == "y":
                        at = slice(int(kind[2]) * T, (int(kind[2]) + 1) * T)
                        m = mg[:, tt, at]
                        g = m if kind[1] == "a" else gg[:, tt, :]
                        dve.wait_ge(*G.evacuated(("g" + kind[1:], tt), l))
                        dve.wait_ge(*G.filled(name, l))
                        tt_(g, g, ps, ALU.mult).then_inc(*G.empty(name))
                        if kind[1] != "a":
                            dve.wait_ge(*G.evacuated(name, l))
                            ins = tt_(m, m, g, ALU.add)
                            if kind == "yc1" and tt == TT - 1:
                                ins.then_inc(*mg_ready.up())
                            else:
                                link(ins)
                    elif kind[:2] in ("wo", "xw"):
                        add_to_h(name, int(kind[2]))
                    elif kind[0] == "d":
                        add_to_h(name, int(kind[2]))

            def step_ret_pair(step):
                p = step[1]
                dve.wait_ge(*G.evacuated(("qP", p), l))
                by_chunk = lambda t: t[:, :].rearrange("p (c q) -> p c q", c=TT)
                tt_(by_chunk(qx), by_chunk(qp), k2["xi"][:, p * P:(p + 1) * P].unsqueeze(1).to_broadcast([P, TT, P]), ALU.mult)
                dve.wait_ge(*G.evacuated(("kP", p), l))
                k = qkr[:, :, 4 + 2 * p:6 + 2 * p, :]
                tt_(k, k, k2["zeta"][:, 2 * p:2 * p + 2].unsqueeze(1).unsqueeze(3).to_broadcast([P, TT, 2, RK]), ALU.mult)\
                    .then_inc(*qx_ready.up())

            def step_ret_in(step):
                hh = step[1]
                part = slice(hh % 2 * RK, (hh % 2 + 1) * RK)
                name = ("rs", hh)
                dve.wait_ge(*G.filled(name, l))
                tt_(ds[:, :].rearrange("p (c q) -> p c q", c=TT), G.ps(name)[:, :].rearrange("p (c q) -> p c q", c=TT),
                    k2["decay"][:, hh * P:(hh + 1) * P].unsqueeze(1).to_broadcast([P, TT, P]), ALU.mult).then_inc(*G.empty(name))
                name = ("rk", hh)
                ps = G.ps(name)[part, :]
                dve.wait_ge(*G.filled(name, l))
                link(nc.vector.tensor_copy(R[part, 0, :], ps[:, 0:P]))
                link(stt(R[part, 1, :], R[part, 0, :], RESCALE[hh], ps[:, P:2 * P], ALU.mult, ALU.add))
                stt(R[part, 2, :], R[part, 1, :], RESCALE[hh], ps[:, 2 * P:3 * P], ALU.mult, ALU.add).then_inc(*G.empty(name))

            def step_ret_out(step):
                hh = step[1]
                name = ("ro", hh)
                by_chunk = lambda t: t.rearrange("p (c q) -> p c q", c=TT)
                ps = by_chunk(G.ps(name)[:, :])
                wide = lambda t: t[:, :].unsqueeze(2).to_broadcast([P, TT, P])
                dve.wait_ge(*G.filled(name, l))
                link(nc.vector.tensor_reduce(mux[:, :], ps, AX, ALU.add))
                link(ts(mux[:, :], mux[:, :], 1.0 / RV, None, ALU.mult))
                tt_(by_chunk(tA[:, :]), ps, wide(mux), ALU.subtract).then_inc(*G.empty(name))
                place = sq[:, n_sq[0] % 2, :]
                n_sq[0] += 1
                dve.wait_ge(*sq_s.next(l))
                nc.vector.tensor_reduce(ssv[:, :], by_chunk(place), AX, ALU.add).then_inc(*ss_s.up())
                dve.wait_ge(*rs.next(l))
                link(tt_(by_chunk(tA[:, :]), by_chunk(tA[:, :]), wide(rsv), ALU.mult))
                g = gg[:, :, hh * P:(hh + 1) * P]
                tt_(g, g, by_chunk(tA[:, :]), ALU.mult).then_inc(*yb_ready.up())

            def step_ret_turn(step):
                lo(ybT[:, 1, step[1], :], ("ybT", step[1]), ybT[:, 0, step[1], :])

            def step_sg_w(step):
                tt_(sgw[:, :, :], sgw[:, :, :], k2["tril"][:, :].unsqueeze(1).to_broadcast([P, SGG, P]), ALU.mult).then_inc(*sgw_ready.up())

            def step_sg_norm(step):
                zv = gg[:, :, 256:512]
                wide = lambda t: t.unsqueeze(2).to_broadcast([P, TT, 256])
                c3 = cx[:, :, :].rearrange("p a (b d) -> p (a b) d", b=2)
                dve.wait_ge(*G.evacuated(("z", TT - 1), l))
                link(nc.vector.tensor_reduce(mux[:, :], zv, AX, ALU.add))
                link(ts(mux[:, :], mux[:, :], 1.0 / 256, None, ALU.mult))
                link(tt_(zv, zv, wide(mux[:, :]), ALU.subtract))
                link(tt_(c3, zv, zv, ALU.mult))
                nc.vector.tensor_reduce(ssm[:, 4:8], c3, AX, ALU.add).then_inc(*ss_s.up())
                n_sq[0] += 1
                dve.wait_ge(*rs.next(l))
                link(tt_(zv, zv, wide(rsm[:, 4:8]), ALU.mult))
                tt_(zv, zv, sgln[:, :].unsqueeze(1).to_broadcast([P, TT, 256]), ALU.mult).then_inc(*sg_ready.up())

            def step_sg_mix(step):
                for tt in range(TT):
                    name = ("vm", tt)
                    dve.wait_ge(*G.filled(name, l))
                    t = (tA, tB)[tt // 2][:, tt % 2 * 256:(tt % 2 + 1) * 256]
                    t3 = t.rearrange("p (g d) -> p g d", g=SGG)
                    link(tt_(t3, G.ps(name)[:, 0:256].rearrange("p (g d) -> p g d", g=SGG), sgb[:, :].unsqueeze(2).to_broadcast([P, SGG, 64]), ALU.add))
                    u = gg[:, tt, 0:256]
                    tt_(u, u, t, ALU.mult).then_inc(*G.empty(name))

            def step_sg_turn(step):
                for k in range(2):
                    lo(ycT[:, 1, k, :], ("ycT", k), ycT[:, 0, k, :])

            def step_mg_turn(step):
                for k in range(KD):
                    lo(xlo[:, k, :], ("mT", k), xhi[:, k, :])

            def greatest(u):
                name = ("xs", *divmod(u, TT))
                dve.wait_ge(*G.filled(name, l))
                nc.vector.tensor_reduce(nmx[:, u % 4:u % 4 + 1], G.ps(name)[:, 0:MEM], AX, ALU.max, negate=True).then_inc(*nm_ready[1].up())

            def shares(u):
                dve.wait_ge(*G.evacuated(("xs", *divmod(u, TT)), l))
                c = slice(u % 4, u % 4 + 1)
                link(nc.vector.reciprocal(recx[:, c], sumx[:, c]))
                ts(Px[:, u % 2, :], Px[:, u % 2, :], recx[:, c], None, ALU.mult).then_inc(*px_ready.up())

            def step_xatt(step):
                hh, qt = step[1:]
                u = hh * TT + qt
                if u == 0:
                    greatest(0)
                    greatest(1)
                    shares(0)
                if u + 2 < XH * TT:
                    greatest(u + 2)
                if u + 1 < XH * TT:
                    shares(u + 1)
                if qt == TT - 1:
                    for i in range(2):
                        lo(xlo[:, 2 * hh + i, :], ("xo", hh, i), xhi[:, 2 * hh + i, :])

            table = {"norm": step_norm, "mem": step_mem, "fm": step_fm, "tm": step_tm, "ret_pair": step_ret_pair, "ret_in": step_ret_in,
                     "ret_out": step_ret_out, "ret_turn": step_ret_turn, "sg_w": step_sg_w, "sg_norm": step_sg_norm,
                     "sg_mix": step_sg_mix, "sg_turn": step_sg_turn, "mg_turn": step_mg_turn, "xatt": step_xatt}
            for step in steps2:
                if step[0] in table:
                    table[step[0]](step)

        def of_layer(name, l):
            return d[name][bass.ds(l, 1)]

        def weights(spec, l):
            key, k0, nk, c0, cols = spec
            if key[:6] == "cmp_w1":
                src = d["cmp_w1"][bass.ds(l, 1), int(key[-1]), k0 * P:(k0 + nk) * P, c0:c0 + cols]
            else:
                src = d[key][bass.ds(l, 1), k0 * P:(k0 + nk) * P, c0:c0 + cols]
            return src.rearrange("o (k p) n -> p (o k) n", p=P)

        block = ctx.enter_context(nc.Block())
        setup_loads = []

        @block.sync
        def _(sp):
            def load(dst, src, done):
                sp.dma_start(dst, src).then_inc(done, 16)

            def load_across(dst, src, done):
                sp.dma_start(dst, src, allow_slow_non_contiguous=True).then_inc(done, 16)

            def load_setup(dst, src):
                load(dst, src, setup)
                setup_loads.append(dst)

            def params_one(l):
                load_across(gmix[:, :], of_layer("norm_g", l).rearrange("o (k p) -> p (o k)", p=P), params[0])
                load_across(gple[:, :], of_layer("ple_norm_g", l).rearrange("o (k p) -> p (o k)", p=P), params[0])
                load(onorm[:, :], of_layer("hgrn_onorm_g", l).to_broadcast([P, P]), params[0])
                load(qg[:, :], of_layer("nsa_qnorm_g", l).to_broadcast([P, DH]), params[0])
                load(kg[:, :, :], of_layer("nsa_knorm_g", l).to_broadcast([P, 3, DH]), params[0])
                load(w2[:, :, :], of_layer("cmp_w2", l).rearrange("o w p d -> p (o w) d"), params[0])
                load(pe_raw[0:32, :], of_layer("cmp_pe", l).rearrange("o w (j a) d -> (o w j) (a d)", a=2), params[0])

            def params_two(l):
                for n, t in k2.items():
                    load(t[:, :], d["two_" + n], params[1])
                for t, n in ((gmix2, "norm_mix_2"), (gxa, "norm_xa_2"), (gmem, "norm_mem_2"), (gffn, "norm_ffn_2")):
                    load_across(t[:, :], of_layer(n, l).rearrange("o (k p) -> p (o k)", p=P), params[1])
                for t in range(2):
                    load_across(convw[:, t, :], of_layer("conv_w_2", l)[:, :, t * P:(t + 1) * P].rearrange("o k p -> p (o k)"), params[1])
                load_across(sgb[:, :], of_layer("sg_b_2", l).rearrange("o g c -> c (o g)"), params[1])
                load(retgn[:, :], of_layer("ret_gn_2", l).to_broadcast([P, T]), params[1])
                load(sgln[:, :], of_layer("sg_ln_2", l).to_broadcast([P, 256]), params[1])
                load(sgw[:, :, :], of_layer("sg_w_2", l).rearrange("o g c m -> c (o g) m"), params[1])

            def stage(l, chunks, ring, emptied, load_params):
                for j, spec in enumerate(chunks):
                    if j == SLOTS:
                        sp.wait_ge(made_ready, 3)
                        sp.wait_ge(*emptied[TT - 1].at(l, 0))
                        load_params(l)
                    _, _, nk, _, cols = spec
                    sp.wait_ge(*ring.raw_free(l, j))
                    load(raw[:, j % SLOTS, 0:nk * cols].rearrange("p (k n) -> p k n", k=nk), weights(spec, l), raw_loaded[j % SLOTS])

            load_setup(h[:, :, :], d["x"][0].rearrange("(t p) c -> p t c", p=P))
            load_setup(ident[:, :], d["one_ident"])
            load_across(lbraw[:, :, :], d["hgrn_lb"].rearrange("a (h p) -> p a h", p=P), setup)
            setup_loads.append(lbraw)
            for n, t in k1.items():
                load_setup(t[:, :], d["one_" + n])
            load_setup(tA[:, 0:P], d["one_causal"])
            load_setup(dE[:, :, :].rearrange("p a t -> p (a t)"), d["masks"])
            with sp.Fori(0, DEPTH) as l:
                stage(l, chunks1, ring1, G1.e, params_one)
            with sp.Fori(0, DEPTH) as l:
                stage(l, chunks2, ring2, G2.e, params_two)
            sp.wait_ge(*g_ready.at(DEPTH - 1, FT))
            load(gfin[:, :], d["final_norm_2"].unsqueeze(0).to_broadcast([P, D]), gain_loaded)
            for tt in range(TT):
                sp.wait_ge(fin_done, tt + 1)
                load(out[0, tt * P:(tt + 1) * P, :], h[:, tt, :], out_done)
            sp.wait_ge(out_done, 16 * TT)

        ready = 16 * len(setup_loads)

        @block.gpsimd
        def _(pool):
            with pool.Fori(0, DEPTH * (N1 + N2) // SLOTS) as it:
                for s in range(SLOTS):
                    pool.wait_ge(hi_split, it * SLOTS + (s + 1))
                    nc.gpsimd.tensor_tensor(wlo[:, s, :], raw[:, s, :], whi[:, s, :].bitcast(F32), ALU.subtract).then_inc(lo_split, 1)

        floor, top, e2, share = (lbs[:, 2 * i:2 * i + 2, :] if i < 3 else lbt[:, :, 2, :] for i in range(4))
        last = DEPTH - 1

        @block.vector
        def _(dve):
            steps = [0]

            def link(ins):
                steps[0] += 1
                ins.then_inc(setup_step, 1)
                dve.wait_ge(setup_step, steps[0])

            tt_, ts = nc.vector.tensor_tensor, nc.vector.tensor_scalar
            nc.vector.memset(lnv[:, 30:31], 0.0).then_inc(lo_split, SLOTS)
            nc.vector.memset(lnv[:, 31:32], 0.0).then_inc(chunk_begun, SLOTS - 1)
            for b in range(8):
                nc.vector.memset(lnv[:, b:b + 1], 0.0).then_inc(G1.e[b].sem, 1)
            link(nc.vector.memset(eps[:, :], EPS))
            link(nc.vector.memset(ones[:, :], 1.0))
            for t in (At[:, :, :, :], Ql[:, :, :], Kl[:, :, :], pe_raw[:, :]):
                link(nc.vector.memset(t, 0.0))
            dve.wait_ge(setup, ready)
            link(nc.vector.tensor_copy(identb[:, :], ident[:, :]))
            link(nc.vector.tensor_copy(masks[:, :, :].rearrange("p a t -> p (a t)"), dE[:, :, :].rearrange("p a t -> p (a t)")))
            link(nc.vector.tensor_copy(causal[:, :], tA[:, 0:P]))
            big = top[:, 0, :]
            link(tt_(big, lbraw[:, 0, :], lbraw[:, 1, :], ALU.max))
            tt_(e2, lbraw[:, :, :], big.unsqueeze(1).to_broadcast([P, 2, HG]), ALU.subtract).then_inc(made_ready, 1)
            dve.wait_ge(act_setup, 1)
            link(tt_(big, e2[:, 0, :], e2[:, 1, :], ALU.add))
            link(nc.vector.reciprocal(big, big))
            link(tt_(e2, e2, big.unsqueeze(1).to_broadcast([P, 2, HG]), ALU.mult))
            link(tt_(big, e2[:, 0, :], e2[:, 1, :], ALU.add))
            link(tt_(floor[:, 0, :], e2[:, 0, :], e2[:, 0, :], ALU.subtract))
            link(tt_(floor[:, 1, :], big, e2[:, 0, :], ALU.subtract))
            link(ts(top, floor, 1e-37, None, ALU.max))
            ts(e2, floor, 1e-37, NEG, ALU.is_lt, ALU.mult).then_inc(made_ready, 1)
            dve.wait_ge(act_setup, 2)
            link(tt_(lbt[:, :, 1, :], lbt[:, :, 1, :], e2, ALU.add))
            link(ts(lbt[:, :, 0, :], lbt[:, :, 0, :], NEG, None, ALU.max))
            tt_(lbt[:, :, 2, :], lbt[:, :, 0, :], lbt[:, :, 1, :], ALU.subtract).then_inc(made_ready, 1)
            dve.wait_ge(made_ready, 3)
            with dve.Fori(0, DEPTH) as l:
                vector_one(dve, l)
            with dve.Fori(0, DEPTH) as l:
                vector_two(dve, l)
            dve.wait_ge(gain_loaded, 16)
            for tt in range(TT):
                dve.wait_ge(fin_root, tt + 1)
                nc.vector.scalar_tensor_tensor(h[:, tt, :], h[:, tt, :], rstd[:, tt:tt + 1], gfin[:, :], ALU.mult, ALU.mult).then_inc(fin_done, 1)

        @block.scalar
        def _(act):
            act.wait_ge(made_ready, 1)
            nc.scalar.activation(e2, e2, ACT.Exp).then_inc(act_setup, 1)
            act.wait_ge(made_ready, 2)
            nc.scalar.activation(lbt[:, :, 0, :], floor, ACT.Ln, scale=-1.0, bias=1.0)
            nc.scalar.activation(lbt[:, :, 1, :], top, ACT.Ln).then_inc(act_setup, 1)
            act.wait_ge(setup, ready)
            act.wait_ge(made_ready, 3)
            with act.Fori(0, DEPTH) as l:
                scalar_one(act, l)
            with act.Fori(0, DEPTH) as l:
                scalar_two(act, l)
            for tt in range(TT):
                act.wait_ge(*G2.evacuated(("d11", tt), last))
                nc.scalar.activation(sq[:, :, :].rearrange("p a t -> p (a t)"), h[:, tt, :], ACT.Square, accum_out=ss[:, tt:tt + 1]).then_inc(fin_step, 1)
                act.wait_ge(fin_step, 2 * tt + 1)
                nc.scalar.activation(lnv[:, tt:tt + 1], ss[:, tt:tt + 1], ACT.Ln, scale=1.0 / D, bias=eps[:, :]).then_inc(fin_step, 1)
                act.wait_ge(fin_step, 2 * tt + 2)
                nc.scalar.activation(rstd[:, tt:tt + 1], lnv[:, tt:tt + 1], ACT.Exp, scale=-0.5).then_inc(fin_root, 1)

        @block.tensor
        def _(pe):
            pe.wait_ge(setup, ready)
            pe.wait_ge(made_ready, 3)
            with pe.Fori(0, DEPTH) as l:
                tensor_one(pe, l)
            with pe.Fori(0, DEPTH) as l:
                tensor_two(pe, l)

        return {(name, stage_): s.made for name, stage_, s in made}


INPUTS = ["x", "p", "norm_g", "w_in", "hgrn_lb", "hgrn_onorm_g", "nsa_qnorm_g", "nsa_knorm_g", "cmp_pe", "cmp_w1", "cmp_w2",
          "w_out", "ple_norm_g", "w_pg", "w_pp", "mem_2", "norm_mix_2", "w_in_2", "conv_w_2", "w_a_out_2", "ret_gn_2",
          "w_b_out_2", "sg_ln_2", "sg_w_2", "sg_b_2", "w_c_out_2", "w_o_2", "norm_xa_2", "norm_mem_2", "xa_q_2", "xa_k_2",
          "xa_v_2", "xa_o_2", "norm_ffn_2", "w1_2", "w3_2", "w2_2", "final_norm_2"]


def kernel(**inputs):
    import numpy as _np
    import concourse.bacc as _bacc
    from concourse import mybir as _mybir
    from concourse.bass_utils import run_bass_kernel_spmd as _run

    one, two, masks = constants()
    arrays = {name: _np.ascontiguousarray(inputs[name]) for name in INPUTS}
    arrays.update({"one_" + n: a for n, a in one.items()})
    arrays.update({"two_" + n: _np.ascontiguousarray(a) for n, a in two.items()})
    arrays["masks"] = masks

    def program(counts):
        nc = _bacc.Bacc("TRN2", target_bir_lowering=False, num_devices=1)
        d = {n: nc.dram_tensor("in_" + n, a.shape, _mybir.dt.from_np(a.dtype), kind="ExternalInput").ap() for n, a in arrays.items()}
        d["w1"] = {n: a.shape[1] for n, a in one.items()}
        d["w2"] = {n: a.shape[1] for n, a in two.items()}
        out = nc.dram_tensor("out_0", (1, T, D), _mybir.dt.float32, kind="ExternalOutput").ap()
        return nc, build(nc, d, out, counts)

    _, counts = program({})
    nc, _ = program(counts)
    r = _run(nc, [{"in_" + n: a for n, a in arrays.items()}], core_ids=[0])
    return r.results[0]["out_0"]
```

```python
from contextlib import ExitStack

import numpy as np

import concourse.bass as bass
from concourse import mybir

F32 = mybir.dt.float32
F32R = mybir.dt.float32r
BF16 = mybir.dt.bfloat16
U8 = mybir.dt.uint8
ALU = mybir.AluOpType
ACT = mybir.ActivationFunctionType
AX = mybir.AxisListType.X

P = 128
DEPTH = 2
D = 1024
T = 512
TT = T // P
KD = D // P
EPS = 1e-6
NEG = -1e30
LOG_EXP_TABLES = 6

HG = 4
LEVELS = 7
NH, NKV, DH = 8, 2, 64
NG = NH // NKV
NCMP = (T - 32) // 16 + 1
PLE = 256
MEM = 256
MT = MEM // P
RH, RK, RV = 4, 64, 128
SGG = 4
XH, XD = 4, 256
FT = 2816 // P

SLOTS = 4
SLOT = 1024
PARAMS_ONE = 16 * 5
PARAMS_TWO = 16 * 12
RESCALE = [float(np.exp(np.float32(np.log(np.float32(1 - 2.0 ** (-5 - i)))) * np.float32(P))) for i in range(RH)]


def constants():
    f = np.float32
    t = np.arange(T)
    tile = lambda a: np.ascontiguousarray(a.reshape(TT, P, -1).transpose(1, 0, 2)).reshape(P, -1)
    i, j = np.arange(P)[:, None], np.arange(P)[None, :]
    one = {}
    one["ident"] = np.eye(P, dtype=f)
    one["causal"] = np.where(j > i, NEG, 0).astype(f)
    inv = f(500000.0) ** (-np.arange(0, 16, 2, dtype=f) / f(16))
    ang = t[:, None].astype(f) * inv[None, :]
    one["cos"], one["sin"] = tile(np.cos(ang).astype(f)), tile(np.sin(ang).astype(f))
    seen = (np.arange(NCMP)[None, :] * 16 + 31) <= t[:, None]
    one["cbias"] = tile(np.where(seen, 0, NEG).astype(f))
    two = {}
    inv = f(10000.0) ** (-np.arange(32, dtype=f) / f(32))
    ang = t[:, None].astype(f) * inv[None, :]
    two["rcos"], two["rsin"] = tile(np.cos(ang).astype(f)), tile(np.sin(ang).astype(f))
    lg = np.log((1.0 - np.exp2(-5.0 - np.arange(RH))).astype(f))
    c = np.arange(P, dtype=f)
    dec = np.where(j >= i, np.exp(lg[:, None, None] * np.maximum(j - i, 0).astype(f)), 0) * f(RK ** -0.5)
    two["decay"] = dec.transpose(1, 0, 2).reshape(P, -1).astype(f)
    two["zeta"] = (np.exp(lg[None, :] * (P - 1 - c)[:, None]) * f(RK ** -0.5)).astype(f)
    xi = np.exp(lg[:, None] * (c + 1)[None, :]).astype(f)
    two["xi"] = np.repeat(xi.reshape(2, 2, 1, P), RK, axis=2).reshape(2, P, P).transpose(1, 0, 2).reshape(P, -1)
    two["tril"] = (j <= i).astype(f)
    masks = np.zeros((P, LEVELS + 1, P), f)
    for lv in range(LEVELS):
        m = 64 >> lv
        masks[:, lv, :] = (i // (2 * m) == j // (2 * m)) & (i // m % 2 == 0) & (j // m % 2 == 1)
    masks[:, LEVELS, :] = i == j
    return one, two, masks.reshape(P, -1)


def fm_chunks(w, c0, tiles):
    return [(w, 0, KD, c0 + P * i, P) for i in range(tiles)]


def tm_chunks(w, c0, cols, tiles=KD, step=2, k0=0):
    return [(w, k, min(step, k0 + tiles - k), c0, cols) for k in range(k0, k0 + tiles, step)]


class Signal:

    def __init__(self, sem, before, per):
        self.sem, self.before, self.per = sem, before, per
        self.made = self.seen = 0

    def up(self):
        self.made += 1
        return self.sem, 1

    def at(self, l, n):
        return self.sem, l * self.per + (self.before + n)

    def next(self, l):
        self.seen += 1
        return self.at(l, self.seen)

    def last(self, l):
        return self.at(l, self.made)


class Groups:

    def __init__(self, steps, groups_of, banks, filled, emptied):
        self.place, used, turn = {}, [0] * 8, {}
        for step in steps:
            for name, choice in groups_of(step):
                n = turn.get(choice, 0)
                turn[choice] = n + 1
                b = choice[n % len(choice)]
                self.place[name] = (b, used[b])
                used[b] += 1
        self.banks, self.f, self.e = banks, filled, emptied

    def ps(self, name):
        return self.banks[self.place[name][0]]

    def free(self, name, l):
        b, n = self.place[name]
        return self.e[b].at(l, n)

    def full(self, name):
        return self.f[self.place[name][0]].up()

    def filled(self, name, l):
        b, n = self.place[name]
        return self.f[b].at(l, n + 1)

    def empty(self, name):
        return self.e[self.place[name][0]].up()

    def evacuated(self, name, l):
        b, n = self.place[name]
        return self.e[b].at(l, n + 1)


ALL, LOW, HIGH = tuple(range(8)), (0, 1, 2, 3), (4, 5, 6, 7)


def merged_in(main, side, first):
    out, n = list(main[:first]), len(main) - first
    done = 0
    for i, step in enumerate(main[first:]):
        out.append(step)
        upto = -(-len(side) * (i + 1) // n)
        out += side[done:upto]
        done = upto
    return out


def fm(kind, w, c0, tiles):
    return [("fm", kind, i, s) for i, s in enumerate(fm_chunks(w, c0, tiles))]


def tm(kind, *a, **k):
    specs = tm_chunks(*a, **k)
    return [("tm", kind, i, len(specs), s) for i, s in enumerate(specs)]


HEADS = [TT // (qt + 1) for qt in range(TT)]
UNITS = [(qt, br, h) for qt in range(TT) for br in range(2) for h in range(0, NH, HEADS[qt])]


def ahead(i):
    first = [("s", 0), ("s", 1), ("p", 0)] if i == 0 else []
    return [(part, *UNITS[j]) for part, j in first + [("s", i + 2), ("p", i + 1)] if j < len(UNITS)]


def steps_one():
    main = (tm("v", "w_in", 1024, 512) + tm("go", "w_in", 1536, 512) + tm("z", "w_in", 2048, 512)
            + tm("nq", "w_in", 2560, 512)
            + tm("ks", "w_in", 3328, 256) + tm("kw", "w_in", 3584, 280))
    side = []
    for h in range(HG):
        side += [("hg_prep", h)]
        for lv in range(LEVELS + 1):
            side += [("hg_level", h, lv)] + ([("z_gate", lv // 2)] if h == HG - 2 and lv % 2 else [])
        side += [("hg_kv", h), ("hg_out", h)]
    s = [("sums", "mix"), ("norm", "mix")] + fm("hq", "w_in", 0, HG) + fm("hf", "w_in", 512, HG) + merged_in(main, side, 4) + tm("kc", "w_in", 3072, 256, step=4)
    nz = tm("nz", "w_in", 3864, 512)
    hid = [[("c_hid", w, i, (f"cmp_w1_{w}", 8 * i, 8, 0, P)) for i in range(2)] for w in range(2)]
    s += nz[:1] + [("q_norm",)] + nz[1:2] + [("k_norm",), ("c_in", 0)] + nz[2:3] + hid[0] + [("c_in", 1)] + nz[3:] + hid[1]
    s += [("hg_turn", h) for h in range(HG)]
    s += [("c_out",), ("q_rope",), ("nz_gate", 0), ("c_key",), ("p_turn",), ("nz_gate", 1)]
    s += [("c_score", 0), ("c_turn", 0)]
    for i, (qt, br, h) in enumerate(UNITS):
        s += [("att", i)]
        units = 2 * NH // HEADS[qt]
        n = (br * NH + h) // HEADS[qt]
        if n < 3 and qt:
            s += [("att_y", qt - 1, 1 + n)]
        if n == units // 4:
            s += [("c_val", qt)]
        if n == 3 and qt:
            s += [("att_turn", qt - 1)]
        if n == units // 4 and qt + 2 < TT:
            s += [("nz_gate", qt + 2)]
        if n == units * 5 // 16 and qt + 1 < TT:
            s += [("c_score", qt + 1)]
        if n == units * 11 // 16 and qt + 1 < TT:
            s += [("c_turn", qt + 1)]
        if n == units - 1:
            s += [("att_y", qt, 0)]
    s += [("att_y", TT - 1, i) for i in (1, 2, 3)] + [("att_turn", TT - 1)]
    for n in range(2):
        s += tm(f"out{n}", "w_out", 512 * n, 512)
    s += [("sums", "ple")]
    for n in range(2):
        s += tm(f"pp{n}", "w_pp", 512 * n, 512, tiles=2)
    s += [("norm", "ple")]
    for n in range(2):
        s += tm(f"pg{n}", "w_pg", 512 * n, 512)
    return s


def followed(steps):
    out = list(steps)
    for i, (step, after) in enumerate(zip(steps, steps[1:])):
        if step[0] == "tm" and step[2] == step[3] - 1 and after[0] in ("hg_level", "hg_prep"):
            out[i:i + 2] = after, step
    return out


def groups_one(step):
    kind = step[0]
    if kind == "norm":
        return [((step[1], k), HIGH + LOW) for k in range(KD)]
    if kind == "fm":
        return [((step[1], step[2]), HIGH)]
    if kind == "tm":
        high = 4 * (step[1] in ("out0", "pp0", "pg0"))
        return [((step[1], tt), (high + tt,)) for tt in range(TT)] if step[2] == 0 else []
    if kind == "hg_prep":
        return [(("kd", step[1]), HIGH)]
    if kind == "hg_level":
        return [(("A", step[1], step[2]), HIGH)]
    if kind == "hg_kv":
        return [(("kv", step[1]), HIGH)]
    if kind == "hg_out":
        return [(("o", step[1]), HIGH)]
    if kind == "hg_turn":
        return [(("yT", step[1]), HIGH)]
    if kind == "p_turn":
        return [(("pT", k), HIGH) for k in range(PLE // P)]
    if kind == "q_norm":
        return [(("qn", n), HIGH) for n in range(NG)]
    if kind == "q_rope":
        return [(("qr", n), HIGH) for n in range(NG)]
    if kind == "k_norm":
        return [(("kT", br), HIGH) for br in range(2)]
    if kind == "c_in":
        return ([(("pe",), HIGH)] if step[1] == 0 else []) + [(("ct", step[1], g), HIGH) for g in range(NKV)]
    if kind == "c_hid":
        return [(("ch", step[1]), HIGH)] if step[2] == 0 else []
    if kind == "c_out":
        return [(("co",), HIGH)]
    if kind == "c_key":
        return [(("ck",), HIGH)]
    if kind == "c_score":
        return [(("cs", step[1], g), (3 + g,)) for g in range(NKV)]
    if kind == "c_turn":
        return [(("cp", step[1], i), (3 + i,)) for i in range(2)]
    if kind == "c_val":
        return [(("o_c", step[1]), (7,))]
    if kind == "att":
        i = step[1]
        qt, br, h = UNITS[i]
        return ([(part, (0, 1, 2) if part[0] == "s" else (3, 4)) for part in ahead(i)] + ([(("o_a", qt, br), (5 + br,))] if h == 0 else []))
    if kind == "att_turn":
        return [(("nT", step[1]), (0, 1, 2))]
    return []


def numbered(steps):
    chunks = [s for s in steps if isinstance(s[-1], tuple) and len(s[-1]) == 5]
    return {s: j for j, s in enumerate(chunks)}, [s[-1] for s in chunks]


HALVES = ((0, 12), (12, FT))


def steps_two():
    s = [("sums", "mix"), ("norm", "mix")] + fm("ax", "w_in_2", 0, 2) + tm("g", "w_in_2", 1792, 512) + tm("qk", "w_in_2", 768, 512) + tm("v", "w_in_2", 1280, 512)
    conv = fm("ac", "w_in_2", 256, 2) + fm("ab", "w_in_2", 512, 2)
    ret = []
    for p in range(RH // 2):
        ret += [("ret_pair", p)]
        for hh in (2 * p, 2 * p + 1):
            ret += [("ret_in", hh), ("ret_out", hh)]
    s += merged_in(conv + tm("z", "w_in_2", 2304, 512)[:3], ret + [("ret_turn", hh) for hh in range(RH)], 0)
    s += tm("z", "w_in_2", 2304, 512)[3:]
    width = {"a": 2, "b": 4, "c": 2}

    def branch(b, n):
        col = 2816 + D * "abc".index(b) + 512 * n
        return tm(f"g{b}{n}", "w_in_2", col, 512) + tm(f"y{b}{n}", f"w_{b}_out_2", 512 * n, 512, tiles=width[b])

    s += merged_in(branch("a", 0) + branch("a", 1), [("sg_w",), ("sg_norm",), ("sg_mix",), ("sg_turn",)], 5)
    for b in "bc":
        s += branch(b, 0) + branch(b, 1)
    wo0, wo1, xk, xv0 = tm("wo0", "w_o_2", 0, 512), tm("wo1", "w_o_2", 512, 512), fm("xk", "xa_k_2", 0, KD), tm("xv0", "xa_v_2", 0, 512)
    s += [("mg_turn",)] + wo0[:3] + [("mem",)] + wo0[3:]
    s += wo1[:1] + xk[:2] + wo1[1:2] + xk[2:4] + wo1[2:3] + xk[4:5] + wo1[3:] + [("sums", "xa")] + xk[5:]
    xv1 = tm("xv1", "xa_v_2", 512, 512)
    xq = fm("xq", "xa_q_2", 0, KD)
    s += [("norm", "xa")]
    for i in range(4):
        s += xq[i:i + 1] + xv0[i:i + 1]
    for hh in range(XH):
        for qt in range(TT):
            s += [("xatt", hh, qt)] + (xv1[qt:qt + 1] if hh == 0 else [])
            s += xq[2 + 2 * hh + qt:3 + 2 * hh + qt] if qt >= 2 else []
        s += [("xout", hh)]
    for n in range(2):
        s += tm(f"xw{n}", "xa_o_2", 512 * n, 512)
    s += [("sums", "ffn"), ("norm", "ffn")]
    for i, (a, b) in enumerate(HALVES):
        for f in range(a, b):
            s += [("fm", "u", f, ("w1_2", 0, KD, f * P, P)), ("fm", "w", f, ("w3_2", 0, KD, f * P, P))]
        for n in range(2):
            s += tm(f"d{i}{n}", "w2_2", 512 * n, 512, tiles=b - a, k0=a)
    return s


def groups_two(step):
    kind = step[0]
    if kind == "norm":
        return [((step[1], k), HIGH + LOW) for k in range(KD)]
    if kind == "fm":
        return [((step[1], step[2]), (5, 6) if step[1] == "xq" else HIGH)]
    if step[:2] == ("tm", "xv1"):
        return [((step[1], tt), ((2, 7)[tt],)) for tt in range(MT)] if step[2] == 0 else []
    if kind == "tm":
        high = 4 * (step[1] in ("qk", "wo0", "xw0", "d01", "d10") or step[1] in ("gb0", "gb1", "gc0", "gc1")) 
        return [((step[1], tt), (high + tt,)) for tt in range(MT if step[1][:2] == "xv" else TT)] if step[2] == 0 else []
    if kind == "ret_pair":
        return [(("qP", step[1]), HIGH), (("kP", step[1]), HIGH)]
    if kind == "ret_in":
        return [(("rs", step[1]), HIGH), (("rk", step[1]), HIGH)]
    if kind == "ret_out":
        return [(("ro", step[1]), HIGH)]
    if kind == "ret_turn":
        return [(("ybT", step[1]), HIGH)]
    if kind == "sg_w":
        return [(("ws",), HIGH)]
    if kind == "sg_mix":
        return [(("vm", tt), HIGH) for tt in range(TT)]
    if kind == "sg_turn":
        return [(("ycT", k), HIGH) for k in range(2)]
    if kind == "mg_turn":
        return [(("mT", tt, i), HIGH + LOW) for tt in range(TT) for i in range(2)]
    if kind == "mem":
        return [(("mm", k), LOW) for k in range(KD)]
    if kind == "xatt":
        hh, qt = step[1:]
        return [(("xs", hh, qt), (0, 1)), (("xp", hh, qt), (3, 4))]
    if kind == "xout":
        return [(("xo", step[1], i), (5, 6)) for i in range(2)]
    return []


def build(nc, d, out, counts):
    made = []

    with ExitStack() as ctx:
        def sb(name, shape, dt=F32, where=ctx):
            return where.enter_context(nc.sbuf_tensor(name, shape, dt))

        def sem(name):
            return ctx.enter_context(nc.semaphore(name))

        raw = sb("raw", [P, SLOTS, SLOT])
        whi = sb("whi", [P, SLOTS, SLOT], F32R)
        wlo = sb("wlo", [P, SLOTS, SLOT], F32R)
        h = sb("h", [P, TT, D])
        xhi = sb("xhi", [P, KD, T], F32R)
        xlo = sb("xlo", [P, KD, T], F32R)
        ident = sb("ident", [P, P])
        eps = sb("eps", [P, 1])
        ones = sb("ones", [P, 1])
        all_gains1 = sb("all_gains1", [P, DEPTH, 2, KD])
        all_gains2 = sb("all_gains2", [P, DEPTH, 4, KD])
        zero = sb("zero", [P, 1])
        ss = sb("ss", [P, TT])
        rstd = sb("rstd", [P, TT])
        lnv = sb("lnv", [P, 32])
        et = sb("et", [P, 2, T])
        sq = sb("sq", [P, 2, T])
        tA, tB, tC, tD = (sb(f"t{c}", [P, T]) for c in "ABCD")
        diag = tD[:, :].rearrange("p (t q) -> p t q", t=TT)
        banks = [ctx.enter_context(nc.psum_tensor(f"bank{b}", [P, 512], F32)) for b in range(8)]

        one = ExitStack()
        k1 = {n: sb("k1_" + n, [P, w], where=one) for n, w in d["w1"].items() if n not in ("ident", "causal")}
        identb = sb("identb", [P, P], BF16, one)
        causal = sb("causal", [P, P], BF16, one)
        masks = sb("masks", [P, LEVELS + 1, P], U8, one)
        lbraw = sb("lbraw", [P, 2, HG], where=one)
        lbt = sb("lbt", [P, DEPTH, 3, HG], where=one)
        lbs = sb("lbs", [P, 6, HG], where=one)
        lbc = sb("lbc", [P, 3, HG], where=one)
        gains1 = sb("gains1", [P, 2, KD], where=one)
        gmix, gple = gains1[:, 0, :], gains1[:, 1, :]
        onorm = sb("onorm", [P, P], where=one)
        qg = sb("qg", [P, DH], where=one)
        kg = sb("kg", [P, 3, DH], where=one)
        w2 = sb("w2", [P, 2, DH], where=one)
        pe_raw = sb("pe_raw", [P, P], where=one)
        qT = sb("qT", [P, HG, T], where=one)
        dE = sb("dE", [P, 2, T], where=one)
        Ql = sb("Ql", [P, 2, T], where=one)
        Kl = sb("Kl", [P, 2, T], where=one)
        At = sb("At", [P, 2, TT, P], where=one)
        decays = sb("decays", [P, 4, T], where=one)
        eB, kdx, qdec, kdec = (decays[:, i, :] for i in range(4))
        kdt = tC[:, :].rearrange("p (c d) -> p c d", c=TT)
        ebl = sb("ebl", [P, TT], where=one)
        S = tB[:, 0:(TT - 1) * P].rearrange("p (c d) -> p c d", c=TT - 1)
        ssh = sb("ssh", [P, TT], where=one)
        rsh = sb("rsh", [P, TT], where=one)
        kk = sb("kk", [P, TT, 2, P], where=one)
        vv = sb("vv", [P, TT, 2, P], where=one)
        nzs = sb("nzs", [P, TT, T], where=one)
        gts = sb("gts", [P, TT, 3, NH], where=one)
        ssq = sb("ssq", [P, TT, NH], where=one)
        rsq = sb("rsq", [P, TT, NH], where=one)
        ssk = sb("ssk", [P, 16], where=one)
        rsk = sb("rsk", [P, 16], where=one)
        peT = sb("peT", [P, 2, 16], where=one)
        ssc = sb("ssc", [32, 2], where=one)
        rsc = sb("rsc", [32, 2], where=one)
        mx = sb("mx", [P, NH], where=one)
        nm = sb("nm", [P, 4, HEADS[0]], where=one)
        sums = sb("sums", [P, 2, 3, NH], where=one)
        coef = sb("coef", [P, 3, NH], where=one)
        qTn = qT
        cin = dE[:, :, :].rearrange("p a t -> p (a t)")[:, 0:16 * 2 * NCMP].rearrange("p (j g c) -> p j g c", j=16, g=2)
        cs = eB[:, 0:NH * NCMP].rearrange("p (h c) -> p h c", h=NH)
        ce = kdx[:, 0:NH * NCMP].rearrange("p (h c) -> p h c", h=NH)
        pcT = Kl[0:32, :, :].rearrange("p a (b q) -> p (a b) q", q=P)
        hid = Ql[:, 0, 0:4 * NCMP].rearrange("p (w c) -> p w c", w=2)
        kcn = Ql[:, 1, 0:P].rearrange("p (g d) -> p g d", g=NKV)
        vc = eB[0:32, 256:256 + P].rearrange("p (g d) -> p g d", g=NKV)
        kcT = eB[:, 384:416]
        kvc = decays[:, :, :].rearrange("p i (w a d) -> p i w a d", a=2, d=DH)
        p_raw = kk[:, :, :, :].rearrange("p t b c -> p t (b c)")
        Pb, Pt, y = dE, Ql, qdec
        with ExitStack() as early:
            bT = sb("bT", [P, HG, T], where=early)
            kT = sb("kT", [P, HG, T], where=early)
            ghg = sb("ghg", [P, TT, T], where=early)
            v = sb("v", [P, TT, T], where=early)
            q = sb("q", [P, TT, NG, NKV, DH], where=early)
        kTn = sb("kTn", [P, 2, 2, T], F32R, one)
        qTr = sb("qTr", [P, 2, NG, T], F32R, one)
        chi, clo = (sb(n, [P, 16, 2, NCMP], F32R, one) for n in ("chi", "clo"))
        sb("beside_q", [P, 64], where=one)
        pT = sb("pT", [P, 2, 2, T], F32R, one)
        one.close()

        two = ExitStack()
        k2 = {n: sb("k2_" + n, [P, w], where=two) for n, w in d["w2"].items()}
        gains2 = sb("gains2", [P, 4, KD], where=two)
        gmix2, gxa, gmem, gffn = (gains2[:, i, :] for i in range(4))
        convw = sb("convw", [P, 2, 3], where=two)
        sgb = sb("sgb", [P, SGG], where=two)
        ssm = sb("ssm", [P, 8], where=two)
        rsm = sb("rsm", [P, 8], where=two)
        mux = sb("mux", [P, TT], where=two)
        ssv = sb("ssv", [P, TT], where=two)
        rsv = sb("rsv", [P, TT], where=two)
        nmx = sb("nmx", [P, 4], where=two)
        sumx = sb("sumx", [P, 4], where=two)
        recx = sb("recx", [P, 4], where=two)
        mix = ExitStack()
        yaT = sb("yaT", [P, 2, 2, T], F32R, mix)
        ybT = sb("ybT", [P, 2, RH, T], F32R, mix)
        ycT = sb("ycT", [P, 2, 2, T], F32R, mix)
        mg = sb("mg", [P, TT, D], where=mix)
        qkr = mg[:, 0:2, :].rearrange("p a (b h d) -> p (a b) h d", b=2, d=RK)
        v2 = mg[:, 2:4, :].rearrange("p a (b n) -> p (a b) n", b=2)
        gg = sb("gg", [P, TT, T], where=mix)
        qp, kp, qx = (sb(n, [P, T], where=mix) for n in ("qp", "kp", "qx"))
        ds = sb("ds", [P, T], where=mix)
        R = sb("R", [P, TT - 1, P], where=mix)
        wsT = sb("wsT", [P, SGG, P], where=mix)
        sgw = sb("sgw", [P, SGG, P], where=mix)
        cx = sb("cx", [P, 2, T], where=mix)
        zp = sb("zp", [P, 2, T + 2], where=mix)
        retgn = sb("retgn", [P, T], where=mix)
        sgln = sb("sgln", [P, 256], where=mix)
        mix.close()
        xat = ExitStack()
        mmT = sb("mmT", [P, 2, KD, MEM], F32R, xat)
        xoT = mmT[:, :, :, :].rearrange("p a (k b) m -> p a k (b m)", b=2)
        qx8 = sb("qx8", [P, 2, 4, T], F32R, xat)
        kx8 = sb("kx8", [P, 2, KD, MEM], F32R, xat)
        vx = sb("vx", [P, 2, MT, D], F32R, xat)
        Px = sb("Px", [P, 2, MEM], where=xat)
        with ExitStack() as early:
            mem = sb("mem", [P, MT, D], where=early)
        PxT = sb("PxT", [P, 2, 2, MT, T], F32R, xat)
        xat.close()
        ffn = ExitStack()
        gT = sb("gT", [P, 2, HALVES[0][1], T], F32R, ffn)
        gfin = sb("gfin", [P, D], where=ffn)
        ffn.close()
        two.close()

        def signal(name, credit=0):
            s = sem(name)
            per = [counts.get((name, st), 0) for st in (1, 2)]
            pair = [Signal(s, credit, per[0]), Signal(s, credit + DEPTH * per[0], per[1])]
            for st, one_ in enumerate(pair):
                made.append((name, st + 1, one_))
            return pair

        f_pairs = [signal(f"filled{b}") for b in range(8)]
        e_pairs = [signal(f"emptied{b}", 1) for b in range(8)]
        steps1, steps2 = steps_one(), steps_two()
        G1 = Groups(steps1, groups_one, banks, [x[0] for x in f_pairs], [x[0] for x in e_pairs])
        G2 = Groups(steps2, groups_two, banks, [x[1] for x in f_pairs], [x[1] for x in e_pairs])
        number1, chunks1 = numbered(steps1)
        number2, chunks2 = numbered(steps2)
        N1, N2 = len(chunks1), len(chunks2)
        assert N1 % SLOTS == 0 and N2 % SLOTS == 0, (N1, N2)

        raw_loaded = [sem(f"raw_loaded{i}") for i in range(SLOTS)]
        hi_split = sem("hi_split")
        lo_split = sem("lo_split")
        chunk_begun = sem("chunk_begun")
        zero_ready = sem("zero_ready")
        setup = sem("setup")
        h_loaded = [sem(f"h_loaded{i}") for i in range(TT)]
        made_ready = sem("made_ready")
        params = [sem("params1"), sem("params2")]

        class Ring:

            def __init__(self, base, n):
                self.base, self.n = base, n

            def loaded(self, l, j):
                return raw_loaded[j % SLOTS], l * (16 * self.n // SLOTS) + 16 * ((self.base + j) // SLOTS + 1)

            def parts_free(self, l, j):
                return chunk_begun, l * self.n + (self.base + j + 1)

            def hi(self, l, j):
                return hi_split, l * self.n + (self.base + j + 1)

            def raw_free(self, l, j):
                return lo_split, l * self.n + (self.base + j + 1)

            def split(self, l, j):
                return lo_split, l * self.n + (self.base + j + 1 + SLOTS)

        ring1, ring2 = Ring(0, N1), Ring(DEPTH * N1, N2)

        dve_step, act_step = signal("dve_step"), signal("act_step")
        hi_done = signal("hi_done")
        exp_done = signal("exp_done")
        et_read = signal("et_read")
        sq_done = signal("sq_done")
        ss_done = signal("ss_done")
        rs_done = signal("rs_done")
        diag_ready = signal("diag_ready")
        fg_b, fg_c, fg_d = (signal(f"forget_{c}")[0] for c in "bcd")
        b_ready = signal("b_ready")[0]
        go_ready = signal("go_ready")[0]
        d_ready, e_ready, qk_ready = signal("d_ready")[0], signal("e_ready")[0], signal("qk_ready")[0]
        prep_exp, prep_done = signal("prep_exp")[0], signal("prep_done")[0]
        q_ready, k_ready, qr_ready, kc_ready = (signal(n)[0] for n in ("q_ready", "k_ready", "qr_ready", "kc_ready"))
        cin_ready, clo_ready = signal("cin_ready")[0], signal("clo_ready")[0]
        cs_ready, ce_done, cp_ready = (signal(n)[0] for n in ("cs_ready", "ce_done", "cp_ready"))
        nm_ready = signal("nm_ready")
        y_ready = signal("y_ready")
        sg_ready, rot_ready, qx_ready, yb_ready, sgw_ready = (signal(n)[1] for n in ("sg_ready", "rot_ready", "qx_ready", "yb_ready", "sgw_ready"))
        ya_ready, g_ready, mg_ready, px_ready = (signal(n)[1] for n in ("ya_ready", "g_ready", "mg_ready", "px_ready"))
        p_loaded = sem("p_loaded")
        mem_loaded = sem("mem_loaded")
        setup_step, act_setup = sem("setup_step"), sem("act_setup")
        gain_loaded = sem("gain_loaded")
        fin_step, fin_root, fin_done = sem("fin_step"), sem("fin_root"), sem("fin_done")
        out_done = sem("out_done")

        def tensor_one(pe, l):
            G, ring = G1, ring1

            def chunk(step):
                pe.wait_ge(*ring.split(l, number1[step]))
                return number1[step] % SLOTS

            def turn(name, tiles, src, m=P):
                pe.wait_ge(*G.free(name, l))
                for i in range(tiles):
                    mm = pe.transpose(G.ps(name)[:, i * P:i * P + m], src(i), ident[0:m, 0:m])
                mm.then_inc(*G.full(name))

            def product(step, names, rows, k_of):
                _, kind, i, n, (_, k0, nk, _, cols) = step
                if kind == "pg1":
                    if i == n - 1:
                        by_tiles(step, names, rows)
                    return
                s = chunk(step)
                for tt in range(TT):
                    if i == 0:
                        pe.wait_ge(*G.free(names[tt], l))
                    for kk_ in range(nk):
                        a, b = rows[0][:, k_of(k0 + kk_), tt * P:(tt + 1) * P], rows[1][:, k_of(k0 + kk_), tt * P:(tt + 1) * P]
                        wh, wl = whi[:, s, kk_ * cols:(kk_ + 1) * cols], wlo[:, s, kk_ * cols:(kk_ + 1) * cols]
                        o = G.ps(names[tt])[:, 0:cols]
                        mm = pe.matmul(o, a, wh, start=(i == 0 and kk_ == 0), stop=False)
                        if tt == 0 and kk_ == 0:
                            mm.then_inc(chunk_begun, 1)
                        pe.matmul(o, a, wl, start=False, stop=False)
                        mm = pe.matmul(o, b, wh, start=False, stop=(i == n - 1 and kk_ == nk - 1))
                    if i == n - 1:
                        mm.then_inc(*G.full(names[tt]))

            def by_tiles(step, names, rows):
                _, _, _, n, (_, _, nk, _, cols) = step
                first = number1[step] - (n - 1)
                for tt in range(TT):
                    o, at = G.ps(names[tt])[:, 0:cols], slice(tt * P, (tt + 1) * P)
                    pe.wait_ge(*G.free(names[tt], l))
                    for i in range(n):
                        s = (first + i) % SLOTS
                        if tt == 0:
                            pe.wait_ge(*ring.split(l, first + i))
                        for kk_ in range(nk):
                            k = i * nk + kk_
                            wh, wl = whi[:, s, kk_ * cols:(kk_ + 1) * cols], wlo[:, s, kk_ * cols:(kk_ + 1) * cols]
                            mm = pe.matmul(o, rows[0][:, k, at], wh, start=(k == 0), stop=False)
                            if tt == (TT - 1 if i else 0) and kk_ == 0:
                                mm.then_inc(chunk_begun, 1)
                            pe.matmul(o, rows[0][:, k, at], wl, start=False, stop=False)
                            mm = pe.matmul(o, rows[1][:, k, at], wh, start=False, stop=(k == n * nk - 1))
                    mm.then_inc(*G.full(names[tt]))

            def step_norm(step):
                which = step[1]
                pe.wait_ge(*diag_ready[0].next(l))
                for k in range(KD):
                    pe.wait_ge(*G.free((which, k), l))
                    for tt in range(TT):
                        mm = pe.matmul(G.ps((which, k))[:, tt * P:(tt + 1) * P], h[:, tt, k * P:(k + 1) * P],
                                       diag[:, tt, :], start=True, stop=True)
                    mm.then_inc(*G.full((which, k)))

            def step_fm(step):
                name = step[1:3]
                s = chunk(step)
                pe.wait_ge(*G.free(name, l))
                for k in range(KD):
                    if name == ("hq", 0):
                        pe.wait_ge(*G.evacuated(("mix", k), l))
                    wh, wl = whi[:, s, k * P:(k + 1) * P], wlo[:, s, k * P:(k + 1) * P]
                    mm = pe.matmul(G.ps(name)[:, :], wh, xhi[:, k, :], start=(k == 0), stop=False)
                    if k == 0:
                        mm.then_inc(chunk_begun, 1)
                    pe.matmul(G.ps(name)[:, :], wh, xlo[:, k, :], start=False, stop=False)
                    mm = pe.matmul(G.ps(name)[:, :], wl, xhi[:, k, :], start=False, stop=(k == KD - 1))
                mm.then_inc(*G.full(name))

            def step_tm(step):
                kind, i = step[1], step[2]
                if i == 0 and kind == "out0":
                    pe.wait_ge(*G.evacuated(("nT", TT - 1), l))
                if kind == "pg0":
                    pe.wait_ge(*G.evacuated(("ple", 2 * i + 1), l))
                if kind[:2] == "pp":
                    pe.wait_ge(*G.evacuated(("pT", 1), l))
                    rows = (pT[:, 0], pT[:, 1])
                else:
                    rows = (xhi, xlo)
                product(step, [(kind, tt) for tt in range(TT)], rows, lambda k: k)

            def step_p_turn(step):
                pe.wait_ge(p_loaded, l * 16 + 16)
                for k in range(2):
                    turn(("pT", k), TT, lambda tt: p_raw[:, tt, k * P:(k + 1) * P])

            def step_hg_prep(step):
                pe.wait_ge(*prep_done.at(l, step[1] + 1))
                turn(("kd", step[1]), TT, lambda c: kdec[:, c * P:(c + 1) * P])

            def step_hg_level(step):
                hh, lv = step[1:]
                name = ("A", hh, lv)
                if lv < LEVELS:
                    pe.wait_ge(*qk_ready.at(l, LEVELS * hh + lv + 1))
                    kl, ql = Kl[:, lv % 2], Ql[:, lv % 2]
                else:
                    kl, ql = kT[:, hh], qT[:, hh]
                pe.wait_ge(*G.free(name, l))
                for c in range(TT):
                    mm = pe.matmul(G.ps(name)[:, c * P:(c + 1) * P], kl[:, c * P:(c + 1) * P], ql[:, c * P:(c + 1) * P],
                                   start=True, stop=True)
                mm.then_inc(*G.full(name))

            def step_hg_kv(step):
                hh = step[1]
                name = ("kv", hh)
                if hh == 0:
                    for tt in range(TT):
                        pe.wait_ge(*G.evacuated(("v", tt), l))
                pe.wait_ge(*G.evacuated(("kd", hh), l))
                pe.wait_ge(*G.free(name, l))
                for c in range(TT - 1):
                    mm = pe.matmul(G.ps(name)[:, c * P:(c + 1) * P], kdt[:, c, :], v[:, c, hh * P:(hh + 1) * P],
                                   start=True, stop=True)
                mm.then_inc(*G.full(name))

            def step_hg_out(step):
                hh = step[1]
                name = ("o", hh)
                pe.wait_ge(*G.evacuated(("kv", hh), l))
                for lv in range(LEVELS - 2, LEVELS + 1):
                    pe.wait_ge(*G.evacuated(("A", hh, lv), l))
                pe.wait_ge(*G.free(name, l))
                for c in range(TT):
                    o = G.ps(name)[:, c * P:(c + 1) * P]
                    mm = pe.matmul(o, At[:, hh % 2, c, :], v[:, c, hh * P:(hh + 1) * P], start=True, stop=(c == 0))
                    if c:
                        mm = pe.matmul(o, qdec[:, c * P:(c + 1) * P], S[:, c - 1, :], start=False, stop=True)
                mm.then_inc(*G.full(name))

            def step_hg_turn(step):
                hh = step[1]
                pe.wait_ge(*G.evacuated(("o", hh), l))
                turn(("yT", hh), TT, lambda c: ghg[:, c, hh * P:(hh + 1) * P])

            def step_q_norm(step):
                pe.wait_ge(*q_ready.next(l))
                for n in range(NG):
                    turn(("qn", n), TT, lambda tt: q[:, tt, n].rearrange("p g d -> p (g d)"))

            def step_q_rope(step):
                pe.wait_ge(*qr_ready.next(l))
                for n in range(NG):
                    turn(("qr", n), TT, lambda tt: q[:, tt, n].rearrange("p g d -> p (g d)"))

            def step_k_norm(step):
                pe.wait_ge(*k_ready.next(l))
                for br in range(2):
                    turn(("kT", br), TT, lambda tt: kk[:, tt, br, :])

            def step_c_in(step):
                w = step[1]
                if w == 0:
                    pe.wait_ge(params[0], l * PARAMS_ONE + PARAMS_ONE)
                    pe.wait_ge(*G.evacuated(("kc", TT - 1), l))
                    pe.wait_ge(*G.free(("pe",), l))
                    pe.transpose(G.ps(("pe",))[:, 0:P], pe_raw[:, :], ident[:, :]).then_inc(*G.full(("pe",)))
                for g in range(NKV):
                    turn(("ct", w, g), TT, lambda tt: kvc[:, tt, 2 * w + g].rearrange("p a d -> p (a d)"))

            def step_c_hid(step):
                w, i = step[1], step[2]
                name = ("ch", w)
                s = chunk(step)
                if i == 0:
                    pe.wait_ge(*clo_ready.next(l))
                    pe.wait_ge(*G.free(name, l))
                o = G.ps(name)[:, 0:2 * NCMP]
                for j in range(8):
                    a, b = (x[:, 8 * i + j].rearrange("p g c -> p (g c)") for x in (chi, clo))
                    wh, wl = whi[:, s, j * P:(j + 1) * P], wlo[:, s, j * P:(j + 1) * P]
                    mm = pe.matmul(o, wh, a, start=(i == 0 and j == 0), stop=False)
                    if j == 0:
                        mm.then_inc(chunk_begun, 1)
                    pe.matmul(o, wh, b, start=False, stop=False)
                    mm = pe.matmul(o, wl, a, start=False, stop=(i == 1 and j == 7))
                if i == 1:
                    mm.then_inc(*G.full(name))

            def step_c_out(step):
                for w in range(2):
                    pe.wait_ge(*G.evacuated(("ch", w), l))
                pe.wait_ge(*G.free(("co",), l))
                for w in range(2):
                    for g in range(NKV):
                        mm = pe.matmul(G.ps(("co",))[0:NCMP, (2 * w + g) * DH:(2 * w + g + 1) * DH],
                                       hid[:, w, g * NCMP:(g + 1) * NCMP], w2[:, w, :], start=True, stop=True)
                mm.then_inc(*G.full(("co",)))

            def step_c_key(step):
                pe.wait_ge(*kc_ready.next(l))
                pe.wait_ge(*G.free(("ck",), l))
                pe.transpose(G.ps(("ck",))[:, 0:P], kcn.rearrange("p g d -> p (g d)"), ident[:, :]).then_inc(*G.full(("ck",)))

            def step_c_score(step):
                qt = step[1]
                if qt == 0:
                    pe.wait_ge(*G.evacuated(("ck",), l))
                for g in range(NKV):
                    name = ("cs", qt, g)
                    pe.wait_ge(*G.free(name, l))
                    for n in range(NG):
                        mm = pe.matmul(G.ps(name)[:, n * 32:n * 32 + NCMP], qTn[g * DH:(g + 1) * DH, n, qt * P:(qt + 1) * P],
                                       kcT[g * DH:(g + 1) * DH, 0:NCMP], start=True, stop=True)
                    mm.then_inc(*G.full(name))

            def step_c_turn(step):
                qt = step[1]
                pe.wait_ge(*cp_ready.next(l))
                for i in range(2):
                    name = ("cp", qt, i)
                    pe.wait_ge(*G.free(name, l))
                    for n in range(4):
                        mm = pe.transpose(G.ps(name)[0:NCMP, n * P:(n + 1) * P], ce[:, 4 * i + n, :], ident[:, :])
                    mm.then_inc(*G.full(name))

            def step_c_val(step):
                qt = step[1]
                name = ("o_c", qt)
                pe.wait_ge(*G.free(name, l))
                for i in range(2):
                    pe.wait_ge(*G.evacuated(("cp", qt, i), l))
                for hh in range(NH):
                    mm = pe.matmul(G.ps(name)[:, hh * DH:(hh + 1) * DH], pcT[0:NCMP, hh, :], vc[0:NCMP, hh // NG, :],
                                   start=True, stop=True)
                mm.then_inc(*G.full(name))

            def scores(qt, br, h0):
                name, n = ("s", qt, br, h0), (qt + 1) * P
                pe.wait_ge(*G.free(name, l))
                for w in range(HEADS[qt]):
                    g, m = divmod(h0 + w, NG)
                    o = G.ps(name)[:, w * n:(w + 1) * n]
                    for i, j in ((0, 0), (0, 1), (1, 0)):
                        pe.matmul(o, qTr[g * DH:(g + 1) * DH, i, m, qt * P:(qt + 1) * P],
                                  kTn[g * DH:(g + 1) * DH, j, br, 0:n], start=(i == 0 and j == 0), stop=False)
                    mm = pe.matmul(o[:, qt * P:n], identb[:, :], causal[:, :], start=False, stop=True)
                mm.then_inc(*G.full(name))

            def probs_turn(qt, br, h0):
                name, place = ("p", qt, br, h0), UNITS.index((qt, br, h0)) % 2
                pe.wait_ge(*G.evacuated(("s", qt, br, h0), l))
                pe.wait_ge(*G.free(name, l))
                for i in range(HEADS[qt] * (qt + 1)):
                    mm = pe.transpose(G.ps(name)[:, i * P:(i + 1) * P], Pb[:, place, i * P:(i + 1) * P], ident[:, :])
                mm.then_inc(*G.full(name))

            def values(qt, br, h0):
                name, place = ("o_a", qt, br), UNITS.index((qt, br, h0)) % 2
                pe.wait_ge(*G.evacuated(("p", qt, br, h0), l))
                if h0 == 0:
                    pe.wait_ge(*G.free(name, l))
                for w in range(HEADS[qt]):
                    hh = h0 + w
                    g = hh // NG
                    for kt in range(qt + 1):
                        at = (w * (qt + 1) + kt) * P
                        mm = pe.matmul(G.ps(name)[:, hh * DH:(hh + 1) * DH], Pt[:, place, at:at + P],
                                       vv[:, kt, br, g * DH:(g + 1) * DH], start=(kt == 0), stop=(kt == qt))
                if hh == NH - 1:
                    mm.then_inc(*G.full(name))

            def step_att(step):
                i = step[1]
                if i == 0:
                    pe.wait_ge(*G.evacuated(("qr", NG - 1), l))
                for part, *unit in ahead(i):
                    if part == "s":
                        scores(*unit)
                    else:
                        probs_turn(*unit)
                values(*UNITS[i])

            def step_att_turn(step):
                pe.wait_ge(*y_ready[0].next(l))
                turn(("nT", step[1]), 4, lambda f: y[:, f * P:(f + 1) * P])

            table = {"norm": step_norm, "fm": step_fm, "tm": step_tm, "p_turn": step_p_turn, "hg_prep": step_hg_prep,
                     "hg_level": step_hg_level, "hg_kv": step_hg_kv, "hg_out": step_hg_out, "hg_turn": step_hg_turn,
                     "q_norm": step_q_norm, "q_rope": step_q_rope, "k_norm": step_k_norm, "c_in": step_c_in,
                     "c_hid": step_c_hid, "c_out": step_c_out, "c_key": step_c_key, "c_score": step_c_score, "c_turn": step_c_turn, "c_val": step_c_val,
                     "att": step_att, "att_turn": step_att_turn}
            for step in steps1:
                if step[0] in table:
                    table[step[0]](step)

        def scalar_one(act, l):
            G = G1
            eu = [None, None]
            n_read = [0]
            n_et = [0]
            n_sq = [0]
            sigs = dict(act_step=act_step[0], hi=hi_done[0], ex=exp_done[0], sq=sq_done[0], ss=ss_done[0], rs=rs_done[0])

            def link(ins):
                ins.then_inc(*sigs["act_step"].up())
                act.wait_ge(*sigs["act_step"].last(l))

            def one_over(x):
                act.wait_ge(*sigs["act_step"].last(l))
                link(nc.scalar.activation(x, x, ACT.Ln, bias=1.0))
                return nc.scalar.activation(x, x, ACT.Exp, scale=-1.0)

            def gate(name, cols=T, src=None):
                i = n_et[0] % 2
                n_et[0] += 1
                if eu[i]:
                    act.wait_ge(*eu[i])
                if src is None:
                    eu[i] = G.evacuated(name, l)
                    act.wait_ge(*G.filled(name, l))
                    src = G.ps(name)[:, 0:cols]
                else:
                    n_read[0] += 1
                    eu[i] = et_read[0].at(l, n_read[0])
                    act.wait_ge(*G.evacuated(name, l))
                nc.scalar.activation(et[:, i, 0:cols], src, ACT.Exp, scale=-1.0).then_inc(*sigs["act_step"].up())
                one_over(et[:, i, 0:cols]).then_inc(*sigs["ex"].up())

            def square_place():
                i = n_sq[0]
                n_sq[0] += 1
                if i >= 2:
                    act.wait_ge(*sigs["ss"].at(l, i - 1))
                return sq[:, i % 2, :]

            def root(dst, src, count, cols, sums_made):
                if sums_made:
                    act.wait_ge(*sigs["ss"].at(l, sums_made))
                if sigs["rs"].made:
                    act.wait_ge(*sigs["rs"].last(l))
                rows = src.shape[0]
                link(nc.scalar.activation(lnv[0:rows, 0:cols], src, ACT.Ln, scale=1.0 / count, bias=eps[0:rows, :]))
                nc.scalar.activation(dst, lnv[0:rows, 0:cols], ACT.Exp, scale=-0.5).then_inc(*sigs["rs"].up())

            def copy_group(dst, name, src=None):
                act.wait_ge(*G.filled(name, l))
                nc.scalar.copy(dst, G.ps(name)[:, :] if src is None else src).then_inc(*G.empty(name))

            def hi(dst, name, src=None):
                act.wait_ge(*G.filled(name, l))
                nc.scalar.copy(dst, G.ps(name)[:, :] if src is None else src).then_inc(*sigs["hi"].up())

            sums_made = [0]

            def step_sums(step):
                which = step[1]
                for tt in range(TT):
                    if which == "mix":
                        act.wait_ge(*G.e[tt].at(l, 0))
                    else:
                        act.wait_ge(*G.evacuated(("out1", tt), l))
                    ins = nc.scalar.activation(sq[:, :, :].rearrange("p a t -> p (a t)"), h[:, tt, :], ACT.Square, accum_out=ss[:, tt:tt + 1])
                    link(ins)
                root(rstd[:, :], ss[:, :], D, TT, 0)

            def step_norm(step):
                which = step[1]
                gain = {"mix": gmix, "ple": gple}[which]
                for k in range(KD):
                    act.wait_ge(*G.filled((which, k), l))
                    nc.scalar.activation(xhi[:, k, :], G.ps((which, k))[:, :], ACT.Identity, scale=gain[:, k:k + 1])\
                      .then_inc(*sigs["hi"].up())

            def step_fm(step):
                name = step[1:3]
                hh = step[2]
                if step[1] == "hq":
                    copy_group(qT[:, hh, :], name)
                    return
                act.wait_ge(*G.filled(name, l))
                link(nc.scalar.activation(tA[:, :], G.ps(name)[:, :], ACT.Abs))
                link(nc.scalar.activation(tA[:, :], tA[:, :], ACT.Exp, scale=-1.0))
                if hh:
                    act.wait_ge(*b_ready.at(l, hh))
                nc.scalar.activation(tB[:, :], tA[:, :], ACT.Ln, bias=1.0).then_inc(*fg_b.up())
                act.wait_ge(*G.evacuated(name, l))
                nc.scalar.activation(kT[:, hh, :], tC[:, :], ACT.Exp, bias=lbc[:, 0, hh:hh + 1])
                act.wait_ge(*fg_c.at(l, hh + 1))
                link(nc.scalar.activation(tB[:, :], tA[:, :], ACT.Exp))
                nc.scalar.activation(tB[:, :], tB[:, :], ACT.Ln, bias=1.0).then_inc(*fg_d.up())

            def step_tm(step):
                _, kind, i, n, _ = step
                if i < n - 1:
                    return
                for tt in range(TT):
                    name = (kind, tt)
                    if kind == "v":
                        copy_group(v[:, tt, :], name)
                    elif kind == "go":
                        act.wait_ge(*G.filled(name, l))
                        nc.scalar.activation(ghg[:, tt, :], G.ps(name)[:, :], ACT.Exp, scale=-1.0).then_inc(*G.empty(name))
                        act.wait_ge(*G.evacuated(name, l))
                        link(nc.scalar.activation(ghg[:, tt, :], ghg[:, tt, :], ACT.Ln, bias=1.0))
                        nc.scalar.activation(ghg[:, tt, :], ghg[:, tt, :], ACT.Exp, scale=-1.0).then_inc(*go_ready.up())
                    elif kind in ("z", "nz"):
                        if kind == "nz":
                            act.wait_ge(*et_read[0].at(l, tt + 1))
                        copy_group(nzs[:, tt, :], name)
                    elif kind in ("pg0", "pg1"):
                        gate(name)
                    elif kind in ("pp0", "pp1"):
                        copy_group((decays, nzs)[int(kind[2])][:, tt, :], name)
                    elif kind == "nq":
                        place = square_place()
                        act.wait_ge(*G.filled(name, l))
                        src = G.ps(name)[:, :].rearrange("p (g n d) -> p g n d", g=NKV, n=NG)
                        for g in range(NKV):
                            nc.scalar.copy(q[:, tt, :, g, :], src[:, g])
                        nc.scalar.activation(place, G.ps(name)[:, :], ACT.Square).then_inc(*G.empty(name))
                        sums_made[0] += 1
                    elif kind == "kc":
                        act.wait_ge(*G.filled(name, l))
                        src = G.ps(name)[:, 0:256].rearrange("p (w d) -> p w d", d=DH)
                        nc.scalar.copy(kvc[:, tt, :, 0, :], src)
                        nc.scalar.copy(kvc[:, tt, :, 1, :], src).then_inc(*G.empty(name))
                    elif kind in ("ks", "kw"):
                        br = 0 if kind == "ks" else 1
                        act.wait_ge(*G.filled(name, l))
                        nc.scalar.copy(kk[:, tt, br, :], G.ps(name)[:, 0:P])
                        ins = nc.scalar.copy(vv[:, tt, br, :], G.ps(name)[:, P:2 * P])
                        if br:
                            ins = nc.scalar.activation(gts[:, tt].rearrange("p b h -> p (b h)"), G.ps(name)[:, 2 * P:2 * P + 24],
                                                       ACT.Exp, scale=-1.0)
                        ins.then_inc(*G.empty(name))

            def step_gate(step):
                gate((step[0][:-5], step[1]), src=nzs[:, step[1], :])

            def level_decay(hh, lv):
                act.wait_ge(*d_ready.next(l))
                nc.scalar.activation(dE[:, lv % 2, :], dE[:, lv % 2, :], ACT.Exp).then_inc(*e_ready.up())

            def step_hg_prep(step):
                hh = step[1]
                act.wait_ge(*b_ready.at(l, hh + 1))
                nc.scalar.activation(eB[:, :], bT[:, hh, :], ACT.Exp)
                for c in range(TT):
                    at = slice(c * P, (c + 1) * P)
                    nc.scalar.activation(kdx[:, at], bT[:, hh, at], ACT.Exp, scale=-1.0, bias=bT[:, hh, (c + 1) * P - 1:(c + 1) * P])
                nc.scalar.activation(ebl[:, :], bT[:, hh, P - 1::P], ACT.Exp).then_inc(*prep_exp.up())
                level_decay(hh, 0)
                copy_group(kdt[:, :, :].rearrange("p c d -> p (c d)"), ("kd", hh))

            def step_hg_level(step):
                hh, lv = step[1:]
                if lv + 1 < LEVELS:
                    level_decay(hh, lv + 1)

            def step_hg_out(step):
                name = ("o", step[1])
                place = square_place()
                act.wait_ge(*G.filled(name, l))
                nc.scalar.activation(place, G.ps(name)[:, :], ACT.Square).then_inc(*sigs["sq"].up())
                sums_made[0] += 1
                root(rsh[:, :], ssh[:, :], P, TT, sums_made[0])

            def step_hg_turn(step):
                hi(xhi[:, step[1], :], ("yT", step[1]))

            def step_p_turn(step):
                for k in range(2):
                    hi(pT[:, 0, k, :], ("pT", k))

            def step_q_norm(step):
                root(rsq[:, :, :].rearrange("p t h -> p (t h)"), ssq[:, :, :].rearrange("p t h -> p (t h)"), DH, 32, sums_made[0])
                for n in range(NG):
                    copy_group(qTn[:, n, :], ("qn", n))

            def step_q_rope(step):
                for n in range(NG):
                    hi(qTr[:, 0, n, :], ("qr", n))

            def step_k_norm(step):
                sums_made[0] += 1
                n_sq[0] += 1
                root(rsk[:, :], ssk[:, :], DH, 16, sums_made[0])
                for br in range(2):
                    hi(kTn[:, 0, br, :], ("kT", br))
                act.dma_start(p_raw, d["p"][bass.ds(l, 1)].rearrange("o b (t p) c -> p (o b t) c", p=P)).then_inc(p_loaded, 16)

            def step_c_in(step):
                w = step[1]
                if w == 0:
                    copy_group(peT[:, :, :].rearrange("p w j -> p (w j)"), ("pe",), G.ps(("pe",))[:, 0:32])
                act.wait_ge(*G.evacuated(("ct", w, 1), l))
                nc.scalar.copy(chi[:, :, :, :], cin).then_inc(*sigs["hi"].up())

            def step_c_hid(step):
                if step[2] == 1:
                    gate(("ch", step[1]), 2 * NCMP)

            def step_c_out(step):
                place = square_place()
                act.wait_ge(*G.filled(("co",), l))
                ps = G.ps(("co",))
                nc.scalar.copy(vc[0:NCMP].rearrange("p g d -> p (g d)"), ps[0:NCMP, P:2 * P])
                nc.scalar.activation(place[0:NCMP, 0:P], ps[0:NCMP, 0:P], ACT.Square).then_inc(*sigs["sq"].up())
                sums_made[0] += 1
                root(rsc[0:NCMP, :], ssc[0:NCMP, :], DH, 2, sums_made[0])

            def step_c_key(step):
                copy_group(kcT[:, 0:NCMP], ("ck",), G.ps(("ck",))[:, 0:NCMP])

            def step_c_score(step):
                act.wait_ge(*cs_ready.next(l))
                nc.scalar.activation(ce, cs, ACT.Exp).then_inc(*ce_done.up())

            def step_c_turn(step):
                qt = step[1]
                for i in range(2):
                    copy_group(pcT[0:NCMP, 4 * i:4 * i + 4, :].rearrange("p b q -> p (b q)"), ("cp", qt, i), G.ps(("cp", qt, i))[0:NCMP, :])

            def probs(qt, br, h0):
                name, u, n = ("s", qt, br, h0), UNITS.index((qt, br, h0)), (qt + 1) * P
                act.wait_ge(*nm_ready[0].next(l))
                for w in range(HEADS[qt]):
                    at = slice(w * n, (w + 1) * n)
                    ins = nc.scalar.activation(Pb[:, u % 2, at], G.ps(name)[:, at], ACT.Exp, bias=nm[:, u % 4, w:w + 1],
                                               accum_out=sums[:, qt % 2, 1 + br, h0 + w:h0 + w + 1])
                ins.then_inc(*G.empty(name))

            def step_att(step):
                for part, *unit in ahead(step[1]):
                    if part == "s":
                        probs(*unit)

            def step_att_turn(step):
                qt = step[1]
                name = ("nT", qt)
                hi(xhi[:, HG:KD, qt * P:(qt + 1) * P], name, G.ps(name)[:, :].rearrange("p (f q) -> p f q", f=4))

            table = {"sums": step_sums, "z_gate": step_gate, "nz_gate": step_gate,
                     "norm": step_norm, "fm": step_fm, "tm": step_tm, "p_turn": step_p_turn, "hg_prep": step_hg_prep,
                     "hg_level": step_hg_level, "hg_out": step_hg_out, "hg_turn": step_hg_turn,
                     "q_norm": step_q_norm, "q_rope": step_q_rope, "k_norm": step_k_norm, "c_in": step_c_in,
                     "c_hid": step_c_hid, "c_out": step_c_out, "c_key": step_c_key, "c_score": step_c_score, "c_turn": step_c_turn,
                     "att": step_att, "att_turn": step_att_turn}
            for step in followed(steps1):
                if step[0] in table:
                    table[step[0]](step)

        def vector_one(dve, l):
            G = G1
            tt_, ts, stt = nc.vector.tensor_tensor, nc.vector.tensor_scalar, nc.vector.scalar_tensor_tensor
            step_sig, hi_s, ex, sq_s, ss_s, rs = dve_step[0], hi_done[0], exp_done[0], sq_done[0], ss_done[0], rs_done[0]
            n_et, n_sq = [0], [0]

            def link(ins):
                ins.then_inc(*step_sig.up())
                dve.wait_ge(*step_sig.last(l))

            def et_place():
                i = n_et[0] % 2
                n_et[0] += 1
                dve.wait_ge(*ex.next(l))
                return et[:, i, :]

            def lo(dst, name, part, src=None, gain=None):
                dve.wait_ge(*hi_s.next(l))
                ps = G.ps(name)[:, :] if src is None else src
                if gain is None:
                    tt_(dst, ps, part.bitcast(F32), ALU.subtract).then_inc(*G.empty(name))
                else:
                    stt(dst, ps, gain, part.bitcast(F32), ALU.mult, ALU.subtract).then_inc(*G.empty(name))

            def step_sums(step):
                if step[1] == "mix":
                    nc.vector.tensor_copy(lbc[:, :, :], lbt[:, bass.ds(l, 1), :, :].rearrange("p a c h -> p (a c) h"))
                    nc.vector.tensor_copy(gains1[:, :, :], all_gains1[:, bass.ds(l, 1), :, :].rearrange("p a i k -> p (a i) k"))
                dve.wait_ge(*rs.next(l))
                for tt in range(TT):
                    ins = ts(diag[:, tt, :], ident[:, :], rstd[:, tt:tt + 1], None, ALU.mult)
                ins.then_inc(*diag_ready[0].up())

            def step_norm(step):
                which = step[1]
                gain = {"mix": gmix, "ple": gple}[which]
                for k in range(KD):
                    lo(xlo[:, k, :], (which, k), xhi[:, k, :], gain=gain[:, k:k + 1])

            def step_fm(step):
                if step[1] == "hq":
                    return
                name, hh = step[1:3], step[2]
                x = G.ps(name)[:, :]
                c1, a, c1a = (lbc[:, i, hh:hh + 1] for i in range(3))
                dve.wait_ge(*G.filled(name, l))
                dve.wait_ge(*fg_b.at(l, hh + 1))
                link(stt(tA[:, :], x, 0.0, tB[:, :], ALU.min, ALU.subtract))
                tt_(tC[:, :], tA[:, :], x, ALU.subtract).then_inc(*G.empty(name))
                ts(tD[:, :], tA[:, :], c1, a, ALU.add, ALU.max)
                link(ts(tA[:, :], tA[:, :], c1a, None, ALU.add))
                stt(tA[:, :], tA[:, :], -1.0, tA[:, :], ALU.mult, ALU.min).then_inc(*fg_c.up())
                dve.wait_ge(*fg_d.at(l, hh + 1))
                link(tt_(tD[:, :], tD[:, :], tB[:, :], ALU.add))
                for c in range(TT):
                    at = slice(c * P, (c + 1) * P)
                    ins = nc.vector.tensor_tensor_scan(bT[:, hh, at], ones[:, :].to_broadcast([P, P]), tD[:, at], 0.0, ALU.mult, ALU.add)
                ins.then_inc(*b_ready.up())

            def step_tm(step):
                _, kind, i, n, _ = step
                if i < n - 1:
                    return
                for tt in range(TT):
                    name = (kind, tt)
                    ps = G.ps(name)[:, :] if name in G.place else None
                    if kind == "nq":
                        place = sq[:, n_sq[0] % 2, :]
                        n_sq[0] += 1
                        dve.wait_ge(*G.evacuated(name, l))
                        nc.vector.tensor_reduce(ssq[:, tt, :].rearrange("p (n g) -> p g n", g=NKV),
                                                place.rearrange("p (g n d) -> p g n d", g=NKV, n=NG), AX, ALU.add).then_inc(*ss_s.up())
                    elif kind[:3] == "out":
                        at = h[:, tt, int(kind[3]) * T:(int(kind[3]) + 1) * T]
                        dve.wait_ge(*G.filled(name, l))
                        tt_(at, at, ps, ALU.add).then_inc(*G.empty(name))
                    elif kind[:2] == "pg":
                        other = ("pp" + kind[2], tt)
                        at = h[:, tt, int(kind[2]) * T:(int(kind[2]) + 1) * T]
                        e = et_place()
                        dve.wait_ge(*G.evacuated(other, l))
                        link(tt_(e, e, (decays, nzs)[int(kind[2])][:, tt, :], ALU.mult))
                        tt_(at, at, e, ALU.add).then_inc(*G.empty(name))

            def step_z_gate(step):
                tt = step[1]
                if tt == 0:
                    dve.wait_ge(params[0], l * PARAMS_ONE + PARAMS_ONE)
                e, g = et_place(), ghg[:, tt, :]
                dve.wait_ge(*go_ready.at(l, tt + 1))
                link(tt_(g, g, e, ALU.mult))
                tt_(g, g, nzs[:, tt, :], ALU.mult).then_inc(*et_read[0].up())
                dve.wait_ge(*et_read[0].last(l))
                g3 = ghg[:, tt, :].rearrange("p (h d) -> p h d", h=HG)
                link(tt_(g3, g3, onorm[:, :].unsqueeze(1).to_broadcast([P, HG, P]), ALU.mult))

            def step_nz_gate(step):
                e, g = et_place(), nzs[:, step[1], :]
                tt_(g, g, e, ALU.mult).then_inc(*et_read[0].up())

            def halves(t, lv):
                m = 64 >> lv
                x = t.rearrange("p (n a m) -> p n a m", a=2, m=m)
                return x[:, :, 0, :], x[:, :, 1, :], x[:, :, 0, m - 1:m].to_broadcast([P, T // (2 * m), m])

            def level_logs(hh, lv):
                before = LEVELS * hh + lv - (2 if lv >= 2 else 1 if lv == 0 else 3)
                if before >= 0:
                    dve.wait_ge(*qk_ready.at(l, before + 1))
                left, right, mid = halves(bT[:, hh, :], lv)
                dl, dr, _ = halves(dE[:, lv % 2, :], lv)
                tt_(dr, right, mid, ALU.subtract)
                tt_(dl, mid, left, ALU.subtract).then_inc(*d_ready.up())

            def keep(hh, lv):
                name = ("A", hh, lv)
                nc.vector.copy_predicated(At[:, hh % 2, :, :], masks[:, lv, :].unsqueeze(1).to_broadcast([P, TT, P]),
                                          G.ps(name)[:, :].rearrange("p (c t) -> p c t", c=TT)).then_inc(*G.empty(name))

            def step_hg_prep(step):
                hh = step[1]
                level_logs(hh, 0)
                dve.wait_ge(*prep_exp.at(l, hh + 1))
                tt_(qdec[:, :], qT[:, hh, :], eB[:, :], ALU.mult)
                tt_(kdec[:, :], kT[:, hh, :], kdx[:, :], ALU.mult).then_inc(*prep_done.up())

            def step_hg_level(step):
                hh, lv = step[1:]
                if lv + 1 < LEVELS:
                    level_logs(hh, lv + 1)
                if lv < LEVELS:
                    if lv >= 2:
                        dve.wait_ge(*G.filled(("A", hh, lv - 2), l))
                    if lv >= 3:
                        dve.wait_ge(*G.evacuated(("A", hh, lv - 3), l))
                    dve.wait_ge(*e_ready.next(l))
                    el, er, _ = halves(dE[:, lv % 2, :], lv)
                    tt_(halves(Ql[:, lv % 2, :], lv)[1], halves(qT[:, hh, :], lv)[1], er, ALU.mult)
                    tt_(halves(Kl[:, lv % 2, :], lv)[0], halves(kT[:, hh, :], lv)[0], el, ALU.mult).then_inc(*qk_ready.up())
                    if lv >= 2:
                        keep(hh, lv - 2)

            def step_hg_kv(step):
                hh = step[1]
                name = ("kv", hh)
                ps = G.ps(name)
                dve.wait_ge(*G.filled(name, l))
                dve.wait_ge(*G.evacuated(("A", hh, LEVELS - 3), l))
                nc.vector.tensor_copy(S[:, 0, :], ps[:, 0:P]).then_inc(*step_sig.up())
                keep(hh, LEVELS - 2)
                dve.wait_ge(*step_sig.last(l))
                dve.wait_ge(*G.evacuated(("A", hh, LEVELS - 2), l))
                stt(S[:, 1, :], S[:, 0, :], ebl[:, 1:2], ps[:, P:2 * P], ALU.mult, ALU.add).then_inc(*step_sig.up())
                keep(hh, LEVELS - 1)
                dve.wait_ge(*step_sig.last(l))
                dve.wait_ge(*G.evacuated(("A", hh, LEVELS - 1), l))
                stt(S[:, 2, :], S[:, 1, :], ebl[:, 2:3], ps[:, 2 * P:3 * P], ALU.mult, ALU.add).then_inc(*G.empty(name))
                keep(hh, LEVELS)

            def step_hg_out(step):
                hh = step[1]
                name = ("o", hh)
                place = sq[:, n_sq[0] % 2, :]
                n_sq[0] += 1
                dve.wait_ge(*sq_s.next(l))
                nc.vector.tensor_reduce(ssh[:, :], place.rearrange("p (c d) -> p c d", c=TT), AX, ALU.add).then_inc(*ss_s.up())
                dve.wait_ge(*rs.next(l))
                t3 = tA[:, :].rearrange("p (c d) -> p c d", c=TT)
                link(tt_(t3, G.ps(name)[:, :].rearrange("p (c d) -> p c d", c=TT), rsh[:, :].unsqueeze(2).to_broadcast([P, TT, P]), ALU.mult))
                if hh == 0:
                    dve.wait_ge(*go_ready.at(l, TT))
                g = ghg[:, :, hh * P:(hh + 1) * P]
                tt_(g, g, t3, ALU.mult).then_inc(*G.empty(name))

            def step_hg_turn(step):
                lo(xlo[:, step[1], :], ("yT", step[1]), xhi[:, step[1], :])

            def step_p_turn(step):
                for k in range(2):
                    lo(pT[:, 1, k, :], ("pT", k), pT[:, 0, k, :])

            def step_q_norm(step):
                q3 = q[:, :, :, :, :].rearrange("p t n g d -> p (t n g) d")
                r = rsq[:, :, :].rearrange("p t h -> p (t h)").unsqueeze(2).to_broadcast([P, TT * NH, DH])
                dve.wait_ge(*rs.next(l))
                link(stt(q3, q3, DH ** -0.5, r, ALU.mult, ALU.mult))
                tt_(q3, q3, qg[:, :].unsqueeze(1).to_broadcast([P, TT * NH, DH]), ALU.mult).then_inc(*q_ready.up())

            def rotate(x, n, done):
                part = [t[:, 0:TT * n * 8].rearrange("p (t n d) -> p t n d", t=TT, n=n) for t in (tA, tB, tC, tD)]
                cos, sin = (k1[c][:, :].rearrange("p (t d) -> p t d", t=TT).unsqueeze(2).to_broadcast([P, TT, n, 8]) for c in ("cos", "sin"))
                a, b = x[:, :, :, 0:8], x[:, :, :, 8:16]
                tt_(part[0], a, cos, ALU.mult)
                tt_(part[1], b, sin, ALU.mult)
                tt_(part[2], a, sin, ALU.mult)
                link(tt_(part[3], b, cos, ALU.mult))
                tt_(a, part[0], part[1], ALU.subtract)
                tt_(b, part[2], part[3], ALU.add).then_inc(*done.up())

            def step_q_rope(step):
                dve.wait_ge(*G.evacuated(("qn", NG - 1), l))
                rotate(q[:, :, :, :, :].rearrange("p t n g d -> p t (n g) d"), NH, qr_ready)
                for n in range(NG):
                    lo(qTr[:, 1, n, :], ("qr", n), qTr[:, 0, n, :])

            def step_k_norm(step):
                g2 = gts[:, :, :, :].rearrange("p t b h -> p (t b h)")
                dve.wait_ge(*G.evacuated(("kw", TT - 1), l))
                link(ts(g2, g2, 1.0, None, ALU.add))
                link(nc.vector.reciprocal(g2, g2))
                k3 = kk[:, :, :, :].rearrange("p t b (g d) -> p (t b g) d", g=NKV)
                s3 = Kl[:, :, :].rearrange("p a (n d) -> p (a n) d", d=DH)
                link(tt_(s3, k3, k3, ALU.mult))
                nc.vector.tensor_reduce(ssk[:, :], s3, AX, ALU.add).then_inc(*ss_s.up())
                n_sq[0] += 1
                dve.wait_ge(*rs.next(l))
                link(tt_(k3, k3, rsk[:, :].unsqueeze(2).to_broadcast([P, 16, DH]), ALU.mult))
                for br in range(2):
                    kb = kk[:, :, br, :].rearrange("p t (g d) -> p t g d", g=NKV)
                    link(tt_(kb, kb, kg[:, 1 + br, :].unsqueeze(1).unsqueeze(1).to_broadcast([P, TT, NKV, DH]), ALU.mult))
                rotate(kk[:, :, :, :].rearrange("p t b (g d) -> p t (b g) d", g=NKV), 2 * NKV, k_ready)
                for br in range(2):
                    lo(kTn[:, 1, br, :], ("kT", br), kTn[:, 0, br, :])

            def step_c_in(step):
                w = step[1]
                dve.wait_ge(*G.evacuated(("pe",), l))
                for g in range(NKV):
                    name = ("ct", w, g)
                    dve.wait_ge(*G.filled(name, l))
                    for a in range(2):
                        rows = slice(a * DH, (a + 1) * DH)
                        tok = G.ps(name)[rows, :].rearrange("p (c j a) -> p a j c", j=8, a=2)[:, a]
                        for b in range(2):
                            pe8 = peT[rows, w, 8 * b:8 * b + 8].unsqueeze(2).to_broadcast([DH, 8, NCMP])
                            ins = tt_(cin[rows, 8 * b:8 * b + 8, g, :], tok[:, :, b:b + NCMP], pe8, ALU.add)
                    ins.then_inc(*G.empty(name))
                dve.wait_ge(*hi_s.next(l))
                tt_(clo[:, :, :, :].rearrange("p j g c -> p (j g c)"), cin.rearrange("p j g c -> p (j g c)"),
                    chi[:, :, :, :].rearrange("p j g c -> p (j g c)").bitcast(F32), ALU.subtract).then_inc(*clo_ready.up())

            def step_c_hid(step):
                if step[2] == 1:
                    name = ("ch", step[1])
                    e = et_place()[:, 0:2 * NCMP]
                    tt_(hid[:, step[1], :], e, G.ps(name)[:, 0:2 * NCMP], ALU.mult).then_inc(*G.empty(name))

            def step_c_out(step):
                place = sq[0:NCMP, n_sq[0] % 2, 0:P]
                n_sq[0] += 1
                dve.wait_ge(*sq_s.next(l))
                nc.vector.tensor_reduce(ssc[0:NCMP, :], place.rearrange("p (g d) -> p g d", g=NKV), AX, ALU.add).then_inc(*ss_s.up())
                dve.wait_ge(*rs.next(l))
                tt_(kcn[0:NCMP], G.ps(("co",))[0:NCMP, 0:P].rearrange("p (g d) -> p g d", g=NKV),
                    rsc[0:NCMP, :].unsqueeze(2).to_broadcast([NCMP, NKV, DH]), ALU.mult).then_inc(*G.empty(("co",)))
                dve.wait_ge(*G.evacuated(("co",), l))
                tt_(kcn[0:NCMP], kcn[0:NCMP], kg[0:NCMP, 0, :].unsqueeze(1).to_broadcast([NCMP, NKV, DH]), ALU.mult).then_inc(*kc_ready.up())

            def step_c_score(step):
                qt = step[1]
                bias = k1["cbias"][:, qt * NCMP:(qt + 1) * NCMP].unsqueeze(1)
                for g in range(NKV):
                    name = ("cs", qt, g)
                    dve.wait_ge(*G.filled(name, l))
                    tt_(cs[:, g * NG:(g + 1) * NG, :], G.ps(name)[:, 0:P].rearrange("p (n c) -> p n c", n=NG)[:, :, 0:NCMP],
                        bias.to_broadcast([P, NG, NCMP]), ALU.add).then_inc(*G.empty(name))
                dve.wait_ge(*G.evacuated(("cs", qt, 1), l))
                link(nc.vector.tensor_reduce(mx[:, :], cs, AX, ALU.max))
                tt_(cs, cs, mx[:, :].unsqueeze(2).to_broadcast([P, NH, NCMP]), ALU.subtract).then_inc(*cs_ready.up())
                dve.wait_ge(*ce_done.next(l))
                stt(ce, bias.to_broadcast([P, NH, NCMP]), 0.0, ce, ALU.is_ge, ALU.mult).then_inc(*cp_ready.up())
                dve.wait_ge(*cp_ready.last(l))
                link(nc.vector.tensor_reduce(sums[:, qt % 2, 0, :], ce, AX, ALU.add))
                link(ts(sums[:, qt % 2, 0, :], sums[:, qt % 2, 0, :], 1e-30, None, ALU.max))

            def greatest(qt, br, h0):
                name, u, heads = ("s", qt, br, h0), UNITS.index((qt, br, h0)), HEADS[qt]
                n = heads * (qt + 1) * P
                dve.wait_ge(*G.filled(name, l))
                nc.vector.tensor_reduce(nm[:, u % 4, 0:heads], G.ps(name)[:, 0:n].rearrange("p (w k) -> p w k", w=heads), AX, ALU.max,
                                        negate=True).then_inc(*nm_ready[0].up())

            def probs_turned(qt, br, h0):
                name, u, n = ("p", qt, br, h0), UNITS.index((qt, br, h0)), HEADS[qt] * (qt + 1) * P
                dve.wait_ge(*G.filled(name, l))
                nc.vector.tensor_copy(Pt[:, u % 2, 0:n], G.ps(name)[:, 0:n]).then_inc(*G.empty(name))

            def step_att(step):
                for part, *unit in ahead(step[1]):
                    if part == "s":
                        greatest(*unit)
                    else:
                        probs_turned(*unit)

            def step_att_y(step):
                qt = step[1]
                wide = lambda i: coef[:, i, :].unsqueeze(2).to_broadcast([P, NH, DH])
                by_head = lambda t: t.rearrange("p (h d) -> p h d", h=NH)
                if step[2] == 0:
                    dve.wait_ge(*G.evacuated(("s", qt, 1, NH - HEADS[qt]), l))
                    link(nc.vector.reciprocal(coef[:, :, :], sums[:, qt % 2, :, :]))
                    link(tt_(coef[:, :, :], coef[:, :, :], gts[:, qt, :, :], ALU.mult))
                if step[2] < 3:
                    dst, name, i = ((y, ("o_a", qt, 0), 1), (tA, ("o_a", qt, 1), 2), (tB, ("o_c", qt), 0))[step[2]]
                    dve.wait_ge(*G.filled(name, l))
                    tt_(by_head(dst[:, :]), by_head(G.ps(name)[:, :]), wide(i), ALU.mult).then_inc(*G.empty(name))
                else:
                    dve.wait_ge(*G.evacuated(("o_c", qt), l))
                    link(tt_(y[:, :], y[:, :], tA[:, :], ALU.add))
                    link(tt_(y[:, :], y[:, :], tB[:, :], ALU.add))
                    tt_(y[:, :], y[:, :], nzs[:, qt, :], ALU.mult).then_inc(*y_ready[0].up())

            def step_att_turn(step):
                qt = step[1]
                at = slice(qt * P, (qt + 1) * P)
                lo(xlo[:, HG:KD, at], ("nT", qt), xhi[:, HG:KD, at], src=G.ps(("nT", qt))[:, :].rearrange("p (f q) -> p f q", f=4))

            table = {"sums": step_sums, "z_gate": step_z_gate, "nz_gate": step_nz_gate,
                     "norm": step_norm, "fm": step_fm, "tm": step_tm, "p_turn": step_p_turn, "hg_prep": step_hg_prep,
                     "hg_level": step_hg_level, "hg_kv": step_hg_kv, "hg_out": step_hg_out, "hg_turn": step_hg_turn,
                     "q_norm": step_q_norm, "q_rope": step_q_rope, "k_norm": step_k_norm, "c_in": step_c_in,
                     "c_hid": step_c_hid, "c_out": step_c_out, "c_score": step_c_score,
                     "att": step_att, "att_y": step_att_y, "att_turn": step_att_turn}
            for step in followed(steps1):
                if step[0] in table:
                    table[step[0]](step)

        def tensor_two(pe, l):
            G, ring = G2, ring2

            def chunk(step):
                pe.wait_ge(*ring.split(l, number2[step]))
                return number2[step] % SLOTS

            def turn(name, tiles, src):
                pe.wait_ge(*G.free(name, l))
                for i in range(tiles):
                    mm = pe.transpose(G.ps(name)[:, i * P:(i + 1) * P], src(i), ident[:, :])
                mm.then_inc(*G.full(name))

            def normed(name, tiles, src, dg):
                pe.wait_ge(*G.free(name, l))
                for tt in range(tiles):
                    mm = pe.matmul(G.ps(name)[:, tt * P:(tt + 1) * P], src(tt), dg[:, tt, :], start=True, stop=True)
                mm.then_inc(*G.full(name))

            def step_norm(step):
                pe.wait_ge(*diag_ready[1].next(l))
                for k in range(KD):
                    normed((step[1], k), TT, lambda tt: h[:, tt, k * P:(k + 1) * P], diag)

            def step_mem(step):
                pe.wait_ge(*diag_ready[1].next(l))
                for k in range(KD):
                    normed(("mm", k), MT, lambda tt: mem[:, tt, k * P:(k + 1) * P], diag)

            first_of = {("ax", 0): "mix", ("xq", 0): "xa", ("u", 0): "ffn"}

            def step_fm(step):
                name = step[1:3]
                s = chunk(step)
                pe.wait_ge(*G.free(name, l))
                rhs = (mmT[:, 0], mmT[:, 1]) if step[1] == "xk" else (xhi, xlo)
                cols = rhs[0].shape[2]
                o = G.ps(name)[:, 0:cols]
                for k in range(KD):
                    if name in first_of:
                        pe.wait_ge(*G.evacuated((first_of[name], k), l))
                    if name == ("xk", 0):
                        pe.wait_ge(*G.evacuated(("mm", k), l))
                    wh, wl = whi[:, s, k * P:(k + 1) * P], wlo[:, s, k * P:(k + 1) * P]
                    mm = pe.matmul(o, wh, rhs[0][:, k, :], start=(k == 0), stop=False)
                    if k == 0:
                        mm.then_inc(chunk_begun, 1)
                    pe.matmul(o, wh, rhs[1][:, k, :], start=False, stop=False)
                    mm = pe.matmul(o, wl, rhs[0][:, k, :], start=False, stop=(k == KD - 1))
                mm.then_inc(*G.full(name))

            def step_tm(step):
                _, kind, i, n, (_, k0, nk, _, cols) = step
                rows, base, tiles = (xhi, xlo), 0, TT
                if kind[0] == "y":
                    rows = {"a": yaT, "b": ybT, "c": ycT}[kind[1]]
                    if i == 0 and kind == "ya0":
                        pe.wait_ge(*ya_ready.at(l, 2))
                    if i == 0 and kind == "yb0":
                        for hh in range(RH):
                            pe.wait_ge(*G.evacuated(("ybT", hh), l))
                    if i == 0 and kind == "yc0":
                        for k in range(2):
                            pe.wait_ge(*G.evacuated(("ycT", k), l))
                    rows = (rows[:, 0], rows[:, 1])
                elif kind[:2] == "xv":
                    rows, tiles = (mmT[:, 0], mmT[:, 1]), MT
                elif kind[0] == "d":
                    rows, base = (gT[:, 0], gT[:, 1]), HALVES[int(kind[1])][0]
                    if i == 0 and kind[2] == "0":
                        pe.wait_ge(*g_ready.at(l, HALVES[int(kind[1])][1]))
                elif i == 0 and kind == "wo0":
                    pe.wait_ge(*G.evacuated(("mT", TT - 1, 1), l))
                elif i == 0 and kind == "xw0":
                    pe.wait_ge(*G.evacuated(("xo", XH - 1, 1), l))
                s = chunk(step)
                for tt in range(tiles):
                    if kind[:2] == "xw" and k0 < 4:
                        rows = (xoT[:, 0], xoT[:, 1])
                    name = (kind, tt)
                    if i == 0:
                        pe.wait_ge(*G.free(name, l))
                    at = slice(tt * P, (tt + 1) * P)
                    for kk_ in range(nk):
                        a, b = rows[0][:, k0 + kk_ - base, at], rows[1][:, k0 + kk_ - base, at]
                        wh, wl = whi[:, s, kk_ * cols:(kk_ + 1) * cols], wlo[:, s, kk_ * cols:(kk_ + 1) * cols]
                        mm = pe.matmul(G.ps(name)[:, :], a, wh, start=(i == 0 and kk_ == 0), stop=False)
                        if tt == 0 and kk_ == 0:
                            mm.then_inc(chunk_begun, 1)
                        pe.matmul(G.ps(name)[:, :], a, wl, start=False, stop=False)
                        mm = pe.matmul(G.ps(name)[:, :], b, wh, start=False, stop=(i == n - 1 and kk_ == nk - 1))
                    if i == n - 1:
                        mm.then_inc(*G.full(name))

            def step_ret_pair(step):
                p = step[1]
                if p == 0:
                    pe.wait_ge(*rot_ready.next(l))
                for w, name in enumerate((("qP", p), ("kP", p))):
                    turn(name, TT, lambda tt: qkr[:, tt, 4 * w + 2 * p:4 * w + 2 * p + 2, :].rearrange("p h d -> p (h d)"))

            def step_ret_in(step):
                hh = step[1]
                part = slice(hh % 2 * RK, (hh % 2 + 1) * RK)
                pe.wait_ge(*qx_ready.at(l, hh // 2 + 1))
                pe.wait_ge(*G.evacuated(("kP", hh // 2), l))
                name = ("rs", hh)
                pe.wait_ge(*G.free(name, l))
                for c in range(TT):
                    at = slice(c * P, (c + 1) * P)
                    mm = pe.matmul(G.ps(name)[:, at], kp[part, at], qp[part, at], start=True, stop=True)
                mm.then_inc(*G.full(name))
                name = ("rk", hh)
                if hh == 0:
                    for tt in range(TT):
                        pe.wait_ge(*G.evacuated(("v", tt), l))
                pe.wait_ge(*G.free(name, l))
                for c in range(TT - 1):
                    mm = pe.matmul(G.ps(name)[part, c * P:(c + 1) * P], qkr[:, c, 4 + hh, :], v2[:, c, hh * P:(hh + 1) * P],
                                   start=True, stop=True)
                mm.then_inc(*G.full(name))

            def step_ret_out(step):
                hh = step[1]
                part = slice(hh % 2 * RK, (hh % 2 + 1) * RK)
                pe.wait_ge(*G.evacuated(("rs", hh), l))
                pe.wait_ge(*G.evacuated(("rk", hh), l))
                name = ("ro", hh)
                pe.wait_ge(*G.free(name, l))
                for c in range(TT):
                    at = slice(c * P, (c + 1) * P)
                    mm = pe.matmul(G.ps(name)[:, at], ds[:, at], v2[:, c, hh * P:(hh + 1) * P], start=True, stop=(c == 0))
                    if c:
                        mm = pe.matmul(G.ps(name)[:, at], qx[part, at], R[part, c - 1, :], start=False, stop=True)
                mm.then_inc(*G.full(name))

            def step_ret_turn(step):
                hh = step[1]
                pe.wait_ge(*yb_ready.at(l, hh + 1))
                turn(("ybT", hh), TT, lambda c: gg[:, c, hh * P:(hh + 1) * P])

            def step_sg_w(step):
                pe.wait_ge(*sgw_ready.next(l))
                turn(("ws",), SGG, lambda g: sgw[:, g, :])

            def step_sg_mix(step):
                pe.wait_ge(*sg_ready.next(l))
                pe.wait_ge(*G.evacuated(("ws",), l))
                for tt in range(TT):
                    name = ("vm", tt)
                    pe.wait_ge(*G.free(name, l))
                    for g in range(SGG):
                        mm = pe.matmul(G.ps(name)[:, g * 64:(g + 1) * 64], wsT[:, g, :], gg[:, tt, 256 + g * 64:256 + (g + 1) * 64],
                                       start=True, stop=True)
                    mm.then_inc(*G.full(name))

            def step_sg_turn(step):
                for tt in range(TT):
                    pe.wait_ge(*G.evacuated(("vm", tt), l))
                for k in range(2):
                    turn(("ycT", k), TT, lambda tt: gg[:, tt, k * P:(k + 1) * P])

            def step_mg_turn(step):
                for tt in range(TT):
                    pe.wait_ge(*mg_ready.at(l, tt + 1))
                    for i in range(2):
                        turn(("mT", tt, i), 4, lambda k: mg[:, tt, (4 * i + k) * P:(4 * i + k + 1) * P])

            def scores(u):
                hh, qt = divmod(u, TT)
                name = ("xs", hh, qt)
                pe.wait_ge(*G.free(name, l))
                if qt == 0:
                    pe.wait_ge(*G.evacuated(("xq", 2 * hh + 1), l))
                for i in range(2):
                    for a, b in ((0, 0), (0, 1), (1, 0)):
                        mm = pe.matmul(G.ps(name)[:, 0:MEM], qx8[:, a, (2 * hh + i) % 4, qt * P:(qt + 1) * P], kx8[:, b, 2 * hh + i, :],
                                       start=(i == 0 and a == b), stop=(i == 1 and a == 1))
                mm.then_inc(*G.full(name))

            def probs_turn(u):
                name = ("xp", *divmod(u, TT))
                pe.wait_ge(*px_ready.at(l, u + 1))
                turn(name, MT, lambda i: Px[:, u % 2, i * P:(i + 1) * P])

            def step_xatt(step):
                hh, qt = step[1:]
                u = hh * TT + qt
                if u == 0:
                    pe.wait_ge(*G.evacuated(("xk", KD - 1), l))
                    scores(0)
                    scores(1)
                    probs_turn(0)
                if u + 2 < XH * TT:
                    scores(u + 2)
                if u + 1 < XH * TT:
                    probs_turn(u + 1)

            def step_xout(step):
                hh = step[1]
                if hh % 2 == 0:
                    pe.wait_ge(*G.evacuated((f"xv{hh // 2}", MT - 1), l))
                pe.wait_ge(*G.evacuated(("xp", hh, TT - 1), l))
                for i in range(2):
                    name, cols = ("xo", hh, i), slice(hh * XD + i * P, hh * XD + (i + 1) * P)
                    pe.wait_ge(*G.free(name, l))
                    for m in range(MT):
                        for a, b in ((0, 0), (0, 1), (1, 0)):
                            mm = pe.matmul(G.ps(name)[:, :], vx[:, a, m, cols], PxT[:, hh % 2, b, m, :],
                                           start=(m == 0 and a == b), stop=(m == MT - 1 and a == 1))
                    mm.then_inc(*G.full(name))

            table = {"norm": step_norm, "mem": step_mem, "fm": step_fm, "tm": step_tm, "ret_pair": step_ret_pair, "ret_in": step_ret_in,
                     "ret_out": step_ret_out, "ret_turn": step_ret_turn, "sg_w": step_sg_w, "sg_mix": step_sg_mix,
                     "sg_turn": step_sg_turn, "mg_turn": step_mg_turn, "xatt": step_xatt, "xout": step_xout}
            for step in steps2:
                if step[0] in table:
                    table[step[0]](step)

        def scalar_two(act, l):
            G = G2
            eu, n_et, n_sq, n_read, sums_made = [None, None], [0], [0], [0], [0]
            step_sig, hi_s, ex, sq_s, ss_s, rs = act_step[1], hi_done[1], exp_done[1], sq_done[1], ss_done[1], rs_done[1]

            def link(ins):
                ins.then_inc(*step_sig.up())
                act.wait_ge(*step_sig.last(l))

            def exp_place(name=None):
                i = n_et[0] % 2
                n_et[0] += 1
                if eu[i]:
                    act.wait_ge(*eu[i])
                if name is None:
                    n_read[0] += 1
                    eu[i] = et_read[1].at(l, n_read[0])
                else:
                    eu[i] = G.evacuated(name, l)
                return et[:, i, :]

            def one_over(x):
                link(nc.scalar.activation(x, x, ACT.Ln, bias=1.0))
                nc.scalar.activation(x, x, ACT.Exp, scale=-1.0).then_inc(*ex.up())

            def gate(name):
                place = exp_place(name)
                act.wait_ge(*G.filled(name, l))
                link(nc.scalar.activation(place, G.ps(name)[:, :], ACT.Exp, scale=-1.0))
                one_over(place)

            def square_place():
                i = n_sq[0]
                n_sq[0] += 1
                if i >= 2:
                    act.wait_ge(*ss_s.at(l, i - 1))
                return sq[:, i % 2, :]

            def root(dst, src, count, cols, need):
                if need:
                    act.wait_ge(*ss_s.at(l, need))
                if rs.made:
                    act.wait_ge(*rs.last(l))
                link(nc.scalar.activation(lnv[:, 0:cols], src, ACT.Ln, scale=1.0 / count, bias=eps[:, :]))
                nc.scalar.activation(dst, lnv[:, 0:cols], ACT.Exp, scale=-0.5).then_inc(*rs.up())

            def hi(dst, name, src=None):
                act.wait_ge(*G.filled(name, l))
                nc.scalar.copy(dst, G.ps(name)[:, :] if src is None else src).then_inc(*hi_s.up())

            def copy_group(dst, name, src=None):
                act.wait_ge(*G.filled(name, l))
                nc.scalar.copy(dst, G.ps(name)[:, :] if src is None else src).then_inc(*G.empty(name))

            def squares(src, sums):
                link(nc.scalar.activation(sq[:, :, :].rearrange("p a t -> p (a t)"), src, ACT.Square, accum_out=sums))

            def step_sums(step):
                which = step[1]
                for tt in range(TT):
                    if which == "mix":
                        act.wait_ge(*G.e[tt].at(l, 0))
                    else:
                        act.wait_ge(*G.evacuated(({"xa": "wo1", "ffn": "xw1"}[which], tt), l))
                    squares(h[:, tt, :], ss[:, tt:tt + 1])
                root(rstd[:, :], ss[:, :], D, TT, 0)

            def step_norm(step):
                which = step[1]
                gain = {"mix": gmix2, "xa": gxa, "ffn": gffn}[which]
                for k in range(KD):
                    act.wait_ge(*G.filled((which, k), l))
                    nc.scalar.activation(xhi[:, k, :], G.ps((which, k))[:, :], ACT.Identity, scale=gain[:, k:k + 1]).then_inc(*hi_s.up())

            def step_mem(step):
                act.wait_ge(mem_loaded, l * 16 + 16)
                for m in range(MT):
                    squares(mem[:, m, :], ssm[:, m:m + 1])
                root(rsm[:, 0:MT], ssm[:, 0:MT], D, MT, 0)
                for k in range(KD):
                    act.wait_ge(*G.filled(("mm", k), l))
                    nc.scalar.activation(mmT[:, 0, k, :], G.ps(("mm", k))[:, 0:MEM], ACT.Identity, scale=gmem[:, k:k + 1]).then_inc(*hi_s.up())

            def step_fm(step):
                name, i = step[1:3], step[2]
                if step[1] == "ax":
                    copy_group(cx[:, i, :], name)
                elif step[1] == "ab":
                    act.wait_ge(*G.evacuated(name, l))
                    nc.scalar.copy(yaT[:, 0, i, :], cx[:, i, :]).then_inc(*hi_s.up())
                elif step[1] == "xq":
                    act.wait_ge(*G.filled(name, l))
                    nc.scalar.activation(qx8[:, 0, i % 4, :], G.ps(name)[:, :], ACT.Identity, scale=XD ** -0.5).then_inc(*hi_s.up())
                elif step[1] == "xk":
                    hi(kx8[:, 0, i, :], name, G.ps(name)[:, 0:MEM])
                elif step[1] == "u":
                    if i >= 2:
                        act.wait_ge(*g_ready.at(l, i - 1))
                    gate(name)
                elif step[1] == "w":
                    act.wait_ge(*G.evacuated(name, l))
                    nc.scalar.copy(gT[:, 0, i % HALVES[0][1], :], et[:, (n_et[0] - 1) % 2, :]).then_inc(*hi_s.up())

            def gelu():
                for tt in range(TT):
                    place = square_place()
                    act.wait_ge(*G.evacuated(("z", tt), l))
                    nc.scalar.activation(place, gg[:, tt, :], ACT.Square).then_inc(*sq_s.up())
                    sums_made[0] += 1
                    e = exp_place()
                    act.wait_ge(*ss_s.at(l, sums_made[0]))
                    link(nc.scalar.activation(e, place, ACT.Exp, scale=-2.0 * (2.0 / np.pi) ** 0.5))
                    one_over(e)

            def step_tm(step):
                _, kind, i, n, _ = step
                if i < n - 1:
                    return
                for tt in range(MT if kind[:2] == "xv" else TT):
                    name = (kind, tt)
                    if kind == "v":
                        copy_group(v2[:, tt, :], name)
                    elif kind[:2] == "xv":
                        c = int(kind[2]) * T
                        hi(vx[:, 0, tt, c:c + T], name)
                    elif kind == "z":
                        copy_group(gg[:, tt, :], name)
                        if tt == TT - 1:
                            gelu()
                    elif kind[0] == "g":
                        e = exp_place()
                        act.wait_ge(*G.filled(name, l))
                        if kind == "g":
                            nc.scalar.copy(gg[:, tt, :], G.ps(name)[:, :])
                        nc.scalar.activation(e, G.ps(name)[:, :], ACT.Exp, scale=-1.0).then_inc(*G.empty(name))
                        act.wait_ge(*G.evacuated(name, l))
                        one_over(e)

            def step_ret_pair(step):
                p = step[1]
                copy_group(qp[:, :], ("qP", p))
                copy_group(kp[:, :], ("kP", p))

            def step_ret_out(step):
                place = square_place()
                act.wait_ge(*G.evacuated(("ro", step[1]), l))
                nc.scalar.activation(place, tA[:, :], ACT.Square).then_inc(*sq_s.up())
                sums_made[0] += 1
                root(rsv[:, :], ssv[:, :], P, TT, sums_made[0])

            def step_ret_turn(step):
                hi(ybT[:, 0, step[1], :], ("ybT", step[1]))

            def step_sg_w(step):
                copy_group(wsT[:, :, :].rearrange("p g c -> p (g c)"), ("ws",))

            def step_sg_norm(step):
                n_sq[0] += 1
                sums_made[0] += 1
                root(rsm[:, 4:8], ssm[:, 4:8], 256, TT, sums_made[0])

            def step_sg_turn(step):
                for k in range(2):
                    hi(ycT[:, 0, k, :], ("ycT", k))

            def step_mg_turn(step):
                for tt in range(TT):
                    for i in range(2):
                        name = ("mT", tt, i)
                        hi(xhi[:, 4 * i:4 * i + 4, tt * P:(tt + 1) * P], name, G.ps(name)[:, :].rearrange("p (k q) -> p k q", k=4))
                act.dma_start(mem[:, :, :], d["mem_2"][0].rearrange("(m p) c -> p m c", p=P)).then_inc(mem_loaded, 16)

            def probs(u):
                name = ("xs", *divmod(u, TT))
                act.wait_ge(*nm_ready[1].next(l))
                nc.scalar.activation(Px[:, u % 2, :], G.ps(name)[:, 0:MEM], ACT.Exp, bias=nmx[:, u % 4:u % 4 + 1],
                                     accum_out=sumx[:, u % 4:u % 4 + 1]).then_inc(*G.empty(name))

            def turned(u):
                hh, qt = divmod(u, TT)
                name = ("xp", hh, qt)
                hi(PxT[:, hh % 2, 0, :, qt * P:(qt + 1) * P], name, G.ps(name)[:, 0:MEM].rearrange("p (m q) -> p m q", m=MT))

            def step_xatt(step):
                hh, qt = step[1:]
                u = hh * TT + qt
                if u == 0:
                    probs(0)
                    probs(1)
                turned(u)
                if u + 2 < XH * TT:
                    probs(u + 2)

            def step_xout(step):
                for i in range(2):
                    k = 2 * step[1] + i
                    hi(xoT[:, 0, k] if k < 4 else xhi[:, k, :], ("xo", step[1], i))

            table = {"sums": step_sums, "norm": step_norm, "mem": step_mem, "fm": step_fm, "tm": step_tm, "ret_pair": step_ret_pair,
                     "ret_out": step_ret_out, "ret_turn": step_ret_turn, "sg_w": step_sg_w, "sg_norm": step_sg_norm,
                     "sg_turn": step_sg_turn, "mg_turn": step_mg_turn, "xatt": step_xatt, "xout": step_xout}
            for step in steps2:
                if step[0] in table:
                    table[step[0]](step)

        def vector_two(dve, l):
            G = G2
            tt_, ts, stt = nc.vector.tensor_tensor, nc.vector.tensor_scalar, nc.vector.scalar_tensor_tensor
            step_sig, hi_s, ex, sq_s, ss_s, rs = dve_step[1], hi_done[1], exp_done[1], sq_done[1], ss_done[1], rs_done[1]
            n_et, n_sq = [0], [0]

            def link(ins):
                ins.then_inc(*step_sig.up())
                dve.wait_ge(*step_sig.last(l))

            def et_place():
                i = n_et[0] % 2
                n_et[0] += 1
                dve.wait_ge(*ex.next(l))
                return et[:, i, :]

            def lo(dst, name, part, src=None, gain=None):
                dve.wait_ge(*hi_s.next(l))
                ps = G.ps(name)[:, :] if src is None else src
                if gain is None:
                    tt_(dst, ps, part.bitcast(F32), ALU.subtract).then_inc(*G.empty(name))
                else:
                    stt(dst, ps, gain, part.bitcast(F32), ALU.mult, ALU.subtract).then_inc(*G.empty(name))

            def diagonals(scale, tiles):
                dve.wait_ge(*rs.next(l))
                for tt in range(tiles):
                    ins = ts(diag[:, tt, :], ident[:, :], scale[:, tt:tt + 1], None, ALU.mult)
                ins.then_inc(*diag_ready[1].up())

            def step_sums(step):
                if step[1] == "mix":
                    nc.vector.tensor_copy(gains2[:, :, :], all_gains2[:, bass.ds(l, 1), :, :].rearrange("p a i k -> p (a i) k"))
                diagonals(rstd, TT)

            def step_norm(step):
                which = step[1]
                gain = {"mix": gmix2, "xa": gxa, "ffn": gffn}[which]
                for k in range(KD):
                    lo(xlo[:, k, :], (which, k), xhi[:, k, :], gain=gain[:, k:k + 1])

            def step_mem(step):
                diagonals(rsm, MT)
                for k in range(KD):
                    lo(mmT[:, 1, k, :], ("mm", k), mmT[:, 0, k, :], src=G.ps(("mm", k))[:, 0:MEM], gain=gmem[:, k:k + 1])

            def step_fm(step):
                name, i = step[1:3], step[2]
                ps = G.ps(name)[:, :]
                if step[1] == "ac":
                    nc.vector.memset(zp[:, i, 0:2], 0.0)
                    dve.wait_ge(*G.evacuated(("ax", i), l))
                    dve.wait_ge(*G.filled(name, l))
                    tt_(zp[:, i, 2:T + 2], cx[:, i, :], ps, ALU.mult).then_inc(*G.empty(name))
                elif step[1] == "ab":
                    dve.wait_ge(*G.evacuated(("ac", i), l))
                    link(ts(tB[:, :], zp[:, i, 0:T], convw[:, i, 0:1], None, ALU.mult))
                    link(stt(tB[:, :], zp[:, i, 1:T + 1], convw[:, i, 1:2], tB[:, :], ALU.mult, ALU.add))
                    link(stt(tB[:, :], zp[:, i, 2:T + 2], convw[:, i, 2:3], tB[:, :], ALU.mult, ALU.add))
                    dve.wait_ge(*G.filled(name, l))
                    tt_(cx[:, i, :], tB[:, :], ps, ALU.mult).then_inc(*G.empty(name))
                    dve.wait_ge(*hi_s.next(l))
                    tt_(yaT[:, 1, i, :], cx[:, i, :], yaT[:, 0, i, :].bitcast(F32), ALU.subtract).then_inc(*ya_ready.up())
                elif step[1] == "xk":
                    lo(kx8[:, 1, i, :], name, kx8[:, 0, i, :], src=G.ps(name)[:, 0:MEM])
                elif step[1] == "xq":
                    lo(qx8[:, 1, i % 4, :], name, qx8[:, 0, i % 4, :], gain=XD ** -0.5)
                elif step[1] == "u":
                    e = et_place()
                    tt_(e, e, ps, ALU.mult).then_inc(*G.empty(name))
                elif step[1] == "w":
                    e = et[:, (n_et[0] - 1) % 2, :]
                    dve.wait_ge(*G.evacuated(("u", i), l))
                    dve.wait_ge(*G.filled(name, l))
                    tt_(e, e, ps, ALU.mult).then_inc(*G.empty(name))
                    dve.wait_ge(*hi_s.next(l))
                    f = i % HALVES[0][1]
                    tt_(gT[:, 1, f, :], e, gT[:, 0, f, :].bitcast(F32), ALU.subtract).then_inc(*g_ready.up())

            def add_to_h(name, n):
                at = h[:, name[1], n * T:(n + 1) * T]
                dve.wait_ge(*G.filled(name, l))
                tt_(at, at, G.ps(name)[:, :], ALU.add).then_inc(*G.empty(name))

            def step_tm(step):
                _, kind, i, n, _ = step
                if i < n - 1 or kind == "v":
                    return
                for tt in range(MT if kind[:2] == "xv" else TT):
                    name = (kind, tt)
                    ps = G.ps(name)[:, :]
                    if kind[:2] == "xv":
                        c = int(kind[2]) * T
                        lo(vx[:, 1, tt, c:c + T], name, vx[:, 0, tt, c:c + T])
                    if kind == "g":
                        if tt == 0:
                            dve.wait_ge(params[1], l * PARAMS_TWO + PARAMS_TWO)
                        e, g = et_place(), gg[:, tt, :]
                        tt_(g, g, e, ALU.mult).then_inc(*et_read[1].up())
                        dve.wait_ge(*et_read[1].last(l))
                        link(tt_(g, g, retgn[:, :], ALU.mult))
                    elif kind == "qk":
                        dve.wait_ge(*G.filled(name, l))
                        x = ps.rearrange("p (h d) -> p h d", d=RK)
                        cos, sin = (k2[c][:, tt * 32:(tt + 1) * 32].unsqueeze(1).to_broadcast([P, 2 * RH, 32]) for c in ("rcos", "rsin"))
                        part = [t[:, 0:256].rearrange("p (h d) -> p h d", d=32) for t in (tA, tB, tC, tD)]
                        tt_(part[0], x[:, :, 0:32], cos, ALU.mult)
                        tt_(part[1], x[:, :, 32:64], sin, ALU.mult)
                        tt_(part[2], x[:, :, 0:32], sin, ALU.mult)
                        tt_(part[3], x[:, :, 32:64], cos, ALU.mult).then_inc(*G.empty(name))
                        dve.wait_ge(*G.evacuated(name, l))
                        tt_(qkr[:, tt, :, 0:32], part[0], part[1], ALU.subtract)
                        ins = tt_(qkr[:, tt, :, 32:64], part[2], part[3], ALU.add)
                        if tt == TT - 1:
                            ins.then_inc(*rot_ready.up())
                        else:
                            link(ins)
                    elif kind == "z":
                        place = sq[:, n_sq[0] % 2, :]
                        n_sq[0] += 1
                        dve.wait_ge(*sq_s.next(l))
                        link(ts(place, place, 0.044715, 1.0, ALU.mult, ALU.add))
                        tt_(place, place, gg[:, tt, :], ALU.mult).then_inc(*ss_s.up())
                        e = et_place()
                        tt_(gg[:, tt, :], e, gg[:, tt, :], ALU.mult).then_inc(*et_read[1].up())
                    elif kind[0] == "g":
                        at = slice(int(kind[2]) * T, (int(kind[2]) + 1) * T)
                        g = mg[:, tt, at] if kind[1] == "a" else gg[:, tt, :]
                        nc.vector.tensor_copy(g, et_place()).then_inc(*et_read[1].up())
                        dve.wait_ge(*et_read[1].last(l))
                    elif kind[0] == "y":
                        at = slice(int(kind[2]) * T, (int(kind[2]) + 1) * T)
                        m = mg[:, tt, at]
                        g = m if kind[1] == "a" else gg[:, tt, :]
                        dve.wait_ge(*G.filled(name, l))
                        tt_(g, g, ps, ALU.mult).then_inc(*G.empty(name))
                        if kind[1] != "a":
                            dve.wait_ge(*G.evacuated(name, l))
                            ins = tt_(m, m, g, ALU.add)
                            if kind == "yc1":
                                ins.then_inc(*mg_ready.up())
                            else:
                                link(ins)
                    elif kind[:2] in ("wo", "xw"):
                        add_to_h(name, int(kind[2]))
                    elif kind[0] == "d":
                        add_to_h(name, int(kind[2]))

            def step_ret_pair(step):
                p = step[1]
                dve.wait_ge(*G.evacuated(("qP", p), l))
                by_chunk = lambda t: t[:, :].rearrange("p (c q) -> p c q", c=TT)
                tt_(by_chunk(qx), by_chunk(qp), k2["xi"][:, p * P:(p + 1) * P].unsqueeze(1).to_broadcast([P, TT, P]), ALU.mult)
                dve.wait_ge(*G.evacuated(("kP", p), l))
                k = qkr[:, :, 4 + 2 * p:6 + 2 * p, :]
                tt_(k, k, k2["zeta"][:, 2 * p:2 * p + 2].unsqueeze(1).unsqueeze(3).to_broadcast([P, TT, 2, RK]), ALU.mult)\
                    .then_inc(*qx_ready.up())

            def step_ret_in(step):
                hh = step[1]
                part = slice(hh % 2 * RK, (hh % 2 + 1) * RK)
                name = ("rs", hh)
                dve.wait_ge(*G.filled(name, l))
                tt_(ds[:, :].rearrange("p (c q) -> p c q", c=TT), G.ps(name)[:, :].rearrange("p (c q) -> p c q", c=TT),
                    k2["decay"][:, hh * P:(hh + 1) * P].unsqueeze(1).to_broadcast([P, TT, P]), ALU.mult).then_inc(*G.empty(name))
                name = ("rk", hh)
                ps = G.ps(name)[part, :]
                dve.wait_ge(*G.filled(name, l))
                link(nc.vector.tensor_copy(R[part, 0, :], ps[:, 0:P]))
                link(stt(R[part, 1, :], R[part, 0, :], RESCALE[hh], ps[:, P:2 * P], ALU.mult, ALU.add))
                stt(R[part, 2, :], R[part, 1, :], RESCALE[hh], ps[:, 2 * P:3 * P], ALU.mult, ALU.add).then_inc(*G.empty(name))

            def step_ret_out(step):
                hh = step[1]
                name = ("ro", hh)
                by_chunk = lambda t: t.rearrange("p (c q) -> p c q", c=TT)
                ps = by_chunk(G.ps(name)[:, :])
                wide = lambda t: t[:, :].unsqueeze(2).to_broadcast([P, TT, P])
                dve.wait_ge(*G.filled(name, l))
                link(nc.vector.tensor_reduce(mux[:, :], ps, AX, ALU.add))
                link(ts(mux[:, :], mux[:, :], 1.0 / RV, None, ALU.mult))
                tt_(by_chunk(tA[:, :]), ps, wide(mux), ALU.subtract).then_inc(*G.empty(name))
                place = sq[:, n_sq[0] % 2, :]
                n_sq[0] += 1
                dve.wait_ge(*sq_s.next(l))
                nc.vector.tensor_reduce(ssv[:, :], by_chunk(place), AX, ALU.add).then_inc(*ss_s.up())
                dve.wait_ge(*rs.next(l))
                link(tt_(by_chunk(tA[:, :]), by_chunk(tA[:, :]), wide(rsv), ALU.mult))
                g = gg[:, :, hh * P:(hh + 1) * P]
                tt_(g, g, by_chunk(tA[:, :]), ALU.mult).then_inc(*yb_ready.up())

            def step_ret_turn(step):
                lo(ybT[:, 1, step[1], :], ("ybT", step[1]), ybT[:, 0, step[1], :])

            def step_sg_w(step):
                tt_(sgw[:, :, :], sgw[:, :, :], k2["tril"][:, :].unsqueeze(1).to_broadcast([P, SGG, P]), ALU.mult).then_inc(*sgw_ready.up())

            def step_sg_norm(step):
                zv = gg[:, :, 256:512]
                wide = lambda t: t.unsqueeze(2).to_broadcast([P, TT, 256])
                c3 = cx[:, :, :].rearrange("p a (b d) -> p (a b) d", b=2)
                dve.wait_ge(*et_read[1].last(l))
                link(nc.vector.tensor_reduce(mux[:, :], zv, AX, ALU.add))
                link(ts(mux[:, :], mux[:, :], 1.0 / 256, None, ALU.mult))
                link(tt_(zv, zv, wide(mux[:, :]), ALU.subtract))
                link(tt_(c3, zv, zv, ALU.mult))
                nc.vector.tensor_reduce(ssm[:, 4:8], c3, AX, ALU.add).then_inc(*ss_s.up())
                n_sq[0] += 1
                dve.wait_ge(*rs.next(l))
                link(tt_(zv, zv, wide(rsm[:, 4:8]), ALU.mult))
                tt_(zv, zv, sgln[:, :].unsqueeze(1).to_broadcast([P, TT, 256]), ALU.mult).then_inc(*sg_ready.up())

            def step_sg_mix(step):
                for tt in range(TT):
                    name = ("vm", tt)
                    dve.wait_ge(*G.filled(name, l))
                    t = (tA, tB)[tt // 2][:, tt % 2 * 256:(tt % 2 + 1) * 256]
                    t3 = t.rearrange("p (g d) -> p g d", g=SGG)
                    link(tt_(t3, G.ps(name)[:, 0:256].rearrange("p (g d) -> p g d", g=SGG), sgb[:, :].unsqueeze(2).to_broadcast([P, SGG, 64]), ALU.add))
                    u = gg[:, tt, 0:256]
                    tt_(u, u, t, ALU.mult).then_inc(*G.empty(name))

            def step_sg_turn(step):
                for k in range(2):
                    lo(ycT[:, 1, k, :], ("ycT", k), ycT[:, 0, k, :])

            def step_mg_turn(step):
                for tt in range(TT):
                    for i in range(2):
                        name, at = ("mT", tt, i), (slice(None), slice(4 * i, 4 * i + 4), slice(tt * P, (tt + 1) * P))
                        lo(xlo[at], name, xhi[at], src=G.ps(name)[:, :].rearrange("p (k q) -> p k q", k=4))

            def greatest(u):
                name = ("xs", *divmod(u, TT))
                dve.wait_ge(*G.filled(name, l))
                nc.vector.tensor_reduce(nmx[:, u % 4:u % 4 + 1], G.ps(name)[:, 0:MEM], AX, ALU.max, negate=True).then_inc(*nm_ready[1].up())

            def shares(u):
                dve.wait_ge(*G.evacuated(("xs", *divmod(u, TT)), l))
                c = slice(u % 4, u % 4 + 1)
                link(nc.vector.reciprocal(recx[:, c], sumx[:, c]))
                ts(Px[:, u % 2, :], Px[:, u % 2, :], recx[:, c], None, ALU.mult).then_inc(*px_ready.up())

            def step_xatt(step):
                hh, qt = step[1:]
                u = hh * TT + qt
                if u == 0:
                    greatest(0)
                    greatest(1)
                    shares(0)
                if u + 1 < XH * TT:
                    shares(u + 1)
                if u + 2 < XH * TT:
                    greatest(u + 2)
                at = (slice(None), slice(None), slice(qt * P, (qt + 1) * P))
                lo(PxT[:, hh % 2, 1][at], ("xp", hh, qt), PxT[:, hh % 2, 0][at], src=G.ps(("xp", hh, qt))[:, 0:MEM].rearrange("p (m q) -> p m q", m=MT))

            def step_xout(step):
                for i in range(2):
                    k = 2 * step[1] + i
                    if k < 4:
                        lo(xoT[:, 1, k], ("xo", step[1], i), xoT[:, 0, k])
                    else:
                        lo(xlo[:, k, :], ("xo", step[1], i), xhi[:, k, :])

            table = {"sums": step_sums, "norm": step_norm, "mem": step_mem, "fm": step_fm, "tm": step_tm, "ret_pair": step_ret_pair, "ret_in": step_ret_in,
                     "ret_out": step_ret_out, "ret_turn": step_ret_turn, "sg_w": step_sg_w, "sg_norm": step_sg_norm,
                     "sg_mix": step_sg_mix, "sg_turn": step_sg_turn, "mg_turn": step_mg_turn, "xatt": step_xatt, "xout": step_xout}
            for step in steps2:
                if step[0] in table:
                    table[step[0]](step)

        def of_layer(name, l):
            return d[name][bass.ds(l, 1)]

        def weights(spec, l):
            key, k0, nk, c0, cols = spec
            if key[:6] == "cmp_w1":
                src = d["cmp_w1"][bass.ds(l, 1), int(key[-1]), k0 * P:(k0 + nk) * P, c0:c0 + cols]
            else:
                src = d[key][bass.ds(l, 1), k0 * P:(k0 + nk) * P, c0:c0 + cols]
            return src.rearrange("o (k p) n -> p (o k) n", p=P)

        block = ctx.enter_context(nc.Block())
        setup_loads = []

        @block.sync
        def _(sp):
            def load(dst, src, done):
                sp.dma_start(dst, src).then_inc(done, 16)

            def load_across(dst, src, done):
                sp.dma_start(dst, src, allow_slow_non_contiguous=True).then_inc(done, 16)

            def load_setup(dst, src):
                load(dst, src, setup)
                setup_loads.append(dst)

            def params_one(l):
                load(onorm[:, :], of_layer("hgrn_onorm_g", l).to_broadcast([P, P]), params[0])
                load(qg[:, :], of_layer("nsa_qnorm_g", l).to_broadcast([P, DH]), params[0])
                load(kg[:, :, :], of_layer("nsa_knorm_g", l).to_broadcast([P, 3, DH]), params[0])
                load(w2[:, :, :], of_layer("cmp_w2", l).rearrange("o w p d -> p (o w) d"), params[0])
                load(pe_raw[0:32, :], of_layer("cmp_pe", l).rearrange("o w (j a) d -> (o w j) (a d)", a=2), params[0])

            def params_two(l):
                for n, t in k2.items():
                    load(t[:, :], d["two_" + n], params[1])
                for t in range(2):
                    load_across(convw[:, t, :], of_layer("conv_w_2", l)[:, :, t * P:(t + 1) * P].rearrange("o k p -> p (o k)"), params[1])
                load_across(sgb[:, :], of_layer("sg_b_2", l).rearrange("o g c -> c (o g)"), params[1])
                load(retgn[:, :], of_layer("ret_gn_2", l).to_broadcast([P, T]), params[1])
                load(sgln[:, :], of_layer("sg_ln_2", l).to_broadcast([P, 256]), params[1])
                load(sgw[:, :, :], of_layer("sg_w_2", l).rearrange("o g c m -> c (o g) m"), params[1])

            def stage(l, chunks, ring, emptied, load_params):
                for j, spec in enumerate(chunks):
                    if j == SLOTS:
                        sp.wait_ge(made_ready, 3)
                        sp.wait_ge(*emptied[TT - 1].at(l, 0))
                        load_params(l)
                    _, _, nk, _, cols = spec
                    sp.wait_ge(*ring.raw_free(l, j))
                    load(raw[:, j % SLOTS, 0:nk * cols].rearrange("p (k n) -> p k n", k=nk), weights(spec, l), raw_loaded[j % SLOTS])

            load_setup(ident[:, :], d["one_ident"])
            for tt in range(TT):
                load(h[:, tt, :], d["x"][0, tt * P:(tt + 1) * P, :], h_loaded[tt])
            load_across(lbraw[:, :, :], d["hgrn_lb"].rearrange("a (h p) -> p a h", p=P), setup)
            setup_loads.append(lbraw)
            for i, n in enumerate(("norm_g", "ple_norm_g")):
                for l in range(DEPTH):
                    load_across(all_gains1[:, l, i, :], d[n][l].rearrange("(k p) -> p k", p=P), setup)
                    setup_loads.append(all_gains1)
            for n, t in k1.items():
                load_setup(t[:, :], d["one_" + n])
            load_setup(tA[:, 0:P], d["one_causal"])
            load_setup(dE[:, :, :].rearrange("p a t -> p (a t)"), d["masks"])
            with sp.Fori(0, DEPTH) as l:
                stage(l, chunks1, ring1, G1.e, params_one)
            with sp.Fori(0, DEPTH) as l:
                stage(l, chunks2, ring2, G2.e, params_two)
            sp.wait_ge(*g_ready.at(DEPTH - 1, FT))
            load(gfin[:, :], d["final_norm_2"].unsqueeze(0).to_broadcast([P, D]), gain_loaded)
            for tt in range(TT):
                sp.wait_ge(fin_done, tt + 1)
                load(out[0, tt * P:(tt + 1) * P, :], h[:, tt, :], out_done)
            sp.wait_ge(out_done, 16 * TT)

        second_gains = ("norm_mix_2", "norm_xa_2", "norm_mem_2", "norm_ffn_2")
        ready = 16 * (len(setup_loads) + DEPTH * len(second_gains))

        @block.gpsimd
        def _(pool):
            nc.gpsimd.memset(zero[:, :], 0.0).then_inc(zero_ready, 1)
            pool.wait_ge(zero_ready, 1)

            def parts(l, chunks, ring):
                for j, (_, _, nk, _, cols) in enumerate(chunks):
                    s, n = j % SLOTS, nk * cols
                    pool.wait_ge(*ring.loaded(l, j))
                    pool.wait_ge(*ring.parts_free(l, j))
                    nc.gpsimd.tensor_tensor(whi[:, s, 0:n], raw[:, s, 0:n], zero[:, :].to_broadcast([P, n]), ALU.add).then_inc(hi_split, 1)
                    pool.wait_ge(*ring.hi(l, j))
                    nc.gpsimd.tensor_tensor(wlo[:, s, 0:n], raw[:, s, 0:n], whi[:, s, 0:n].bitcast(F32), ALU.subtract).then_inc(lo_split, 1)

            with pool.Fori(0, DEPTH) as l:
                parts(l, chunks1, ring1)
            with pool.Fori(0, DEPTH) as l:
                parts(l, chunks2, ring2)

        floor, top, e2, share = (lbs[:, 2 * i:2 * i + 2, :] if i < 3 else lbt[:, :, 2, :] for i in range(4))
        last = DEPTH - 1

        @block.vector
        def _(dve):
            steps = [0]

            def link(ins):
                steps[0] += 1
                ins.then_inc(setup_step, 1)
                dve.wait_ge(setup_step, steps[0])

            tt_, ts = nc.vector.tensor_tensor, nc.vector.tensor_scalar
            nc.vector.memset(lnv[:, 30:31], 0.0).then_inc(lo_split, SLOTS)
            nc.vector.memset(lnv[:, 31:32], 0.0).then_inc(chunk_begun, SLOTS - 1)
            for b in range(8):
                nc.vector.memset(lnv[:, b:b + 1], 0.0).then_inc(G1.e[b].sem, 1)
            link(nc.vector.memset(eps[:, :], EPS))
            link(nc.vector.memset(ones[:, :], 1.0))
            for t in (At[:, :, :, :], Ql[:, :, :], Kl[:, :, :], pe_raw[:, :]):
                link(nc.vector.memset(t, 0.0))
            dve.wait_ge(setup, ready)
            link(nc.vector.tensor_copy(identb[:, :], ident[:, :]))
            link(nc.vector.tensor_copy(masks[:, :, :].rearrange("p a t -> p (a t)"), dE[:, :, :].rearrange("p a t -> p (a t)")))
            link(nc.vector.tensor_copy(causal[:, :], tA[:, 0:P]))
            big = top[:, 0, :]
            link(tt_(big, lbraw[:, 0, :], lbraw[:, 1, :], ALU.max))
            tt_(e2, lbraw[:, :, :], big.unsqueeze(1).to_broadcast([P, 2, HG]), ALU.subtract).then_inc(made_ready, 1)
            dve.wait_ge(act_setup, 1)
            link(tt_(big, e2[:, 0, :], e2[:, 1, :], ALU.add))
            link(nc.vector.reciprocal(big, big))
            link(tt_(e2, e2, big.unsqueeze(1).to_broadcast([P, 2, HG]), ALU.mult))
            link(tt_(big, e2[:, 0, :], e2[:, 1, :], ALU.add))
            link(tt_(floor[:, 0, :], e2[:, 0, :], e2[:, 0, :], ALU.subtract))
            link(tt_(floor[:, 1, :], big, e2[:, 0, :], ALU.subtract))
            link(ts(top, floor, 1e-37, None, ALU.max))
            ts(e2, floor, 1e-37, NEG, ALU.is_lt, ALU.mult).then_inc(made_ready, 1)
            dve.wait_ge(act_setup, 2)
            link(tt_(lbt[:, :, 1, :], lbt[:, :, 1, :], e2, ALU.add))
            link(ts(lbt[:, :, 0, :], lbt[:, :, 0, :], NEG, None, ALU.max))
            tt_(lbt[:, :, 2, :], lbt[:, :, 0, :], lbt[:, :, 1, :], ALU.subtract).then_inc(made_ready, 1)
            dve.wait_ge(made_ready, 3)
            for tt in range(TT):
                dve.wait_ge(h_loaded[tt], 16)
            with dve.Fori(0, DEPTH) as l:
                vector_one(dve, l)
            with dve.Fori(0, DEPTH) as l:
                vector_two(dve, l)
            dve.wait_ge(gain_loaded, 16)
            for tt in range(TT):
                dve.wait_ge(fin_root, tt + 1)
                nc.vector.scalar_tensor_tensor(h[:, tt, :], h[:, tt, :], rstd[:, tt:tt + 1], gfin[:, :], ALU.mult, ALU.mult).then_inc(fin_done, 1)

        @block.scalar
        def _(act):
            act.add_instruction(mybir.InstLoadActFuncSet(name=nc.get_next_instruction_name(), act_func_set_id=LOG_EXP_TABLES, ins=[], outs=[]))
            for i, n in enumerate(second_gains):
                for l in range(DEPTH):
                    act.dma_start(all_gains2[:, l, i, :], d[n][l].rearrange("(k p) -> p k", p=P), allow_slow_non_contiguous=True).then_inc(setup, 16)
            act.wait_ge(made_ready, 1)
            nc.scalar.activation(e2, e2, ACT.Exp).then_inc(act_setup, 1)
            act.wait_ge(made_ready, 2)
            nc.scalar.activation(lbt[:, :, 0, :], floor, ACT.Ln, scale=-1.0, bias=1.0)
            nc.scalar.activation(lbt[:, :, 1, :], top, ACT.Ln).then_inc(act_setup, 1)
            for tt in range(TT):
                act.wait_ge(h_loaded[tt], 16)
            act.wait_ge(made_ready, 3)
            with act.Fori(0, DEPTH) as l:
                scalar_one(act, l)
            with act.Fori(0, DEPTH) as l:
                scalar_two(act, l)
            for tt in range(TT):
                act.wait_ge(*G2.evacuated(("d11", tt), last))
                nc.scalar.activation(sq[:, :, :].rearrange("p a t -> p (a t)"), h[:, tt, :], ACT.Square, accum_out=ss[:, tt:tt + 1]).then_inc(fin_step, 1)
                act.wait_ge(fin_step, 2 * tt + 1)
                nc.scalar.activation(lnv[:, tt:tt + 1], ss[:, tt:tt + 1], ACT.Ln, scale=1.0 / D, bias=eps[:, :]).then_inc(fin_step, 1)
                act.wait_ge(fin_step, 2 * tt + 2)
                nc.scalar.activation(rstd[:, tt:tt + 1], lnv[:, tt:tt + 1], ACT.Exp, scale=-0.5).then_inc(fin_root, 1)

        @block.tensor
        def _(pe):
            for tt in range(TT):
                pe.wait_ge(h_loaded[tt], 16)
            pe.wait_ge(made_ready, 3)
            with pe.Fori(0, DEPTH) as l:
                tensor_one(pe, l)
            with pe.Fori(0, DEPTH) as l:
                tensor_two(pe, l)

        return {(name, stage_): s.made for name, stage_, s in made}


INPUTS = ["x", "p", "norm_g", "w_in", "hgrn_lb", "hgrn_onorm_g", "nsa_qnorm_g", "nsa_knorm_g", "cmp_pe", "cmp_w1", "cmp_w2",
          "w_out", "ple_norm_g", "w_pg", "w_pp", "mem_2", "norm_mix_2", "w_in_2", "conv_w_2", "w_a_out_2", "ret_gn_2",
          "w_b_out_2", "sg_ln_2", "sg_w_2", "sg_b_2", "w_c_out_2", "w_o_2", "norm_xa_2", "norm_mem_2", "xa_q_2", "xa_k_2",
          "xa_v_2", "xa_o_2", "norm_ffn_2", "w1_2", "w3_2", "w2_2", "final_norm_2"]


def kernel(**inputs):
    import numpy as _np
    import concourse.bacc as _bacc
    from concourse import mybir as _mybir
    from concourse.bass_utils import run_bass_kernel_spmd as _run

    one, two, masks = constants()
    arrays = {name: _np.ascontiguousarray(inputs[name]) for name in INPUTS}
    arrays.update({"one_" + n: a for n, a in one.items()})
    arrays.update({"two_" + n: _np.ascontiguousarray(a) for n, a in two.items()})
    arrays["masks"] = masks

    def program(counts):
        nc = _bacc.Bacc("TRN2", target_bir_lowering=False, num_devices=1)
        d = {n: nc.dram_tensor("in_" + n, a.shape, _mybir.dt.from_np(a.dtype), kind="ExternalInput").ap() for n, a in arrays.items()}
        d["w1"] = {n: a.shape[1] for n, a in one.items()}
        d["w2"] = {n: a.shape[1] for n, a in two.items()}
        out = nc.dram_tensor("out_0", (1, T, D), _mybir.dt.float32, kind="ExternalOutput").ap()
        return nc, build(nc, d, out, counts)

    _, counts = program({})
    nc, _ = program(counts)
    r = _run(nc, [{"in_" + n: a for n, a in arrays.items()}], core_ids=[0])
    return r.results[0]["out_0"]
```
